# Optimizing a Trainium2 kernel written in Bass

```python
import jax, jax.numpy as jnp
from jax import lax
import numpy as np
import jax
import jax.numpy as jnp

D_MODEL = 1024
BATCH = 1
SEQ = 256
DEPTH = 2

GRID_W = 64
CTX_LEN = 256
N_Q_HEADS = 8
N_KV_HEADS = 2
GQA_GROUP = N_Q_HEADS // N_KV_HEADS
HEAD_DIM = 64
WINDOW = 128
ATT_BLOCK = 128
ROPE_BASE = 10000.0
Q_DIM = N_Q_HEADS * HEAD_DIM
KV_DIM = N_KV_HEADS * HEAD_DIM
SG_GROUPS = 8
SG_HEAD = 64
SG_WIDTH = SG_GROUPS * SG_HEAD
SG_CHUNK = 128
EVEN_IN = Q_DIM + 2 * KV_DIM + 2 * SG_WIDTH
EVEN_MIX = Q_DIM + SG_WIDTH
CONV_WIDTH = D_MODEL
CONV_K = 3
N_GROUPS = 4
EXPERTS_PER_GROUP = 8
N_EXPERTS = N_GROUPS * EXPERTS_PER_GROUP
TOP_K_IN_GROUP = 2
EXPERT_HIDDEN = D_MODEL // 2
MOE_BLOCK = 128
N_EVEN = (DEPTH + 1) // 2
N_ODD = DEPTH // 2
EPS = 1e-6
NEG_INF = -1e30


def rms_norm(x, g):
    xf = x.astype(jnp.float32)
    y = xf * lax.rsqrt(jnp.mean(xf * xf, axis=-1, keepdims=True) + EPS)
    return (y * g.astype(jnp.float32)).astype(x.dtype)

def layer_norm(x, g):
    xf = x.astype(jnp.float32)
    mu = jnp.mean(xf, axis=-1, keepdims=True)
    xc = xf - mu
    y = xc * lax.rsqrt(jnp.mean(xc * xc, axis=-1, keepdims=True) + EPS)
    return (y * g.astype(jnp.float32)).astype(x.dtype)

def modulate(h, shift, scale):
    return h * (1 + scale) + shift

def axial_rope_tables(rows, dtype):
    quarter = HEAD_DIM // 4
    row_ids = jnp.repeat(jnp.arange(rows, dtype=jnp.float32), GRID_W)
    col_ids = jnp.tile(jnp.arange(GRID_W, dtype=jnp.float32), rows)
    inv = ROPE_BASE ** (-jnp.arange(quarter, dtype=jnp.float32) / quarter)
    ang_r = row_ids[:, None] * inv
    ang_c = col_ids[:, None] * inv
    return (jnp.cos(ang_r)[:, None, :].astype(dtype), jnp.sin(ang_r)[:, None, :].astype(dtype),
            jnp.cos(ang_c)[:, None, :].astype(dtype), jnp.sin(ang_c)[:, None, :].astype(dtype))

def apply_axial_rope(t, rope):
    cos_r, sin_r, cos_c, sin_c = rope
    half = HEAD_DIM // 2
    quarter = HEAD_DIM // 4

    def rot(u, cos, sin):
        u1, u2 = u[..., :quarter], u[..., quarter:]
        return jnp.concatenate([u1 * cos - u2 * sin, u2 * cos + u1 * sin], axis=-1)

    return jnp.concatenate([rot(t[..., :half], cos_r, sin_r), rot(t[..., half:], cos_c, sin_c)], axis=-1)

def windowed_attention(q, k, v, kc, vc, sink):
    b, s = q.shape[:2]
    nb = s // ATT_BLOCK
    scale = HEAD_DIM ** -0.5
    f32 = jnp.float32
    qb = q.reshape(b, nb, ATT_BLOCK, N_KV_HEADS, GQA_GROUP, HEAD_DIM)

    def band(t):
        tp = jnp.pad(t, ((0, 0), (ATT_BLOCK, ATT_BLOCK), (0, 0), (0, 0)))
        tp = tp.reshape(b, nb + 2, ATT_BLOCK, N_KV_HEADS, HEAD_DIM)
        return jnp.concatenate([tp[:, :-2], tp[:, 1:-1], tp[:, 2:]], axis=2)

    kb, vb = band(k), band(v)
    s_loc = jnp.einsum('bnqhgd,bnkhd->bnhgqk', qb, kb, preferred_element_type=f32) * scale
    s_ctx = jnp.einsum('bnqhgd,bchd->bnhgqc', qb, kc, preferred_element_type=f32) * scale
    qi = jnp.arange(ATT_BLOCK)[:, None]
    kj = jnp.arange(3 * ATT_BLOCK)[None, :]
    in_win = jnp.abs(kj - qi - ATT_BLOCK) <= WINDOW
    kpos = (jnp.arange(nb)[:, None] - 1) * ATT_BLOCK + jnp.arange(3 * ATT_BLOCK)[None, :]
    mask = in_win[None] & ((kpos >= 0) & (kpos < s))[:, None, :]
    s_loc = jnp.where(mask[None, :, None, None], s_loc, NEG_INF)
    sink_l = jnp.broadcast_to(sink.astype(f32).reshape(1, 1, N_KV_HEADS, GQA_GROUP, 1, 1), s_ctx.shape[:-1] + (1,))
    p = jax.nn.softmax(jnp.concatenate([sink_l, s_ctx, s_loc], axis=-1), axis=-1)
    n_ctx = kc.shape[1]
    p_ctx = p[..., 1:1 + n_ctx].astype(vc.dtype)
    p_loc = p[..., 1 + n_ctx:].astype(vb.dtype)
    o = (jnp.einsum('bnhgqc,bchd->bnqhgd', p_ctx, vc)
         + jnp.einsum('bnhgqk,bnkhd->bnqhgd', p_loc, vb))
    return o.reshape(b, s, Q_DIM)

def context_attention(qc, kc, vc, sink):
    b, n = qc.shape[:2]
    f32 = jnp.float32
    qh = qc.reshape(b, n, N_KV_HEADS, GQA_GROUP, HEAD_DIM)
    sc = jnp.einsum('bqhgd,bkhd->bhgqk', qh, kc, preferred_element_type=f32) * (HEAD_DIM ** -0.5)
    sink_c = jnp.broadcast_to(sink.astype(f32).reshape(1, N_KV_HEADS, GQA_GROUP, 1, 1), sc.shape[:-1] + (1,))
    p = jax.nn.softmax(jnp.concatenate([sink_c, sc], axis=-1), axis=-1)
    o = jnp.einsum('bhgqk,bkhd->bqhgd', p[..., 1:].astype(vc.dtype), vc)
    return o.reshape(b, n, Q_DIM)

def spatial_gating(u, z, g_sgu, w_sp, b_sp):
    b, n = u.shape[:2]
    u = jax.nn.gelu(u, approximate=False)
    z = layer_norm(jax.nn.gelu(z, approximate=False), g_sgu)
    zc = z.reshape(b, n // SG_CHUNK, SG_CHUNK, SG_GROUPS, SG_HEAD)
    sgate = jnp.einsum('hij,bnjhc->bnihc', w_sp, zc) + b_sp.T[:, :, None]
    return (u.reshape(zc.shape) * sgate).reshape(b, n, SG_WIDTH)

def even_mixer(h, hc, w_in, sink, g_sgu, w_sp, b_sp, w_out, rope, need_ctx):
    b, s, _ = h.shape
    n_ctx = hc.shape[1]
    q, k, v, u, z = jnp.split(h @ w_in, [Q_DIM, Q_DIM + KV_DIM, Q_DIM + 2 * KV_DIM, Q_DIM + 2 * KV_DIM + SG_WIDTH], axis=-1)
    q = apply_axial_rope(q.reshape(b, s, N_Q_HEADS, HEAD_DIM), rope)
    k = apply_axial_rope(k.reshape(b, s, N_KV_HEADS, HEAD_DIM), rope)
    v = v.reshape(b, s, N_KV_HEADS, HEAD_DIM)
    kc, vc = jnp.split(hc @ w_in[:, Q_DIM:Q_DIM + 2 * KV_DIM], 2, axis=-1)
    kc = kc.reshape(b, n_ctx, N_KV_HEADS, HEAD_DIM)
    vc = vc.reshape(b, n_ctx, N_KV_HEADS, HEAD_DIM)
    att = windowed_attention(q, k, v, kc, vc, sink)
    sg = spatial_gating(u, z, g_sgu, w_sp, b_sp)
    out_lat = jnp.concatenate([att, sg], axis=-1) @ w_out
    if not need_ctx:
        return out_lat, None
    qc = hc @ w_in[:, :Q_DIM]
    uc, zc = jnp.split(hc @ w_in[:, Q_DIM + 2 * KV_DIM:], 2, axis=-1)
    att_c = context_attention(qc, kc, vc, sink)
    sg_c = spatial_gating(uc, zc, g_sgu, w_sp, b_sp)
    return out_lat, jnp.concatenate([att_c, sg_c], axis=-1) @ w_out

def short_conv_mixer(h, w_in, conv_w, w_out):
    bg, cg, xt = jnp.split(h @ w_in, 3, axis=-1)
    y = cg * xt
    yp = jnp.pad(y, ((0, 0), (1, 1), (0, 0)))
    conv = yp[:, :-2] * conv_w[0] + yp[:, 1:-1] * conv_w[1] + yp[:, 2:] * conv_w[2]
    return (bg * conv) @ w_out

def moe_ffn(h, w_rg, b_rg, w_re, b_re, w_gate, w_up, w_down):
    n, d = h.shape
    f32 = jnp.float32
    g_logits = jnp.einsum('nd,dg->ng', h, w_rg, preferred_element_type=f32) + b_rg.astype(f32)
    g_idx = jnp.argmax(g_logits, axis=-1).astype(jnp.int32)
    g_w = jnp.take_along_axis(jax.nn.softmax(g_logits, axis=-1), g_idx[:, None], axis=-1)
    e_logits = (jnp.einsum('nd,de->ne', h, w_re, preferred_element_type=f32) + b_re.astype(f32))
    e_logits = e_logits.reshape(n, N_GROUPS, EXPERTS_PER_GROUP)
    e_sel = jnp.take_along_axis(e_logits, g_idx[:, None, None], axis=1)[:, 0]
    top_v, top_i = lax.top_k(e_sel, TOP_K_IN_GROUP)
    gate = g_w * jax.nn.softmax(top_v, axis=-1)
    expert = g_idx[:, None] * EXPERTS_PER_GROUP + top_i.astype(jnp.int32)
    n_assign = n * TOP_K_IN_GROUP
    flat_e = expert.reshape(-1)
    flat_tok = jnp.repeat(jnp.arange(n, dtype=jnp.int32), TOP_K_IN_GROUP)
    flat_w = gate.reshape(-1).astype(h.dtype)
    order = jnp.argsort(flat_e)
    sorted_e = flat_e[order]
    counts = jnp.bincount(flat_e, length=N_EXPERTS)
    padded = (counts + MOE_BLOCK - 1) // MOE_BLOCK * MOE_BLOCK
    pad_end = jnp.cumsum(padded)
    pad_start = pad_end - padded
    raw_start = jnp.cumsum(counts) - counts
    dest = pad_start[sorted_e] + jnp.arange(n_assign, dtype=pad_start.dtype) - raw_start[sorted_e]
    n_blocks = -(-n_assign // MOE_BLOCK) + N_EXPERTS
    n_rows = n_blocks * MOE_BLOCK
    row_tok = jnp.zeros((n_rows,), jnp.int32).at[dest].set(flat_tok[order])
    row_w = jnp.zeros((n_rows,), h.dtype).at[dest].set(flat_w[order])
    block_e = jnp.clip(jnp.searchsorted(pad_end, jnp.arange(n_blocks, dtype=pad_end.dtype) * MOE_BLOCK, side='right'), 0, N_EXPERTS - 1)
    xb = h[row_tok].reshape(n_blocks, MOE_BLOCK, d)

    def expert_block(args):
        xblk, e = args
        hid = jax.nn.silu(xblk @ w_gate[e]) * (xblk @ w_up[e])
        return hid @ w_down[e]

    yb = lax.map(expert_block, (xb, block_e)).reshape(n_rows, d)
    return jnp.zeros_like(h).at[row_tok].add(yb * row_w[:, None])

def first_inputs(seed: int = 0) -> dict:
    key = jax.random.key(seed)
    ks = jax.random.split(key, 25)
    D = D_MODEL

    def nrm(k, shape, s):
        return jax.random.normal(k, shape, jnp.float32) * s

    return {
        'x': nrm(ks[0], (BATCH, SEQ, D), 1.0),
        'c': nrm(ks[1], (BATCH, D), 1.0),
        'ctx': nrm(ks[2], (BATCH, CTX_LEN, D), 1.0),
        'c_ctx': nrm(ks[3], (D,), 1.0),
        'w_ada': nrm(ks[4], (DEPTH, D, 6 * D), 0.5 * D ** -0.5),
        'b_ada': nrm(ks[5], (DEPTH, 6 * D), 0.02),
        'g_norm1': 1.0 + nrm(ks[6], (DEPTH, D), 0.1),
        'g_norm2': 1.0 + nrm(ks[7], (DEPTH, D), 0.1),
        'g_final': 1.0 + nrm(ks[8], (D,), 0.1),
        'w_in_even': nrm(ks[9], (N_EVEN, D, EVEN_IN), D ** -0.5),
        'attn_sink': nrm(ks[10], (N_EVEN, N_Q_HEADS), 1.0),
        'g_sgu': 1.0 + nrm(ks[11], (N_EVEN, SG_WIDTH), 0.1),
        'w_spatial': nrm(ks[12], (N_EVEN, SG_GROUPS, SG_CHUNK, SG_CHUNK), SG_CHUNK ** -0.5),
        'b_spatial': 1.0 + nrm(ks[13], (N_EVEN, SG_GROUPS, SG_CHUNK), 0.1),
        'w_out_even': nrm(ks[14], (N_EVEN, EVEN_MIX, D), EVEN_MIX ** -0.5),
        'w_in_odd': nrm(ks[15], (N_ODD, D, 3 * CONV_WIDTH), D ** -0.5),
        'conv_w': nrm(ks[16], (N_ODD, CONV_K, CONV_WIDTH), CONV_K ** -0.5),
        'w_out_odd': nrm(ks[17], (N_ODD, CONV_WIDTH, D), CONV_WIDTH ** -0.5),
        'w_router_group': nrm(ks[18], (DEPTH, D, N_GROUPS), D ** -0.5),
        'b_router_group': nrm(ks[19], (DEPTH, N_GROUPS), 0.01),
        'w_router_expert': nrm(ks[20], (DEPTH, D, N_EXPERTS), D ** -0.5),
        'b_router_expert': nrm(ks[21], (DEPTH, N_EXPERTS), 0.01),
        'w_gate': nrm(ks[22], (DEPTH, N_EXPERTS, D, EXPERT_HIDDEN), D ** -0.5),
        'w_up': nrm(ks[23], (DEPTH, N_EXPERTS, D, EXPERT_HIDDEN), D ** -0.5),
        'w_down': nrm(ks[24], (DEPTH, N_EXPERTS, EXPERT_HIDDEN, D), EXPERT_HIDDEN ** -0.5),
    }

def first_block(x, c, ctx, c_ctx, w_ada, b_ada, g_norm1, g_norm2, g_final, w_in_even, attn_sink, g_sgu,
              w_spatial, b_spatial, w_out_even, w_in_odd, conv_w, w_out_odd, w_router_group,
              b_router_group, w_router_expert, b_router_expert, w_gate, w_up, w_down):
    b, s, d = x.shape
    rows = s // GRID_W
    rope = axial_rope_tables(rows, x.dtype)
    silu_c = jax.nn.silu(c)
    silu_cc = jax.nn.silu(c_ctx)
    lat, cx = x, ctx
    for l in range(DEPTH):
        need_ctx = any(j % 2 == 0 for j in range(l + 1, DEPTH))
        m = jnp.split(silu_c @ w_ada[l] + b_ada[l], 6, axis=-1)
        sh1, sc1, g1, sh2, sc2, g2 = [t[:, None, :] for t in m]
        h = modulate(rms_norm(lat, g_norm1[l]), sh1, sc1)
        mix_c = None
        if l % 2 == 0 or need_ctx:
            csh1, csc1, cg1, csh2, csc2, cg2 = jnp.split(silu_cc @ w_ada[l] + b_ada[l], 6, axis=-1)
            hc = modulate(rms_norm(cx, g_norm1[l]), csh1, csc1)
        i = l // 2
        if l % 2 == 0:
            mix, mix_c = even_mixer(h, hc, w_in_even[i], attn_sink[i], g_sgu[i], w_spatial[i],
                                    b_spatial[i], w_out_even[i], rope, need_ctx)
        else:
            mix = short_conv_mixer(h, w_in_odd[i], conv_w[i], w_out_odd[i])
            if need_ctx:
                mix_c = short_conv_mixer(hc, w_in_odd[i], conv_w[i], w_out_odd[i])
        lat = lat + g1 * mix
        h2 = modulate(rms_norm(lat, g_norm2[l]), sh2, sc2)
        lat = lat + g2 * moe_ffn(h2.reshape(-1, d), w_router_group[l], b_router_group[l], w_router_expert[l],
                                 b_router_expert[l], w_gate[l], w_up[l], w_down[l]).reshape(b, s, d)
        if need_ctx:
            cx = cx + cg1 * mix_c
            hc2 = modulate(rms_norm(cx, g_norm2[l]), csh2, csc2)
            cx = cx + cg2 * moe_ffn(hc2.reshape(-1, d), w_router_group[l], b_router_group[l], w_router_expert[l],
                                    b_router_expert[l], w_gate[l], w_up[l], w_down[l]).reshape(cx.shape)
    return rms_norm(lat, g_final)


FNET_GROUPS = 4
FNET_GROUP_DIM = 128
FNET_WIDTH = FNET_GROUPS * FNET_GROUP_DIM

NA_HEADS = 8
NA_HEAD_DIM = 64
NA_WIDTH = NA_HEADS * NA_HEAD_DIM
NA_KH = 8
NA_KW = 16
NA_SCALE = NA_HEAD_DIM ** -0.5

MLA_HEADS = 8
MLA_Q_LORA = 256
MLA_KV_LORA = 128
MLA_NOPE_DIM = 64
MLA_ROPE_DIM = 32
MLA_V_DIM = 64
MLA_WIDTH = MLA_HEADS * MLA_V_DIM
MLA_SCALE = (MLA_NOPE_DIM + MLA_ROPE_DIM) ** -0.5
ATTN_BLOCK = 128

N_BRANCH = 3
BRANCH_DIM = 512

FFN_HIDDEN = -(-8 * D_MODEL // (3 * 256)) * 256

NORM_EPS = 1e-5
DEEPNORM_ALPHA = (2 * DEPTH) ** 0.25
DEEPNORM_BETA = (8 * DEPTH) ** -0.25

IN_SIZES = (FNET_WIDTH, NA_WIDTH, NA_WIDTH, NA_WIDTH, MLA_Q_LORA, MLA_KV_LORA, MLA_ROPE_DIM, N_BRANCH * D_MODEL)
IN_DIM = int(sum(IN_SIZES))
IN_OFFSETS = [int(v) for v in np.cumsum(IN_SIZES)[:-1]]


def layer_norm_2(x, g, b):
    xf = x.astype(jnp.float32)
    mu = jnp.mean(xf, axis=-1, keepdims=True)
    var = jnp.mean(jnp.square(xf - mu), axis=-1, keepdims=True)
    y = (xf - mu) * lax.rsqrt(var + NORM_EPS) * g.astype(jnp.float32) + b.astype(jnp.float32)
    return y.astype(x.dtype)

def rms_norm_2(x, g):
    xf = x.astype(jnp.float32)
    y = xf * lax.rsqrt(jnp.mean(jnp.square(xf), axis=-1, keepdims=True) + NORM_EPS) * g.astype(jnp.float32)
    return y.astype(x.dtype)

def rope_tables(n):
    t = jnp.arange(n, dtype=jnp.int32)
    rows = (t // GRID_W).astype(jnp.float32)
    cols = (t % GRID_W).astype(jnp.float32)
    n_freq = MLA_ROPE_DIM // 4
    inv_freq = ROPE_BASE ** (-jnp.arange(n_freq, dtype=jnp.float32) / n_freq)
    ang = jnp.concatenate([rows[:, None] * inv_freq, cols[:, None] * inv_freq], axis=-1)
    return jnp.cos(ang), jnp.sin(ang)

def axial_rope(x, cos, sin):
    xf = x.astype(jnp.float32)
    half = x.shape[-1] // 2
    x1, x2 = xf[..., :half], xf[..., half:]
    return jnp.concatenate([x1 * cos - x2 * sin, x2 * cos + x1 * sin], axis=-1).astype(x.dtype)

def split_heads(z, n_heads):
    b, n, w = z.shape
    return z.reshape(b, n, n_heads, w // n_heads)

def fourier_mix(z):
    b, n, _ = z.shape
    zg = z.reshape(b, n, FNET_GROUPS, FNET_GROUP_DIM).astype(jnp.float32)
    y = jnp.fft.fft2(zg, axes=(1, 3), norm='ortho').real
    return y.reshape(b, n, FNET_WIDTH).astype(z.dtype)

def softmax_attend(q, k, v, scale):
    s = jnp.einsum('bqhd,bkhd->bhqk', q, k, preferred_element_type=jnp.float32) * scale
    p = jax.nn.softmax(s, axis=-1).astype(v.dtype)
    return jnp.einsum('bhqk,bkhd->bqhd', p, v)

def blocked_attend(q, k, v, scale):
    b, n, h, dq = q.shape
    qb = q.reshape(b, n // ATTN_BLOCK, ATTN_BLOCK, h, dq).transpose(1, 0, 2, 3, 4)
    out = lax.map(lambda qi: softmax_attend(qi, k, v, scale), qb)
    return out.transpose(1, 0, 2, 3, 4).reshape(b, n, h, v.shape[-1])

def neighbourhood_attention(q, k, v, k_ctx, v_ctx, rpb, n_rows):
    b, n, h, dh = q.shape
    kh = min(NA_KH, n_rows)
    kw = NA_KW
    qg = q.reshape(b, n_rows, GRID_W, h, dh).transpose(1, 0, 2, 3, 4)
    kg = k.reshape(b, n_rows, GRID_W, h, dh)
    vg = v.reshape(b, n_rows, GRID_W, h, dh)
    cols = jnp.arange(GRID_W, dtype=jnp.int32)
    col_start = jnp.clip(cols - kw // 2, 0, GRID_W - kw)
    col_idx = col_start[:, None] + jnp.arange(kw, dtype=jnp.int32)
    dc = col_idx - cols[:, None] + (NA_KW - 1)
    rpb_c = rpb.astype(jnp.float32)[:, :, dc]
    n_loc = kh * kw

    def row_fn(args):
        r, q_r = args
        rs = jnp.clip(r - kh // 2, 0, n_rows - kh)
        k_rows = lax.dynamic_slice_in_dim(kg, rs, kh, axis=1)
        v_rows = lax.dynamic_slice_in_dim(vg, rs, kh, axis=1)
        k_win = k_rows[:, :, col_idx]
        v_win = v_rows[:, :, col_idx]
        dr = rs + jnp.arange(kh, dtype=jnp.int32) - r + (NA_KH - 1)
        bias = jnp.take(rpb_c, dr, axis=1).transpose(0, 2, 1, 3)
        s_loc = jnp.einsum('bwhd,bkwjhd->bhwkj', q_r, k_win, preferred_element_type=jnp.float32) * NA_SCALE + bias[None]
        s_ctx = jnp.einsum('bwhd,bchd->bhwc', q_r, k_ctx, preferred_element_type=jnp.float32) * NA_SCALE
        s = jnp.concatenate([s_loc.reshape(b, h, GRID_W, n_loc), s_ctx], axis=-1)
        p = jax.nn.softmax(s, axis=-1).astype(v.dtype)
        p_loc = p[..., :n_loc].reshape(b, h, GRID_W, kh, kw)
        p_ctx = p[..., n_loc:]
        return (jnp.einsum('bhwkj,bkwjhd->bwhd', p_loc, v_win)
                + jnp.einsum('bhwc,bchd->bwhd', p_ctx, v_ctx))

    out = lax.map(row_fn, (jnp.arange(n_rows, dtype=jnp.int32), qg))
    return out.transpose(1, 0, 2, 3, 4).reshape(b, n, h * dh)

def mla_queries(cq, g_q, w_uq, w_qr, rope):
    b, n, _ = cq.shape
    cq = rms_norm_2(cq, g_q)
    q_nope = (cq @ w_uq).reshape(b, n, MLA_HEADS, MLA_NOPE_DIM)
    q_rope = (cq @ w_qr).reshape(b, n, MLA_HEADS, MLA_ROPE_DIM)
    if rope is not None:
        q_rope = axial_rope(q_rope, rope[0][:, None, :], rope[1][:, None, :])
    return jnp.concatenate([q_nope, q_rope], axis=-1)

def mla_keys_values(ckv, kr, g_kv, w_uk, w_uv, rope):
    b, n, _ = ckv.shape
    ckv = rms_norm_2(ckv, g_kv)
    k_nope = (ckv @ w_uk).reshape(b, n, MLA_HEADS, MLA_NOPE_DIM)
    v = (ckv @ w_uv).reshape(b, n, MLA_HEADS, MLA_V_DIM)
    if rope is not None:
        kr = axial_rope(kr, rope[0], rope[1])
    k_rope = jnp.broadcast_to(kr[:, :, None, :], (b, n, MLA_HEADS, MLA_ROPE_DIM))
    return jnp.concatenate([k_nope, k_rope], axis=-1), v

def merge_branches(ys, g, w_branch, w_out):
    b, n, _ = g.shape
    y = jnp.stack(ys, axis=2)
    proj = jnp.einsum('bngi,gio->bngo', y, w_branch)
    gate = jax.nn.sigmoid(g.reshape(b, n, N_BRANCH, D_MODEL).astype(jnp.float32)).astype(proj.dtype)
    return jnp.sum(gate * proj, axis=2) @ w_out

def mixer(h, hc, lp, rope, n_rows, need_ctx):
    b, n, _ = h.shape
    f, nq, nk, nv, cq, ckv, kr, g = jnp.split(h @ lp['w_in'], IN_OFFSETS, axis=-1)
    fc, nqc, nkc, nvc, cqc, ckvc, krc, gc = jnp.split(hc @ lp['w_in'], IN_OFFSETS, axis=-1)
    na_kc, na_vc = split_heads(nkc, NA_HEADS), split_heads(nvc, NA_HEADS)
    mla_kc, mla_vc = mla_keys_values(ckvc, krc, lp['g_kv'], lp['w_uk'], lp['w_uv'], None)
    y_f = fourier_mix(f)
    y_na = neighbourhood_attention(split_heads(nq, NA_HEADS), split_heads(nk, NA_HEADS), split_heads(nv, NA_HEADS),
                                   na_kc, na_vc, lp['rpb'], n_rows)
    mla_k, mla_v = mla_keys_values(ckv, kr, lp['g_kv'], lp['w_uk'], lp['w_uv'], rope)
    mla_q = mla_queries(cq, lp['g_q'], lp['w_uq'], lp['w_qr'], rope)
    y_mla = blocked_attend(mla_q, jnp.concatenate([mla_kc, mla_k], axis=1),
                           jnp.concatenate([mla_vc, mla_v], axis=1), MLA_SCALE).reshape(b, n, MLA_WIDTH)
    out = merge_branches([y_f, y_na, y_mla], g, lp['w_branch'], lp['w_out'])
    if not need_ctx:
        return out, None
    n_ctx = hc.shape[1]
    yc_f = fourier_mix(fc)
    yc_na = softmax_attend(split_heads(nqc, NA_HEADS), na_kc, na_vc, NA_SCALE).reshape(b, n_ctx, NA_WIDTH)
    mla_qc = mla_queries(cqc, lp['g_q'], lp['w_uq'], lp['w_qr'], None)
    yc_mla = softmax_attend(mla_qc, mla_kc, mla_vc, MLA_SCALE).reshape(b, n_ctx, MLA_WIDTH)
    out_c = merge_branches([yc_f, yc_na, yc_mla], gc, lp['w_branch'], lp['w_out'])
    return out, out_c

def swiglu(h, w_gate, w_up, w_down):
    return (jax.nn.silu(h @ w_gate) * (h @ w_up)) @ w_down

def second_inputs(seed: int = 0) -> dict:
    key = jax.random.key(seed)
    ks = jax.random.split(key, 32)

    def nrm(k, shape, scale):
        return jax.random.normal(k, shape, dtype=jnp.float32) * scale

    L, D, F = DEPTH, D_MODEL, FFN_HIDDEN
    return {
        'x': nrm(ks[0], (BATCH, SEQ, D), 1.0),
        'c': nrm(ks[1], (BATCH, D), 1.0),
        'ctx': nrm(ks[2], (BATCH, CTX_LEN, D), 1.0),
        'c_ctx': nrm(ks[3], (D,), 1.0),
        'ln_in_g': 1.0 + nrm(ks[4], (D,), 0.02),
        'ln_in_b': nrm(ks[5], (D,), 0.02),
        'w_mod': nrm(ks[6], (L, D, 6 * D), 0.1 * D ** -0.5),
        'b_mod': nrm(ks[7], (L, 6 * D), 0.02),
        'w_in': nrm(ks[8], (L, D, IN_DIM), D ** -0.5),
        'mla_q_norm_g': 1.0 + nrm(ks[9], (L, MLA_Q_LORA), 0.02),
        'mla_kv_norm_g': 1.0 + nrm(ks[10], (L, MLA_KV_LORA), 0.02),
        'w_uq': nrm(ks[11], (L, MLA_Q_LORA, MLA_HEADS * MLA_NOPE_DIM), MLA_Q_LORA ** -0.5),
        'w_qr': nrm(ks[12], (L, MLA_Q_LORA, MLA_HEADS * MLA_ROPE_DIM), MLA_Q_LORA ** -0.5),
        'w_uk': nrm(ks[13], (L, MLA_KV_LORA, MLA_HEADS * MLA_NOPE_DIM), MLA_KV_LORA ** -0.5),
        'w_uv': nrm(ks[14], (L, MLA_KV_LORA, MLA_HEADS * MLA_V_DIM), MLA_KV_LORA ** -0.5),
        'na_rpb': nrm(ks[15], (L, NA_HEADS, 2 * NA_KH - 1, 2 * NA_KW - 1), 0.1),
        'w_branch': nrm(ks[16], (L, N_BRANCH, BRANCH_DIM, D), BRANCH_DIM ** -0.5),
        'w_out': nrm(ks[17], (L, D, D), DEEPNORM_BETA * D ** -0.5),
        'ln1_g': 1.0 + nrm(ks[18], (L, D), 0.02),
        'ln1_b': nrm(ks[19], (L, D), 0.02),
        'ln2_g': 1.0 + nrm(ks[20], (L, D), 0.02),
        'ln2_b': nrm(ks[21], (L, D), 0.02),
        'w_ffn_gate': nrm(ks[22], (L, D, F), D ** -0.5),
        'w_ffn_up': nrm(ks[23], (L, D, F), D ** -0.5),
        'w_ffn_down': nrm(ks[24], (L, F, D), DEEPNORM_BETA * F ** -0.5),
    }

def second_block(x, c, ctx, c_ctx, ln_in_g, ln_in_b, w_mod, b_mod, w_in, mla_q_norm_g, mla_kv_norm_g,
              w_uq, w_qr, w_uk, w_uv, na_rpb, w_branch, w_out, ln1_g, ln1_b, ln2_g, ln2_b,
              w_ffn_gate, w_ffn_up, w_ffn_down):
    n = x.shape[1]
    n_rows = n // GRID_W
    rope = rope_tables(n)
    x_lat = layer_norm_2(x, ln_in_g, ln_in_b)
    x_ctx = layer_norm_2(ctx, ln_in_g, ln_in_b)
    silu_c = jax.nn.silu(c)
    silu_cc = jax.nn.silu(c_ctx)
    for l in range(DEPTH):
        last = l == DEPTH - 1
        lp = {'w_in': w_in[l], 'g_q': mla_q_norm_g[l], 'g_kv': mla_kv_norm_g[l], 'w_uq': w_uq[l],
              'w_qr': w_qr[l], 'w_uk': w_uk[l], 'w_uv': w_uv[l], 'rpb': na_rpb[l],
              'w_branch': w_branch[l], 'w_out': w_out[l]}
        sh1, sc1, g1, sh2, sc2, g2 = [m[:, None, :] for m in jnp.split(silu_c @ w_mod[l] + b_mod[l], 6, axis=-1)]
        csh1, csc1, cg1, csh2, csc2, cg2 = jnp.split(silu_cc @ w_mod[l] + b_mod[l], 6, axis=-1)
        a_lat = x_lat * (1 + sc1) + sh1
        a_ctx = x_ctx * (1 + csc1) + csh1
        m_lat, m_ctx = mixer(a_lat, a_ctx, lp, rope, n_rows, not last)
        x_lat = layer_norm_2(DEEPNORM_ALPHA * x_lat + (1 + g1) * m_lat, ln1_g[l], ln1_b[l])
        f_lat = swiglu(x_lat * (1 + sc2) + sh2, w_ffn_gate[l], w_ffn_up[l], w_ffn_down[l])
        x_lat = layer_norm_2(DEEPNORM_ALPHA * x_lat + (1 + g2) * f_lat, ln2_g[l], ln2_b[l])
        if not last:
            x_ctx = layer_norm_2(DEEPNORM_ALPHA * x_ctx + (1 + cg1) * m_ctx, ln1_g[l], ln1_b[l])
            f_ctx = swiglu(x_ctx * (1 + csc2) + csh2, w_ffn_gate[l], w_ffn_up[l], w_ffn_down[l])
            x_ctx = layer_norm_2(DEEPNORM_ALPHA * x_ctx + (1 + cg2) * f_ctx, ln2_g[l], ln2_b[l])
    return x_lat


def setup_inputs(seed=0):
    out = dict(first_inputs(seed))
    for name, value in second_inputs(seed + 1).items():
        if name != "x":
            out[name + "_2"] = value
    return out


def reference(
    x, c, ctx, c_ctx, w_ada, b_ada, g_norm1, g_norm2, g_final, w_in_even, attn_sink, g_sgu,
    w_spatial, b_spatial, w_out_even, w_in_odd, conv_w, w_out_odd, w_router_group,
    b_router_group, w_router_expert, b_router_expert, w_gate, w_up, w_down, c_2, ctx_2, c_ctx_2,
    ln_in_g_2, ln_in_b_2, w_mod_2, b_mod_2, w_in_2, mla_q_norm_g_2, mla_kv_norm_g_2, w_uq_2,
    w_qr_2, w_uk_2, w_uv_2, na_rpb_2, w_branch_2, w_out_2, ln1_g_2, ln1_b_2, ln2_g_2, ln2_b_2,
    w_ffn_gate_2, w_ffn_up_2, w_ffn_down_2,
):
    x = first_block(
        x, c, ctx, c_ctx, w_ada, b_ada, g_norm1, g_norm2, g_final, w_in_even, attn_sink, g_sgu,
        w_spatial, b_spatial, w_out_even, w_in_odd, conv_w, w_out_odd, w_router_group,
        b_router_group, w_router_expert, b_router_expert, w_gate, w_up, w_down,
    )
    return second_block(
        x, c_2, ctx_2, c_ctx_2, ln_in_g_2, ln_in_b_2, w_mod_2, b_mod_2, w_in_2, mla_q_norm_g_2,
        mla_kv_norm_g_2, w_uq_2, w_qr_2, w_uk_2, w_uv_2, na_rpb_2, w_branch_2, w_out_2, ln1_g_2,
        ln1_b_2, ln2_g_2, ln2_b_2, w_ffn_gate_2, w_ffn_up_2, w_ffn_down_2,
    )


_drawn_inputs = setup_inputs


def setup_inputs(seed=0):
    import zlib

    import numpy as np

    out = dict(_drawn_inputs(seed))
    spreads = {}
    factors = {'attn_sink': 8.0,
     'b_router_group': 8.0,
     'b_router_expert': 6.199,
     'c_ctx_2': 3.522,
     'ln_in_g_2': 2.775,
     'b_mod_2': 3.321,
     'mla_q_norm_g_2': 8.0,
     'mla_kv_norm_g_2': 8.0,
     'w_qr_2': 5.008,
     'na_rpb_2': 8.0}
    for name, (base, spread) in spreads.items():
        noise = np.random.default_rng([zlib.crc32(name.encode()), seed]).standard_normal(out[name].shape)
        drawn = base * np.exp(spread * noise) if base else spread * noise
        out[name] = jnp.asarray(drawn.astype(out[name].dtype))
    for name, factor in factors.items():
        out[name] = (out[name] * factor).astype(out[name].dtype)
    return out
```

```python
import math
from contextlib import ExitStack

import concourse.bass as bass
import numpy as np
from concourse import mybir

F32 = mybir.dt.float32
I32 = mybir.dt.int32
U32 = mybir.dt.uint32
ALU = mybir.AluOpType
ACT = mybir.ActivationFunctionType
AXX = mybir.AxisListType.X

P = 128
D = 1024
KD = D // P
T = 256
TB = T // P
HEADS = 8
NMOD = 6 * KD
EXPERTS, GROUPS = 32, 4
PAIRS = EXPERTS // 2
HID = 512
C = 64
PASSES = T // C
FFN = 2816
KF = FFN // P
ROUTES = GROUPS + EXPERTS
ALPHA = 4.0 ** 0.25
EPS1, EPS2 = 1e-6, 1e-5
NEG = -1e30
MLA_SCALE = 96.0 ** -0.5
MLA_ROWS = 96

TILES = 32
RING = 6
STRIP = TILES * P
STAGES = [
    ("ada0a", 4), ("even_in", 4), ("ada0b", 8), ("ada1a", 8), ("even_out", 2), ("ada1b", 4),
    ("moe0", 3 * EXPERTS), ("odd", 6 + 24 + 2), ("moe1", 3 * EXPERTS),
    ("l0_na", 4), ("l0_bias", 1), ("l0_low", 1), ("l0_up", 1), ("l0_merge", 9), ("l0_out", 2), ("l0_ffn", 17),
    ("l1_na", 4), ("l1_bias", 1), ("l1_low", 1), ("l1_up", 1), ("l1_merge", 9), ("l1_out", 2), ("l1_ffn", 17),
]
FIRST = {}
_at = 0
for _name, _n in STAGES:
    FIRST[_name] = _at
    _at += _n
STRIPS = _at

LAYER_STREAMS = (2, 1)
LIN = [
    ("even_q", "DDDD"), ("even_k", "D"), ("even_v", "D"), ("even_u", "AAAA"), ("even_z", "AA"),
    ("even_rope", "DDDDD"), ("even_gate", "DD"), ("even_out", "D" * KD),
    ("turn0", "AAAA"), ("route0", "D"), ("rank0", "D"),
    ("odd_in", "AAD" * KD), ("odd_out", "D" * KD),
    ("turn1", "AAAA"), ("route1", "D"), ("rank1", "D"),
]
for _l, _s in enumerate(LAYER_STREAMS):
    LIN += [(f"f{_l}", "D" * 2 * _s), (f"dft{_l}", "A" * 4 * _s), (f"idft{_l}", "D" * 4 * _s),
            (f"nq{_l}", "DDDD"), (f"nk{_l}", "AAAA"), (f"nv{_l}", "AAAA"),
            (f"low{_l}", "DDDD"), (f"krope{_l}", "D"), (f"mq{_l}", "A" * 8), (f"mk{_l}", "A" * 8),
            (f"mv{_l}", "DDDD"), (f"qrope{_l}", "D" * 8),
            (f"merge{_l}", "ADADAD" * KD), (f"out{_l}", "D" * KD), (f"up{_l}", "AD" * KF), (f"down{_l}", "D" * KD)]
GROUP0, TAKER, TAKEN = {}, [], []
for _name, _who in LIN:
    GROUP0[_name] = len(TAKER)
    for _w in _who:
        TAKER.append(_w)
        TAKEN.append(TAKER.count(_w))
LIN_BANKS = 4

NORMS = ["n1_0", "n2_0", "n1_1", "n2_1", "final", "ln_in",
         "cq0", "ckv0", "ln1_0", "ln2_0", "cq1", "ckv1", "ln1_1", "ln2_1"]
NCHUNK = {n: 2 if n[:2] == "cq" else 1 if n[:3] == "ckv" else KD for n in NORMS}
NBASE, NMEAN, NSTAT, NOUT, NMID, NXC = {}, {}, {}, {}, {}, {}
_b = _m = _o = _d = _x = 0
for _i, _n in enumerate(NORMS):
    NBASE[_n], NSTAT[_n], NMEAN[_n], NOUT[_n], NMID[_n], NXC[_n] = _b, _i, _m, _o, _d, _x
    _b += NCHUNK[_n]
    _d += NCHUNK[_n]
    if _n[:2] == "ln":
        _m += 1
        _x += KD
    if _n[:2] in ("n1", "n2", "ln"):
        _o += KD

ATT, _u = {}, 0
for _n, _q in [("even", 2), ("na0", 4), ("mla0", 4), ("na1", 2), ("mla1", 2)]:
    ATT[_n] = (_q, _u)
    _u += _q * HEADS

def columns(parts):
    at, out = 0, {}
    for name, n in parts:
        out[name] = (at, n)
        at += n
    return out, at


PAR, N_PAR = columns([
    ("c", 2 * KD), ("c_2", 2 * KD), ("bias", 4 * NMOD * 2), ("g1", 2 * KD), ("g2", 2 * KD), ("gf", KD),
    ("sgu", 4), ("conv", 3 * KD), ("lni_g", KD), ("lni_b", KD),
    ("ln1_g", 2 * KD), ("ln1_b", 2 * KD), ("ln2_g", 2 * KD), ("ln2_b", 2 * KD),
    ("gq", 4), ("gkv", 2), ("sink", HEADS), ("rbias", 2 * TB * ROUTES),
    ("ident", P), ("ones", P), ("before", P), ("expert", EXPERTS), ("group", EXPERTS), ("slot", C),
])
TA, N_TA = columns([("cos", T), ("sin", T), ("swap", P), ("mask", TB * T), ("bsp", 4 * P), ("router", 2 * KD * ROUTES)])
TC, N_TC = columns([("dft", TB * 2 * T), ("cd", P), ("sd", P), ("cos", T), ("sin", T), ("swap", P)])


def build_program(nc, stream, par, tab_a, tab_b, wsp_d, xt, ctx2t, out):
    with ExitStack() as ctx:
        def sb(name, shape, dt=F32):
            return ctx.enter_context(nc.sbuf_tensor(name, shape, dt))

        def sem(name):
            return ctx.enter_context(nc.semaphore(name))

        ring = sb("ring", [P, RING, STRIP])
        X = sb("X", [P, KD, 2 * T])
        A = sb("A", [P, KD, 2 * T])
        par_sb = sb("par_sb", [P, N_PAR])
        tab_sb = sb("tab_sb", [P, max(N_TA, N_TC)])
        MOD = sb("MOD", [P, 4, NMOD, 2])
        MODP = sb("MODP", [P, 2, NMOD, 2])
        GSC = sb("GSC", [P, 5, KD])
        SILC = sb("SILC", [P, 2, KD, 2])
        EPS = sb("EPS", [P, 2])
        MX = sb("MX", [P, 2, HEADS])
        NM = sb("NM", [P, 2, HEADS])
        SM = sb("SM", [P, 2, HEADS])
        ES = sb("ES", [P, 2, HEADS])
        BN = sb("BN", [P, TB, 10])
        FLAG = sb("FLAG", [P, 2], I32)
        work = sb("work", [P, 15360])
        bank = [ctx.enter_context(nc.psum_tensor(f"bank{i}", [P, 512], F32)) for i in range(8)]

        def par_(name, a=0, n=None):
            o, full = PAR[name]
            return par_sb[:, o + a:o + (full if n is None else a + n)]

        def tab(where, name, a=0, n=None):
            o, full = where[name]
            return tab_sb[:, o + a:o + (full if n is None else a + n)]

        def wk(at, *shape):
            n = int(np.prod(shape))
            v = work[:, at:at + n]
            if len(shape) == 2:
                v = v.rearrange("p (a b) -> p a b", b=shape[1])
            if len(shape) == 3:
                v = v.rearrange("p (a b c) -> p a b c", b=shape[1], c=shape[2])
            return v

        ident, ones, before = par_("ident"), par_("ones"), par_("before")

        SQ, MEAN, RSTD = wk(13312, 2, 512), wk(14336, 512), wk(14848, 512)
        QRAW, QK, KV_K = wk(0, 5, T), wk(1280, 5, T), wk(2560, 2 * T)
        V1, U1, Z1 = wk(3072, 4, P), wk(3584, 4, T), wk(4608, TB, 512)
        PR1, PT1, YT1 = wk(5632, 3, 512), wk(7168, 2, 512), wk(8192, 512)
        CAT, WSP, TMP1 = wk(8704, KD, T), wk(10752, HEADS, P), wk(11776, 2, T)
        HT, XG = wk(0, TB, D), wk(2048, KD, P)
        SIL, HE = wk(3072, 2, 4 * C), wk(3584, 2, 4 * C)
        YP, GE, GW, SPT = wk(4096, D), wk(5120, TB, P), wk(5376, TB, P), wk(5632, T)
        RK, MM, GG = wk(5888, TB, 34), wk(5956, TB, 34), wk(6024, TB, 34)
        LG, GL8, MX8, V8 = wk(6100, TB, ROUTES), wk(6172, TB, 8), wk(6188, TB, 8), wk(6204, TB, 8)
        IX8, IE8 = wk(6220, TB, 8).bitcast(U32), wk(6236, TB, 8).bitcast(U32)
        IXF, IEF = wk(6252, TB, 8), wk(6268, TB, 8)
        SML = wk(6284, TB, 16)
        GM, ME, O0, O1 = wk(6316, TB, 32), wk(6380, TB, 32), wk(6444, TB, 32), wk(6508, TB, 32)
        MS, CMAX, OPEN = wk(6572, 32), wk(6604, 1), wk(6606, 1)
        BG, CG, YC = wk(0, 2, T), wk(512, 2, T), wk(1024, 2, T + 2)
        CV, CT = wk(1600, KD, T), wk(3648, 2, T)
        FT, FU = wk(0, 4, 512), wk(2048, 8, 512)
        NQ, NK, V2 = wk(0, 4, 512), wk(2048, 4, 512), wk(4096, 4, 512)
        MK = wk(0, KD, 512)
        YB = [wk(6144 + 2048 * b, 4, 512) for b in range(3)]
        LOW = YB[2]
        PR2, YT2, PT2 = wk(12288, 3, 512), wk(13824, 512), wk(14336, 2, 512)
        MG, SG = wk(0, KD, 512), wk(4096, 2, 512)
        HB, SB_, RB = wk(0, KF, 512), wk(11264, 2, 512), wk(12288, 2, 512)
        RT = wk(12288, 2, 512)
        QT = wk(12288, 2, T)

        par_in, x_in, taba_in, tabb_in, wsp_in = (sem(n) for n in ("par_in", "x_in", "taba_in", "tabb_in", "wsp_in"))
        ctx2_in, out_sent = sem("ctx2_in"), sem("out_sent")
        strip_in = [sem(f"strip_in{i}") for i in range(RING)]
        strip_used = sem("strip_used")
        silc_ready, eps_ready = sem("silc_ready"), sem("eps_ready")
        lin_ready = sem("lin_ready")
        taken = {"D": sem("taken_by_vector"), "A": sem("taken_by_scalar")}
        sum_ready, xc_ready, sq_ready, sq_used = (sem(n) for n in ("sum_ready", "xc_ready", "sq_ready", "sq_used"))
        std_ready, mid_ready, norm_out = (sem(n) for n in ("std_ready", "mid_ready", "norm_out"))
        mod_taken = sem("mod_taken")
        at_s, at_nm, at_p, at_t, at_ptc = (sem(n) for n in ("at_s", "at_nm", "at_p", "at_t", "at_ptc"))
        at_pv, at_ytm, at_yt, at_y, at_es, at_d = (sem(n) for n in ("at_pv", "at_ytm", "at_yt", "at_y", "at_es", "at_d"))
        z_var, z_std, z_norm, sg_ready = (sem(n) for n in ("z_var", "z_std", "z_norm", "sg_ready"))
        rt_exp_in, rt_exp, rt_mask, flag_ready = (sem(n) for n in ("rt_exp_in", "rt_exp", "rt_mask", "flag_ready"))
        cv_ready, a_ready, kr_copied, low_out, rope_done = (sem(n) for n in ("cv_ready", "a_ready", "kr_copied", "low_out", "rope_done"))
        tmp_ready = sem("tmp_ready")
        dve_own, act_own = sem("dve_own"), sem("act_own")

        NAMES = ["xg_ready", "ge_ready", "gw_ready", "gath_ready", "gate_ready", "up_ready", "sil_ready", "hid_ready",
                 "y_ready", "y_copied", "comb_ready", "res_added", "tr_ready", "spt_ready"]
        main = {n: sem("m_" + n) for n in NAMES}
        over = [{n: sem(f"o{l}_{n}") for n in NAMES} for l in range(2)]
        over_in = [[sem(f"o{l}_in{i}") for i in range(RING)] for l in range(2)]
        over_used = [sem(f"o{l}_used") for l in range(2)]

        def last_taken(eng, stage):
            end = GROUP0[stage] + len(dict(LIN)[stage]) - 1
            for w in "DA":
                n = TAKER[:end + 1].count(w)
                if n:
                    eng.wait_ge(taken[w], n)

        def wait_taken(eng, stage, j):
            g = GROUP0[stage] + j
            eng.wait_ge(taken[TAKER[g]], TAKEN[g])

        def streams(l):
            return LAYER_STREAMS[l] * T

        MOD_PARTS = {"ada0a": (0, 0, 16, FIRST["ada0a"]), "ada0b": (0, 16, 32, FIRST["ada0b"]),
                     "ada1": (1, 0, 48, FIRST["ada1a"]), "m2": (2, 0, 96, FIRST["odd"])}

        block = ctx.enter_context(nc.Block())

        @block.sync
        def _(sp):
            def strips(a, b):
                while a < b and a < RING:
                    sp.dma_start(ring[:, a % RING, :], stream[a]).then_inc(strip_in[a % RING], 16)
                    a += 1
                turns = (b - a) // RING
                if turns:
                    with sp.Fori(0, turns) as i:
                        for j in range(RING):
                            sp.wait_ge(strip_used, i * RING + (a + j - RING + 1))
                            sp.dma_start(ring[:, (a + j) % RING, :], stream[i * RING + (a + j)])\
                              .then_inc(strip_in[(a + j) % RING], 16)
                for s in range(a + turns * RING, b):
                    sp.wait_ge(strip_used, s - RING + 1)
                    sp.dma_start(ring[:, s % RING, :], stream[s]).then_inc(strip_in[s % RING], 16)

            def overflow(l):
                first = FIRST[f"moe{l}"]
                sp.wait_ge(flag_ready, l + 1)
                full = sp.value_load(FLAG[0:1, l:l + 1], min_val=0, max_val=1)
                with sp.If(full > 0):
                    sp.wait_ge(strip_used, first + 3 * EXPERTS)
                    for j in range(RING):
                        sp.dma_start(ring[:, (first + j) % RING, :], stream[first + j])\
                          .then_inc(over_in[l][j], 16)
                    n = 3 * EXPERTS // RING
                    with sp.Fori(1, n * (PASSES - 1)) as i:
                        for j in range(RING):
                            sp.wait_ge(over_used[l], i * RING + (j - RING + 1))
                            sp.dma_start(ring[:, (first + j) % RING, :], stream[(i % n) * RING + (first + j)])\
                              .then_inc(over_in[l][j], 16)
                    sp.wait_ge(over_used[l], 3 * EXPERTS * (PASSES - 1))

            strips(0, FIRST["odd"])
            overflow(0)
            strips(FIRST["odd"], FIRST["l0_na"])
            overflow(1)
            strips(FIRST["l0_na"], STRIPS)
            sp.wait_ge(norm_out, NOUT["ln2_1"] + KD)
            sp.dma_start(out, X[:, :, 0:T]).then_inc(out_sent, 16)
            sp.wait_ge(out_sent, 16)

        @block.tensor
        def _(pe):
            have = {}
            owed = [0]

            def strip(s):
                if s not in have:
                    pe.wait_ge(strip_in[s % RING], 16 * (s // RING + 1))
                    have[s] = ring[:, s % RING, :]
                return have[s]

            def tile(stage, n, width=1):
                v = strip(FIRST[stage] + n // TILES)
                at = n % TILES
                return v[:, at * P:(at + width) * P]

            def mm(o, w, x, start, stop, tells=False):
                m = pe.matmul(o, w, x, start=start, stop=stop)
                if owed[0] and not tells:
                    m.then_inc(strip_used, 1)
                    owed[0] -= 1
                return m

            def group(g):
                if g >= LIN_BANKS:
                    pe.wait_ge(taken[TAKER[g - LIN_BANKS]], TAKEN[g - LIN_BANKS])
                return bank[g % LIN_BANKS]

            def linear(stage, j, n, lhs, rhs, K, at=0, rows=P):
                b = group(GROUP0[stage] + j)
                for k in range(K):
                    m = mm(b[0:rows, at:at + n], lhs(k), rhs(k), k == 0, k == K - 1, tells=k == K - 1)
                m.then_inc(lin_ready, 1)

            def used():
                owed[0] += 1

            def mods(part, a, b):
                which, first, n, s0 = MOD_PARTS[part]
                for o in range(a, b):
                    s = s0 + o // 4
                    v = strip(s)
                    col = (which * NMOD + first + o) * 2
                    for k in range(KD):
                        at = ((o % 4) * KD + k) * P
                        m = pe.matmul(bank[7][:, col:col + 2], v[:, at:at + P], SILC[:, which // 2, k, :],
                                      start=(k == 0), stop=(k == KD - 1))
                        if owed[0] and k == 0:
                            m.then_inc(strip_used, 1)
                            owed[0] -= 1
                    if o % 4 == 3:
                        m.then_inc(strip_used, 1)

            def norm(name, w, x, mean=False):
                K, base = NCHUNK[name], NBASE[name]
                if mean:
                    for k in range(K):
                        m = mm(bank[6][:, 0:w], ones, x(k), k == 0, k == K - 1, tells=k == K - 1)
                    m.then_inc(sum_ready, 1)
                for k in range(K):
                    pe.wait_ge(sq_ready, base + k + 1)
                    pe.matmul(bank[6][:, 0:w], ones, SQ[:, (base + k) % 2, 0:w], start=(k == 0), stop=(k == K - 1))\
                      .then_inc(sq_used, 1)

            def attention(name, q, k, v, PR, PT, YT, bias=None, fill=None):
                nb, u0 = ATT[name]
                b0 = u0 // HEADS
                for t in range(nb * HEADS + 5):
                    if t < nb * HEADS:
                        g, b, h = u0 + t, t // HEADS, t % HEADS
                        lo = 0 if b < TB else T
                        if g >= 3:
                            pe.wait_ge(at_p, g - 2)
                        s = bank[g % 3][:, 0:2 * T - lo]
                        masked = bias is not None and b < TB
                        m = mm(s, q(h, b), k(h, lo), True, not masked, tells=not masked)
                        if masked:
                            m = pe.matmul(s[:, 0:T], ident, bias(h, b), start=False, stop=True)
                        m.then_inc(at_s, 1)
                    if fill is not None:
                        fill(t)
                    if 0 <= t - 2 < nb * HEADS:
                        g, b = u0 + t - 2, (t - 2) // HEADS
                        kb = 4 if b < TB else 2
                        pe.wait_ge(at_p, g + 1)
                        if g >= 2:
                            pe.wait_ge(at_ptc, g - 1)
                        for j in range(kb):
                            m = pe.transpose(bank[3 + g % 2][:, j * P:(j + 1) * P],
                                             PR[:, g % 3, j * P:(j + 1) * P], ident)
                        m.then_inc(at_t, 1)
                    if 0 <= t - 3 < nb * HEADS:
                        g, b, h = u0 + t - 3, (t - 3) // HEADS, (t - 3) % HEADS
                        kb, off = (4, 0) if b < TB else (2, 2)
                        pe.wait_ge(at_ptc, g + 1)
                        if h == 0 and b0 + b:
                            pe.wait_ge(at_ytm, b0 + b)
                        for j in range(kb):
                            m = mm(bank[5][:, h * 64:(h + 1) * 64], PT[:, g % 2, j * P:(j + 1) * P],
                                   v(off + j, h), j == 0, j == kb - 1, tells=j == kb - 1)
                        m.then_inc(at_pv, 1)
                    if t >= 4 and (t - 4) % HEADS == HEADS - 1:
                        b = b0 + (t - 4) // HEADS
                        pe.wait_ge(at_ytm, b + 1)
                        if b:
                            pe.wait_ge(at_y, b)
                        for c in range(4):
                            m = pe.transpose(bank[6][:, c * P:(c + 1) * P], YT[:, c * P:(c + 1) * P], ident)
                        m.then_inc(at_yt, 1)

            pe.wait_ge(par_in, 16)
            pe.wait_ge(x_in, 16)
            norm("n1_0", 2 * T, None)
            pe.wait_ge(silc_ready, 1)
            mods("ada0a", 0, 16)

            pe.wait_ge(norm_out, NOUT["n1_0"] + KD)
            for j in range(4):
                linear("even_q", j, T, lambda k: tile("even_in", j * KD + k), lambda k: A[:, k, 0:T], KD)
            used()
            linear("even_k", 0, 2 * T, lambda k: tile("even_in", 32 + k), lambda k: A[:, k, :], KD)
            b = group(GROUP0["even_v"])
            for blk in range(4):
                for k in range(KD):
                    m = mm(b[:, blk * P:(blk + 1) * P], A[:, k, blk * P:(blk + 1) * P], tile("even_in", 40 + k),
                           k == 0, k == KD - 1, tells=blk == 3 and k == KD - 1)
            m.then_inc(lin_ready, 1)
            for j in range(4):
                linear("even_u", j, T, lambda k: tile("even_in", 48 + j * KD + k), lambda k: A[:, k, 0:T], KD)
                if j == 1:
                    used()
            for blk in range(TB):
                linear("even_z", blk, 512, lambda k: A[:, k, blk * P:(blk + 1) * P],
                       lambda k: tile("even_in", 80 + 4 * k, 4), KD)
            used()
            used()
            pe.wait_ge(taba_in, 16)
            for j in range(5):
                wait_taken(pe, "even_k" if j == 4 else "even_q", 0 if j == 4 else j)
                linear("even_rope", j, T, lambda k: tab(TA, "swap"), lambda k: QRAW[:, j, :], 1)
            pe.wait_ge(wsp_in, 16)
            for n in range(TB):
                pe.wait_ge(z_norm, n + 1)
                b = group(GROUP0["even_gate"] + n)
                for h in range(HEADS):
                    r = 64 * (h % 2)
                    m = mm(b[r:r + 64, (h // 2) * P:(h // 2 + 1) * P], Z1[:, n, h * 64:(h + 1) * 64], WSP[:, h, :],
                           True, True, tells=h == HEADS - 1)
                m.then_inc(lin_ready, 1)
            last_taken(pe, "even_gate")
            pe.wait_ge(rope_done, 5)

            def fill_even(t):
                if t < 8:
                    mods("ada0b", 4 * t, 4 * t + 4)
                elif 10 <= t < 18:
                    if t == 10:
                        pe.wait_ge(mod_taken, 2)
                    mods("ada1", 4 * (t - 10), 4 * (t - 10) + 4)

            attention("even",
                      lambda h, b: QK[64 * (h // 4):64 * (h // 4) + 64, h % 4, b * P:(b + 1) * P],
                      lambda h, lo: KV_K[64 * (h // 4):64 * (h // 4) + 64, lo:2 * T],
                      lambda kb, h: V1[:, kb, 64 * (h // 4):64 * (h // 4) + 64],
                      PR1, PT1, YT1, bias=lambda h, b: tab(TA, "mask", b * T, T), fill=fill_even)
            pe.wait_ge(at_y, 2)
            pe.wait_ge(sg_ready, TB * 4)
            for j in range(KD):
                linear("even_out", j, T, lambda k: tile("even_out", j * KD + k), lambda k: CAT[:, k, :], KD)
                if j % 4 == 3:
                    used()
            assert FIRST["ada1b"] == FIRST["even_out"] + 2
            for o in range(32, 48):
                v = strip(FIRST["ada1b"] + (o - 32) // 4)
                for k in range(KD):
                    at = ((o % 4) * KD + k) * P
                    m = pe.matmul(bank[7][:, (NMOD + o) * 2:(NMOD + o) * 2 + 2], v[:, at:at + P], SILC[:, 0, k, :],
                                  start=(k == 0), stop=(k == KD - 1))
                    if owed[0] and k < KD - 1:
                        m.then_inc(strip_used, 1)
                        owed[0] -= 1
                if o % 4 == 3:
                    m.then_inc(strip_used, 1)

            def gather(q, e):
                for c in range(KD):
                    b = bank[c // 4]
                    for blk in range(TB):
                        m = mm(b[:, (c % 4) * P:(c % 4 + 1) * P], HT[:, blk, c * P:(c + 1) * P], GE[:, blk, :],
                               blk == 0, blk == TB - 1, tells=c == KD - 1 and blk == TB - 1)
                m.then_inc(q["gath_ready"], 1)

            def combine(q, p, i):
                pe.wait_ge(q["y_copied"], i * 2 + 33 * p + 1)
                pe.wait_ge(q["spt_ready"], i + 17 * p + 1)
                for r in range(4):
                    pe.wait_ge(q["res_added"], i * 4 + (70 * p + r + 1))
                    for h in range(2):
                        c = 2 * r + h
                        m = pe.matmul(bank[6 + r % 2][:, h * T:(h + 1) * T], YP[:, c * P:(c + 1) * P], SPT[:, :],
                                      start=True, stop=True)
                    m.then_inc(q["comb_ready"], 1)

            def moe_pass(q, p, first, came, used_sem):
                pe.wait_ge(q["ge_ready"], 17 * p + 1)
                gather(q, 0)
                with pe.Fori(0, PAIRS) as i:
                    slot = [ring[:, (first + j) % RING, :] for j in range(RING)]
                    due = [0]

                    def expert_up(e):
                        for half, ready in ((0, "gate_ready"), (1, "up_ready")):
                            j = 2 * e + half
                            came(i, j)
                            for o in range(4):
                                for k in range(KD):
                                    m = pe.matmul(bank[j][:, o * C:(o + 1) * C],
                                                  slot[j][:, (o * KD + k) * P:(o * KD + k + 1) * P],
                                                  XG[:, k, e * C:(e + 1) * C], start=(k == 0), stop=(k == KD - 1))
                                    if due[0] and k == 0:
                                        m.then_inc(used_sem, 1)
                                        due[0] -= 1
                            m.then_inc(q[ready], 1)
                            due[0] += 1

                    def expert_down(e):
                        came(i, 4 + e)
                        pe.wait_ge(q["hid_ready"], i * 2 + (32 * p + e + 1))
                        for h in range(2):
                            for k in range(4):
                                m = pe.matmul(bank[4 + h][e * C:(e + 1) * C, :], HE[:, e, k * C:(k + 1) * C],
                                              slot[4 + e][:, k * D + h * 512:k * D + (h + 1) * 512],
                                              start=(k == 0), stop=(k == 3))
                                if due[0] and k == 0:
                                    m.then_inc(used_sem, 1)
                                    due[0] -= 1
                        m.then_inc(q["y_ready"], 1)
                        due[0] += 1

                    pe.wait_ge(q["xg_ready"], i + 17 * p + 1)
                    expert_up(0)
                    combine(q, p, i)
                    expert_up(1)
                    expert_down(0)
                    pe.wait_ge(q["ge_ready"], i + (17 * p + 2))
                    gather(q, i + 1)
                    expert_down(1)
                    pe.wait_ge(q["gw_ready"], i + (17 * p + 1))
                    pe.wait_ge(q["res_added"], i * 4 + (70 * p + 6))
                    pe.transpose(bank[6][:, 0:P], GW[:, 0, :], ident).then_inc(used_sem, 1)
                    pe.transpose(bank[6][:, P:2 * P], GW[:, 1, :], ident).then_inc(q["tr_ready"], 1)
                combine(q, p, PAIRS)

            def moe(l):
                for j in range(4):
                    b = group(GROUP0[f"turn{l}"] + j)
                    for c in range(4):
                        cc = (j % 2) * 4 + c
                        m = pe.transpose(b[:, c * P:(c + 1) * P], A[:, cc, (j // 2) * P:(j // 2 + 1) * P], ident)
                        if owed[0] and c < 3:
                            m.then_inc(strip_used, 1)
                            owed[0] -= 1
                    m.then_inc(lin_ready, 1)
                b = group(GROUP0[f"route{l}"])
                for blk in range(TB):
                    for k in range(KD):
                        m = mm(b[:, blk * ROUTES:(blk + 1) * ROUTES], A[:, k, blk * P:(blk + 1) * P],
                               tab(TA, "router", (l * KD + k) * ROUTES, ROUTES), k == 0, k == KD - 1, tells=blk == 1 and k == KD - 1)
                m.then_inc(lin_ready, 1)
                b = group(GROUP0[f"rank{l}"])
                pe.wait_ge(rt_mask, l + 1)
                mm(b[:, 0:32], before, MM[:, 0, 0:32], True, True)
                mm(b[:, 32:64], ones, MM[:, 0, 0:32], True, False)
                mm(b[:, 32:64], before, MM[:, 1, 0:32], False, True)
                mm(b[:, 64:96], ones, MM[:, 0, 0:32], True, False)
                mm(b[:, 64:96], ones, MM[:, 1, 0:32], False, True, tells=True).then_inc(lin_ready, 1)
                last_taken(pe, f"rank{l}")
                assert not owed[0]
                first = FIRST[f"moe{l}"]

                def came(i, j):
                    s = first + j
                    pe.wait_ge(strip_in[s % RING], i * 16 + 16 * (s // RING + 1))

                moe_pass(main, l, first, came, strip_used)
                full = pe.value_load(FLAG[0:1, l:l + 1], min_val=0, max_val=1)
                with pe.If(full > 0):
                    with pe.Fori(0, PASSES - 1) as p:
                        moe_pass(over[l], p, first,
                                 lambda i, j: pe.wait_ge(over_in[l][j], p * (16 * PAIRS) + i * 16 + 16), over_used[l])
                    pe.wait_ge(over[l]["res_added"], 70 * (PASSES - 1))
                pe.wait_ge(main["res_added"], 70 * (l + 1))

            norm("n2_0", T, None)
            pe.wait_ge(norm_out, NOUT["n2_0"] + KD)
            pe.wait_ge(mod_taken, 3)
            moe(0)

            norm("n1_1", T, None)
            pe.wait_ge(norm_out, NOUT["n1_1"] + KD)

            def odd_strip(n):
                return FIRST["odd"] + n * 4 + n if n < 6 else FIRST["odd"] + 30 + (n - 6)

            def odd_tile(n):
                v = strip(odd_strip(n // TILES))
                return v[:, (n % TILES) * P:(n % TILES + 1) * P]

            filler = [s for s in range(FIRST["odd"], FIRST["moe1"]) if s not in [odd_strip(n) for n in range(8)]]

            def m2(n):
                v = strip(filler[n])
                for o in range(4 * n, 4 * n + 4):
                    col = (2 * NMOD + o) * 2
                    for k in range(KD):
                        at = ((o % 4) * KD + k) * P
                        m = mm(bank[7][:, col:col + 2], v[:, at:at + P], SILC[:, 1, k, :], k == 0, k == KD - 1)
                used()

            n = 0
            for j in range(3 * KD):
                linear("odd_in", j, T, lambda k: odd_tile(j * KD + k), lambda k: A[:, k, 0:T], KD)
                if j % 4 == 3:
                    used()
                    for _ in range(4):
                        m2(n)
                        n += 1
            pe.wait_ge(cv_ready, KD)
            for j in range(KD):
                linear("odd_out", j, T, lambda k: odd_tile(192 + j * KD + k), lambda k: CV[:, k, :], KD)
                if j % 4 == 3:
                    used()
            norm("n2_1", T, None)
            pe.wait_ge(norm_out, NOUT["n2_1"] + KD)
            pe.wait_ge(mod_taken, 4)
            moe(1)
            norm("final", T, None)

            pe.wait_ge(ctx2_in, 16)
            pe.wait_ge(tabb_in, 16)
            pe.wait_ge(mid_ready, NMID["final"] + KD)
            norm("ln_in", 2 * T, lambda k: X[:, k, :], mean=True)
            for l in range(2):
                w = streams(l)
                pe.wait_ge(a_ready, KD * (1 + 3 * l))
                st = f"l{l}_na"
                for blk in range(w // P):
                    linear(f"f{l}", blk, 512, lambda k: A[:, k, blk * P:(blk + 1) * P], lambda k: tile(st, 4 * k, 4), KD)
                used()
                for s in range(w // T):
                    for g in range(4):
                        for blk in range(TB):
                            wait_taken(pe, f"f{l}", s * TB + blk)
                        linear(f"dft{l}", s * 4 + g, 2 * T, lambda k: FT[:, s * TB + k, g * P:(g + 1) * P],
                               lambda k: tab(TC, "dft", k * 2 * T, 2 * T), TB)
                for j in range(4 * w // T):
                    wait_taken(pe, f"dft{l}", j)
                    linear(f"idft{l}", j, T, lambda k: tab(TC, "cd" if k == 0 else "sd"),
                           lambda k: FU[:, j, k * T:(k + 1) * T], 2)
                last_taken(pe, f"idft{l}")
                for j in range(4):
                    linear(f"nq{l}", j, w, lambda k: tile(st, 32 + j * KD + k), lambda k: A[:, k, 0:w], KD)
                used()
                for j in range(4):
                    linear(f"nk{l}", j, 2 * T, lambda k: tile(st, 64 + j * KD + k), lambda k: A[:, k, :], KD)
                used()
                for blk in range(4):
                    linear(f"nv{l}", blk, 512, lambda k: A[:, k, blk * P:(blk + 1) * P],
                           lambda k: tile(st, 96 + 4 * k, 4), KD)
                used()
                last_taken(pe, f"nv{l}")
                bs = strip(FIRST[f"l{l}_bias"])
                attention(f"na{l}",
                          lambda h, b: NQ[64 * (h % 2):64 * (h % 2) + 64, h // 2, b * P:(b + 1) * P],
                          lambda h, lo: NK[64 * (h % 2):64 * (h % 2) + 64, h // 2, lo:2 * T],
                          lambda kb, h: V2[:, kb, h * 64:(h + 1) * 64], PR2, PT2, YT2,
                          bias=lambda h, b: bs[:, (h * TB + b) * T:(h * TB + b + 1) * T])
                used()
                st = f"l{l}_low"
                for j in range(4):
                    n = w if j < 2 else 2 * T
                    linear(f"low{l}", j, n, lambda k: tile(st, j * KD + k), lambda k: A[:, k, 0:n], KD)
                used()
                pe.wait_ge(at_y, (ATT[f"na{l}"][1] // HEADS) + ATT[f"na{l}"][0])
                norm(f"cq{l}", w, None)
                norm(f"ckv{l}", 2 * T, None)
                wait_taken(pe, f"low{l}", 3)
                linear(f"krope{l}", 0, T, lambda k: tab(TC, "swap"), lambda k: LOW[:, 3, 0:T], 1)
                pe.wait_ge(mid_ready, NMID[f"ckv{l}"] + 1)
                st = f"l{l}_up"
                for j in range(8):
                    linear(f"mq{l}", j, w, lambda k: tile(st, 2 * j + k), lambda k: LOW[:, k, 0:w], 2)
                for j in range(8):
                    linear(f"mk{l}", j, 2 * T, lambda k: tile(st, 16 + j), lambda k: LOW[:, 2, :], 1)
                for blk in range(4):
                    linear(f"mv{l}", blk, 512, lambda k: LOW[:, 2, blk * P:(blk + 1) * P], lambda k: tile(st, 24, 4), 1)
                used()
                for j in range(8):
                    wait_taken(pe, f"mq{l}", j)
                    linear(f"qrope{l}", j, T, lambda k: tab(TC, "swap"), lambda k: A[:, j, 0:T], 1)
                last_taken(pe, f"qrope{l}")
                pe.wait_ge(rope_done, 5 + 9 * (l + 1))
                pe.wait_ge(kr_copied, 8 * (l + 1))
                attention(f"mla{l}",
                          lambda h, b: A[0:MLA_ROWS, h, b * P:(b + 1) * P],
                          lambda h, lo: MK[0:MLA_ROWS, h, lo:2 * T],
                          lambda kb, h: V2[:, kb, h * 64:(h + 1) * 64], PR2, PT2, YT2)
                pe.wait_ge(at_y, (ATT[f"mla{l}"][1] // HEADS) + ATT[f"mla{l}"][0])
                pe.wait_ge(a_ready, KD * (2 + 3 * l))
                st = f"l{l}_merge"
                for o in range(KD):
                    for b in range(3):
                        at = (o * 3 + b) * 12
                        j = (o * 3 + b) * 2
                        linear(f"merge{l}", j, w, lambda k: tile(st, at + k), lambda k: A[:, k, 0:w], KD)
                        linear(f"merge{l}", j + 1, w, lambda k: tile(st, at + KD + k), lambda k: YB[b][:, k, 0:w], 4)
                        if (at + 12) // TILES > at // TILES:
                            used()
                wait_taken(pe, f"merge{l}", 6 * KD - 1)
                for j in range(KD):
                    linear(f"out{l}", j, w, lambda k: tile(f"l{l}_out", j * KD + k), lambda k: MG[:, k, 0:w], KD)
                    if j % 4 == 3:
                        used()
                wait_taken(pe, f"out{l}", KD - 1)
                norm(f"ln1_{l}", w, lambda k: X[:, k, 0:w], mean=True)
                pe.wait_ge(a_ready, KD * (3 + 3 * l))
                st = f"l{l}_ffn"
                for j in range(2 * KF):
                    linear(f"up{l}", j, w, lambda k: tile(st, j * KD + k), lambda k: A[:, k, 0:w], KD)
                    if j % 4 == 3:
                        used()
                wait_taken(pe, f"up{l}", 2 * KF - 1)
                for j in range(KD):
                    at = 2 * KF * KD + j * KF
                    linear(f"down{l}", j, w, lambda k: tile(st, at + k), lambda k: HB[:, k, 0:w], KF)
                    if (at + KF) // TILES > at // TILES:
                        used()
                used()
                wait_taken(pe, f"down{l}", KD - 1)
                norm(f"ln2_{l}", w, lambda k: X[:, k, 0:w], mean=True)

        @block.scalar
        def _(act):
            act.dma_start(par_sb[:, :], par).then_inc(par_in, 16)
            act.dma_start(X[:, :, :], xt).then_inc(x_in, 16)
            act.dma_start(tab_sb[:, 0:N_TA], tab_a).then_inc(taba_in, 16)
            act.dma_start(WSP, wsp_d).then_inc(wsp_in, 16)

            def take(stage, j, n, rows=P):
                g = GROUP0[stage] + j
                act.wait_ge(lin_ready, g + 1)
                return bank[g % LIN_BANKS][0:rows, 0:n]

            def norm(name, w, x, out_, halves, dim, eps, mean=False):
                K, base = NCHUNK[name], NBASE[name]
                for k in range(K):
                    if mean:
                        act.wait_ge(xc_ready, NXC[name] + k + 1)
                    if base + k >= 2:
                        act.wait_ge(sq_used, base + k - 1)
                    act.activation(SQ[:, (base + k) % 2, 0:w], x(k), ACT.Square).then_inc(sq_ready, 1)
                act.wait_ge(sq_used, base + K)
                act.activation(RSTD[:, 0:w], bank[6][:, 0:w], ACT.Sqrt, bias=EPS[:, eps:eps + 1], scale=1.0 / dim)\
                   .then_inc(std_ready, 1)
                for k in range(K if halves else 0):
                    act.wait_ge(mid_ready, NMID[name] + k + 1)
                    for lo, hi, b in halves:
                        m = act.activation(out_(k)[:, lo:hi], out_(k)[:, lo:hi], ACT.Identity, bias=b(k))
                    m.then_inc(norm_out, 1)

            def attention(name, scale, PR, PT, sink=False):
                nb, u0 = ATT[name]
                for t in range(nb * HEADS + 4):
                    if t < nb * HEADS:
                        g, b, h = u0 + t, t // HEADS, t % HEADS
                        n = 2 * T if b < TB else T
                        pb = (u0 // HEADS + b) % 2
                        act.wait_ge(at_nm, g + 1)
                        if g >= 3:
                            act.wait_ge(at_t, g - 2)
                        act.activation(PR[:, g % 3, 0:n], bank[g % 3][:, 0:n], ACT.Exp, bias=NM[:, pb, h:h + 1],
                                       scale=scale, accum_out=SM[:, pb, h:h + 1]).then_inc(at_p, 1)
                    if 0 <= t - 2 < nb * HEADS:
                        g, b = u0 + t - 2, (t - 2) // HEADS
                        n = 2 * T if b < TB else T
                        act.wait_ge(at_t, g + 1)
                        if g >= 2:
                            act.wait_ge(at_pv, g - 1)
                        act.activation(PT[:, g % 2, 0:n], bank[3 + g % 2][:, 0:n], ACT.Copy).then_inc(at_ptc, 1)
                    if sink and t >= 3 and (t - 3) % HEADS == HEADS - 1:
                        b = (t - 3) // HEADS
                        act.wait_ge(at_d, b + 1)
                        act.activation(ES[:, b % 2, :], ES[:, b % 2, :], ACT.Exp).then_inc(at_es, 1)

            act.wait_ge(par_in, 16)
            for i, name in enumerate(("c", "c_2")):
                m = act.activation(SILC[:, i, :, :].rearrange("p a b -> p (a b)"), par_(name), ACT.Silu)
            m.then_inc(silc_ready, 1)
            act.wait_ge(x_in, 16)
            act.wait_ge(eps_ready, 1)
            mod = lambda which, first, k, s: MOD[:, which, first + k, s:s + 1]
            norm("n1_0", 2 * T, lambda k: X[:, k, :], lambda k: A[:, k, :],
                 [(0, T, lambda k: mod(0, 0, k, 0)), (T, 2 * T, lambda k: mod(0, 0, k, 1))], D, 0)
            for j in range(4):
                act.activation(U1[:, j, :], take("even_u", j, T), ACT.Gelu).then_inc(taken["A"], 1)
            for blk in range(TB):
                act.activation(Z1[:, blk, :], take("even_z", blk, 512), ACT.Gelu).then_inc(taken["A"], 1)
            for n in range(TB):
                act.wait_ge(z_var, n + 1)
                act.activation(BN[:, n, 8:9], BN[:, n, 7:8], ACT.Sqrt, bias=EPS[:, 0:1]).then_inc(z_std, 1)
            attention("even", 1.0, PR1, PT1, sink=True)

            def moe_pass(q, p):
                act.activation(OPEN, ident[:, 0:1], ACT.Copy).then_inc(q["y_copied"], 1)

                def rows(i):
                    act.wait_ge(q["gath_ready"], i + (17 * p + 1))
                    for h in range(2):
                        m = act.activation(XG[:, 4 * h:4 * h + 4, :].rearrange("p a b -> p (a b)"), bank[h][:, :], ACT.Copy)
                    m.then_inc(q["xg_ready"], 1)

                rows(0)
                with act.Fori(0, PAIRS) as i:
                    def silu(e):
                        act.wait_ge(q["gate_ready"], i * 2 + (32 * p + e + 1))
                        act.activation(SIL[:, e, :], bank[2 * e][:, 0:4 * C], ACT.Silu).then_inc(q["sil_ready"], 1)

                    def copy(e):
                        act.wait_ge(q["y_ready"], i * 2 + (32 * p + e + 1))
                        for h in range(2):
                            m = act.activation(YP[e * C:(e + 1) * C, h * 512:(h + 1) * 512],
                                               bank[4 + h][e * C:(e + 1) * C, :], ACT.Copy)
                        m.then_inc(q["y_copied"], 1)

                    silu(0)
                    silu(1)
                    copy(0)
                    rows(i + 1)
                    copy(1)

            def moe(l):
                for j in range(4):
                    act.activation(HT[:, j // 2, (j % 2) * 512:(j % 2) * 512 + 512], take(f"turn{l}", j, 512), ACT.Copy)\
                       .then_inc(taken["A"], 1)
                act.wait_ge(rt_exp_in, l + 1)
                for b in range(TB):
                    act.activation(SML[:, b, 8:12], LG[:, b, 0:4], ACT.Exp, bias=SML[:, b, 0:1], accum_out=SML[:, b, 1:2])
                    m = act.activation(SML[:, b, 3:4], SML[:, b, 2:3], ACT.Exp)
                m.then_inc(rt_exp, 1)
                if l == 1:
                    act.wait_ge(lin_ready, GROUP0["route1"] + 1)
                    act.wait_ge(flag_ready, 2)
                    act.dma_start(tab_sb[:, 0:N_TC], tab_b).then_inc(tabb_in, 16)
                    act.dma_start(X[:, :, T:2 * T], ctx2t).then_inc(ctx2_in, 16)
                moe_pass(main, l)
                act.wait_ge(flag_ready, l + 1)
                full = act.value_load(FLAG[0:1, l:l + 1], min_val=0, max_val=1)
                with act.If(full > 0):
                    with act.Fori(0, PASSES - 1) as p:
                        moe_pass(over[l], p)
                    act.wait_ge(over[l]["res_added"], 70 * (PASSES - 1))
                act.wait_ge(main["res_added"], 70 * (l + 1))

            last_taken(act, "even_out")
            norm("n2_0", T, lambda k: X[:, k, 0:T], lambda k: A[:, k, 0:T], [(0, T, lambda k: mod(0, 24, k, 0))], D, 0)
            moe(0)
            norm("n1_1", T, lambda k: X[:, k, 0:T], lambda k: A[:, k, 0:T], [(0, T, lambda k: mod(1, 0, k, 0))], D, 0)
            for c in range(KD):
                if c >= 2:
                    act.wait_ge(cv_ready, c - 1)
                act.activation(BG[:, c % 2, :], take("odd_in", 3 * c, T), ACT.Copy).then_inc(taken["A"], 1)
                act.activation(CG[:, c % 2, :], take("odd_in", 3 * c + 1, T), ACT.Copy).then_inc(taken["A"], 1)
            last_taken(act, "odd_out")
            norm("n2_1", T, lambda k: X[:, k, 0:T], lambda k: A[:, k, 0:T], [(0, T, lambda k: mod(1, 24, k, 0))], D, 0)
            moe(1)
            norm("final", T, lambda k: X[:, k, 0:T], None, None, D, 0)

            act.wait_ge(ctx2_in, 16)
            norm("ln_in", 2 * T, lambda k: X[:, k, :], lambda k: X[:, k, :],
                 [(0, 2 * T, lambda k: par_("lni_b", k, 1))], D, 1, mean=True)
            for l in range(2):
                w = streams(l)
                for j in range(4 * w // T):
                    act.activation(FU[:, j, :], take(f"dft{l}", j, 512), ACT.Copy).then_inc(taken["A"], 1)
                last_taken(act, f"idft{l}")
                for j in range(4):
                    act.activation(NK[:, j, :], take(f"nk{l}", j, 512), ACT.Copy).then_inc(taken["A"], 1)
                for j in range(4):
                    act.activation(V2[:, j, :], take(f"nv{l}", j, 512), ACT.Copy).then_inc(taken["A"], 1)
                attention(f"na{l}", 1.0, PR2, PT2)
                for j in range(2):
                    wait_taken(act, f"low{l}", j)
                norm(f"cq{l}", w, lambda k: LOW[:, k, 0:w], None, None, 2 * P, 1)
                wait_taken(act, f"low{l}", 2)
                act.wait_ge(mid_ready, NMID[f"cq{l}"] + 2)
                norm(f"ckv{l}", 2 * T, lambda k: LOW[:, 2, :], None, None, P, 1)
                for j in range(8):
                    act.activation(A[:, j, 0:w], take(f"mq{l}", j, w), ACT.Copy).then_inc(taken["A"], 1)
                for j in range(8):
                    act.activation(MK[0:64, j, :], take(f"mk{l}", j, 512, 64), ACT.Copy).then_inc(taken["A"], 1)
                attention(f"mla{l}", MLA_SCALE, PR2, PT2)
                act.wait_ge(at_y, (ATT[f"mla{l}"][1] // HEADS) + ATT[f"mla{l}"][0])
                for j in range(3 * KD):
                    if j >= 2:
                        wait_taken(act, f"merge{l}", 2 * (j - 2) + 1)
                    act.activation(SG[:, j % 2, 0:w], take(f"merge{l}", 2 * j, w), ACT.Sigmoid).then_inc(taken["A"], 1)
                norm(f"ln1_{l}", w, lambda k: X[:, k, 0:w], lambda k: X[:, k, 0:w],
                     [(0, w, lambda k: par_("ln1_b", l * KD + k, 1))], D, 1, mean=True)
                for j in range(KF):
                    if j >= 2:
                        wait_taken(act, f"up{l}", 2 * (j - 2) + 1)
                    act.activation(SB_[:, j % 2, 0:w], take(f"up{l}", 2 * j, w), ACT.Silu).then_inc(taken["A"], 1)
                norm(f"ln2_{l}", w, lambda k: X[:, k, 0:w], lambda k: X[:, k, 0:w],
                     [(0, w, lambda k: par_("ln2_b", l * KD + k, 1))], D, 1, mean=True)

        @block.vector
        def _(dve):
            own = [0]

            def link(ins):
                own[0] += 1
                ins.then_inc(dve_own, 1)
                dve.wait_ge(dve_own, own[0])

            def take(stage, j, n=None, rows=None):
                g = GROUP0[stage] + j
                dve.wait_ge(lin_ready, g + 1)
                b = bank[g % LIN_BANKS]
                return b[:, 0:n] if n else b

            def norm(name, w, x, out_, halves, dim, mean=False):
                K = NCHUNK[name]
                src = x
                if mean:
                    dve.wait_ge(sum_ready, NMEAN[name] + 1)
                    link(dve.tensor_scalar(MEAN[:, 0:w], bank[6][:, 0:w], 1.0 / dim, None, ALU.mult))
                    for k in range(K):
                        dve.tensor_tensor(out_(k), x(k), MEAN[:, 0:w], ALU.subtract).then_inc(xc_ready, 1)
                    dve.wait_ge(xc_ready, NXC[name] + K)
                    src = out_
                dve.wait_ge(std_ready, NSTAT[name] + 1)
                link(dve.reciprocal(RSTD[:, 0:w], RSTD[:, 0:w]))
                for k in range(K):
                    for lo, hi, s in halves:
                        m = dve.scalar_tensor_tensor(out_(k)[:, lo:hi], src(k)[:, lo:hi], s(k), RSTD[:, lo:hi],
                                                     ALU.mult, ALU.mult)
                    m.then_inc(mid_ready, 1)

            def attention(name, scale, YT, y, sink=False):
                nb, u0 = ATT[name]
                for t in range(nb * HEADS + 5):
                    if t < nb * HEADS:
                        g, b, h = u0 + t, t // HEADS, t % HEADS
                        n = 2 * T if b < TB else T
                        pb = (u0 // HEADS + b) % 2
                        dve.wait_ge(at_s, g + 1)
                        link(dve.reduce_max(MX[:, pb, h:h + 1], bank[g % 3][:, 0:n], AXX))
                        if sink:
                            i = dve.tensor_scalar(NM[:, pb, h:h + 1], MX[:, pb, h:h + 1], par_("sink", h, 1), -1.0,
                                                  ALU.max, ALU.mult)
                        else:
                            i = dve.tensor_scalar(NM[:, pb, h:h + 1], MX[:, pb, h:h + 1], -scale, None, ALU.mult)
                        i.then_inc(at_nm, 1)
                    if name == "even" and t == 9:
                        take_mods(0, 16, 48, FIRST["ada0b"] + 8, 2)
                    if t >= 3 and (t - 3) % HEADS == HEADS - 1:
                        b = u0 // HEADS + (t - 3) // HEADS
                        pb = b % 2
                        if sink:
                            dve.wait_ge(at_nm, 8 * b + 8)
                            dve.tensor_tensor(ES[:, pb, :], par_("sink"), NM[:, pb, :], ALU.add).then_inc(at_d, 1)
                            dve.wait_ge(at_es, b + 1)
                            link(dve.tensor_tensor(SM[:, pb, :], SM[:, pb, :], ES[:, pb, :], ALU.add))
                        dve.wait_ge(at_p, 8 * b + 8)
                        link(dve.reciprocal(SM[:, pb, :], SM[:, pb, :]))
                        dve.wait_ge(at_pv, 8 * b + 8)
                        dve.tensor_tensor(YT.rearrange("p (h d) -> p h d", h=HEADS),
                                          bank[5][:, :].rearrange("p (h d) -> p h d", h=HEADS),
                                          SM[:, pb, :].unsqueeze(2).to_broadcast([P, HEADS, 64]), ALU.mult)\
                           .then_inc(at_ytm, 1)
                    if t >= 4 and (t - 4) % HEADS == HEADS - 1:
                        bb = (t - 4) // HEADS
                        dve.wait_ge(at_yt, u0 // HEADS + bb + 1)
                        dve.tensor_copy(y(bb), bank[6][:, :].rearrange("p (c n) -> p c n", c=4)).then_inc(at_y, 1)

            def take_mods(which, a, b, strips_, n):
                dve.wait_ge(strip_used, strips_)
                at, end = (which * NMOD + a) * 2, (which * NMOD + b) * 2
                flat = MOD[:, :, :, :].rearrange("p a b c -> p (a b c)")
                dve.tensor_tensor(flat[:, at:end], bank[7][:, at:end], par_("bias", at, end - at), ALU.add)\
                   .then_inc(mod_taken, 1)
                dve.wait_ge(mod_taken, n)

            def gain(slot, which, first, s, g):
                return dve.scalar_tensor_tensor(GSC[:, slot, :], MOD[:, which, first:first + KD, s], 1.0, g, ALU.add, ALU.mult)

            def residual(stage, j, n, gate):
                dve.scalar_tensor_tensor(X[:, j, 0:n], take(stage, j, n), gate, X[:, j, 0:n], ALU.mult, ALU.add)\
                   .then_inc(taken["D"], 1)

            dve.memset(EPS[:, 0:1], EPS1)
            dve.memset(EPS[:, 1:2], EPS2).then_inc(eps_ready, 1)
            dve.wait_ge(par_in, 16)
            dve.wait_ge(x_in, 16)
            take_mods(0, 0, 16, 4, 1)
            gain(0, 0, 8, 0, par_("g1", 0, KD))
            link(gain(1, 0, 8, 1, par_("g1", 0, KD)))
            norm("n1_0", 2 * T, lambda k: X[:, k, :], lambda k: A[:, k, :],
                 [(0, T, lambda k: GSC[:, 0, k:k + 1]), (T, 2 * T, lambda k: GSC[:, 1, k:k + 1])], D)
            for j in range(4):
                dve.tensor_scalar(QRAW[:, j, :], take("even_q", j, T), 0.125, None, ALU.mult).then_inc(taken["D"], 1)
            dve.tensor_copy(QRAW[:, 4, :], take("even_k", 0)[:, 0:T])
            dve.tensor_copy(KV_K[:, T:2 * T], take("even_k", 0)[:, T:2 * T]).then_inc(taken["D"], 1)
            dve.tensor_copy(V1.rearrange("p a b -> p (a b)"), take("even_v", 0)[:, :]).then_inc(taken["D"], 1)
            wait_taken(dve, "even_v", 0)
            dve.wait_ge(taba_in, 16)
            for j in range(5):
                o = QK[:, j, :] if j < 4 else KV_K[:, 0:T]
                dve.tensor_tensor(TMP1[:, j % 2, :], take("even_rope", j, T), tab(TA, "sin"), ALU.mult).then_inc(taken["D"], 1)
                link(dve.tensor_tensor(QK[:, j, :], QRAW[:, j, :], tab(TA, "cos"), ALU.mult))
                dve.tensor_tensor(o, QK[:, j, :], TMP1[:, j % 2, :], ALU.add).then_inc(rope_done, 1)
            for n in range(TB):
                wait_taken(dve, "even_z", n)
                link(dve.bn_stats(BN[:, n, 0:6], Z1[:, n, :]))
                dve.bn_aggr(BN[:, n, 6:8], BN[:, n, 0:6]).then_inc(z_var, 1)
            for n in range(TB):
                dve.wait_ge(z_std, n + 1)
                link(dve.reciprocal(BN[:, n, 9:10], BN[:, n, 8:9]))
                dve.tensor_scalar(Z1[:, n, :], Z1[:, n, :], BN[:, n, 6:7], BN[:, n, 9:10], ALU.subtract, ALU.mult)\
                   .then_inc(z_norm, 1)
            dve.wait_ge(taken["A"], TAKEN[GROUP0["even_u"] + 3])
            for n in range(TB):
                b = take("even_gate", n)
                for c in range(4):
                    i = dve.scalar_tensor_tensor(CAT[:, 4 + c, n * P:(n + 1) * P], b[:, c * P:(c + 1) * P],
                                                 par_("sgu", c, 1), tab(TA, "bsp", c * P, P), ALU.mult, ALU.add)
                i.then_inc(taken["D"], 1)
                dve.wait_ge(taken["D"], TAKEN[GROUP0["even_gate"] + n])
                for c in range(4):
                    dve.tensor_tensor(CAT[:, 4 + c, n * P:(n + 1) * P], CAT[:, 4 + c, n * P:(n + 1) * P],
                                      U1[:, c, n * P:(n + 1) * P], ALU.mult).then_inc(sg_ready, 1)
            attention("even", 1.0, YT1, lambda b: CAT[:, 0:4, b * P:(b + 1) * P], sink=True)
            for j in range(KD):
                residual("even_out", j, T, MOD[:, 0, 16 + j, 0:1])

            def moe_pass(q, p, g2):
                dve.memset(YP[:, :], 0.0).then_inc(q["res_added"], 1)
                dve.memset(SPT[:, :], 0.0).then_inc(q["res_added"], 1)
                dve.wait_ge(q["res_added"], 70 * p + 2)
                dve.tensor_copy(SPT[:, 0:1], SPT[:, 0:1]).then_inc(q["spt_ready"], 1)

                def columns_of(i, dst, by, ready):
                    for e in range(2):
                        for blk in range(TB):
                            m = dve.tensor_scalar(dst[:, blk, e * C:(e + 1) * C], par_("slot"),
                                                  RK[:, blk, bass.ds(i * 2 + e, 1)], by[:, blk, bass.ds(i * 2 + e, 1)],
                                                  ALU.is_equal, ALU.mult)
                    m.then_inc(q[ready], 1)

                def add(i):
                    dve.wait_ge(q["res_added"], i * 4 + (70 * p + 2))
                    for r in range(4):
                        dve.wait_ge(q["comb_ready"], i * 4 + (68 * p + r + 1))
                        for h in range(2):
                            c = 2 * r + h
                            m = dve.scalar_tensor_tensor(X[:, c, 0:T], bank[6 + r % 2][:, h * T:(h + 1) * T], g2(c),
                                                         X[:, c, 0:T], ALU.mult, ALU.add)
                        m.then_inc(q["res_added"], 1)

                columns_of(0, GE, MM, "ge_ready")
                columns_of(0, GW, GG, "gw_ready")
                with dve.Fori(0, PAIRS) as i:
                    def hidden(e):
                        dve.wait_ge(q["sil_ready"], i * 2 + (32 * p + e + 1))
                        dve.wait_ge(q["up_ready"], i * 2 + (32 * p + e + 1))
                        dve.tensor_tensor(HE[:, e, :], SIL[:, e, :], bank[2 * e + 1][:, 0:4 * C], ALU.mult)\
                           .then_inc(q["hid_ready"], 1)

                    hidden(0)
                    add(i)
                    dve.wait_ge(q["gath_ready"], i + (17 * p + 1))
                    columns_of(i + 1, GE, MM, "ge_ready")
                    hidden(1)
                    dve.wait_ge(q["tr_ready"], i + (16 * p + 1))
                    dve.tensor_copy(SPT[:, :], bank[6][:, 0:T]).then_inc(q["spt_ready"], 1)
                    columns_of(i + 1, GW, GG, "gw_ready")
                add(PAIRS)

            def moe(l):
                g2 = lambda c: MOD[:, l, 40 + c, 0:1]
                big = -NEG
                lg = take(f"route{l}", 0, TB * ROUTES)
                for b in range(TB):
                    dve.memset(GL8[:, b, :], NEG)
                for t_ in (RK, MM, GG):
                    dve.memset(t_, 0.0)
                dve.tensor_tensor(LG.rearrange("p a b -> p (a b)"), lg, par_("rbias", l * TB * ROUTES, TB * ROUTES), ALU.add)\
                   .then_inc(taken["D"], 1)
                wait_taken(dve, f"route{l}", 0)
                link(dve.tensor_copy(GL8[:, :, 0:4], LG[:, :, 0:4]))
                for b in range(TB):
                    m = dve.max(MX8[:, b, :], GL8[:, b, :])
                link(m)
                for b in range(TB):
                    m = dve.max_index(IX8[:, b, :], MX8[:, b, :], GL8[:, b, :])
                link(m)
                link(dve.tensor_copy(IXF, IX8))
                for b in range(TB):
                    m = dve.tensor_scalar(GM[:, b, :], par_("group"), IXF[:, b, 0:1], None, ALU.is_equal)
                link(m)
                for b in range(TB):
                    m = dve.tensor_scalar(ME[:, b, :], GM[:, b, :], big, -big, ALU.mult, ALU.add)
                link(m)
                link(dve.tensor_tensor(GM, GM, LG[:, :, 4:36], ALU.mult))
                link(dve.tensor_tensor(ME, ME, GM, ALU.add))
                for b in range(TB):
                    m = dve.max(V8[:, b, :], ME[:, b, :])
                link(m)
                for b in range(TB):
                    dve.max_index(IE8[:, b, :], V8[:, b, :], ME[:, b, :])
                dve.tensor_scalar(SML[:, :, 0], MX8[:, :, 0], -1.0, None, ALU.mult)
                link(dve.tensor_tensor(SML[:, :, 2], V8[:, :, 1], V8[:, :, 0], ALU.subtract))
                dve.tensor_copy(IEF, IE8).then_inc(rt_exp_in, 1)
                dve.wait_ge(rt_exp_in, l + 1)
                for b in range(TB):
                    dve.tensor_scalar(O0[:, b, :], par_("expert"), IEF[:, b, 0:1], None, ALU.is_equal)
                    m = dve.tensor_scalar(O1[:, b, :], par_("expert"), IEF[:, b, 1:2], None, ALU.is_equal)
                link(m)
                dve.tensor_tensor(MM[:, :, 0:32], O0, O1, ALU.add).then_inc(rt_mask, 1)
                dve.wait_ge(rt_exp, l + 1)
                link(dve.tensor_scalar(SML[:, :, 4], SML[:, :, 3], 1.0, None, ALU.add))
                link(dve.tensor_tensor(SML[:, :, 5], SML[:, :, 4], SML[:, :, 1], ALU.mult))
                link(dve.reciprocal(SML[:, :, 6], SML[:, :, 5]))
                link(dve.tensor_tensor(SML[:, :, 7], SML[:, :, 6], SML[:, :, 3], ALU.mult))
                for b in range(TB):
                    m = dve.tensor_scalar(O0[:, b, :], O0[:, b, :], SML[:, b, 6:7], None, ALU.mult)
                link(m)
                for b in range(TB):
                    m = dve.scalar_tensor_tensor(GG[:, b, 0:32], O1[:, b, :], SML[:, b, 7:8], O0[:, b, :], ALU.mult, ALU.add)
                link(m)
                r = take(f"rank{l}", 0)
                dve.tensor_copy(RK[:, :, 0:32], r[:, 0:64].rearrange("p (a b) -> p a b", a=TB))
                dve.tensor_copy(MS, r[:, 64:96]).then_inc(taken["D"], 1)
                wait_taken(dve, f"rank{l}", 0)
                link(dve.reduce_max(CMAX, MS, AXX))
                link(dve.tensor_scalar(CMAX, CMAX, float(C), None, ALU.is_gt))
                dve.tensor_copy(FLAG[:, l:l + 1], CMAX).then_inc(flag_ready, 1)
                moe_pass(main, l, g2)
                dve.wait_ge(flag_ready, l + 1)
                full = dve.value_load(FLAG[0:1, l:l + 1], min_val=0, max_val=1)
                with dve.If(full > 0):
                    q = over[l]
                    dve.wait_ge(main["res_added"], 70 * (l + 1))
                    with dve.Fori(0, PASSES - 1) as p:
                        dve.tensor_scalar(RK, RK, -float(C), None, ALU.add).then_inc(tmp_ready, 1)
                        dve.wait_ge(tmp_ready, p + 1 if l == 0 else p + 1)
                        moe_pass(q, p, g2)
                    dve.wait_ge(q["res_added"], 70 * (PASSES - 1))
                dve.wait_ge(main["res_added"], 70 * (l + 1))

            take_mods(1, 0, 48, FIRST["moe0"], 3)
            gain(2, 0, 32, 0, par_("g2", 0, KD))
            gain(3, 1, 8, 0, par_("g1", KD, KD))
            link(gain(4, 1, 32, 0, par_("g2", KD, KD)))
            last_taken(dve, "even_out")
            norm("n2_0", T, lambda k: X[:, k, 0:T], lambda k: A[:, k, 0:T], [(0, T, lambda k: GSC[:, 2, k:k + 1])], D)
            moe(0)

            norm("n1_1", T, lambda k: X[:, k, 0:T], lambda k: A[:, k, 0:T], [(0, T, lambda k: GSC[:, 3, k:k + 1])], D)
            for s in range(2):
                m = dve.memset(YC[:, s, :], 0.0)
            link(m)
            for c in range(KD):
                cw = lambda tap: par_("conv", tap * KD + c, 1)
                y, t_ = YC[:, c % 2, :], CT[:, c % 2, :]
                wait_taken(dve, "odd_in", 3 * c + 1)
                dve.tensor_tensor(y[:, 1:T + 1], CG[:, c % 2, :], take("odd_in", 3 * c + 2, T), ALU.mult)\
                   .then_inc(taken["D"], 1)
                wait_taken(dve, "odd_in", 3 * c + 2)
                link(dve.tensor_scalar(t_, y[:, 0:T], cw(0), None, ALU.mult))
                link(dve.scalar_tensor_tensor(t_, y[:, 1:T + 1], cw(1), t_, ALU.mult, ALU.add))
                link(dve.scalar_tensor_tensor(t_, y[:, 2:T + 2], cw(2), t_, ALU.mult, ALU.add))
                dve.tensor_tensor(CV[:, c, :], t_, BG[:, c % 2, :], ALU.mult).then_inc(cv_ready, 1)
            for j in range(KD):
                residual("odd_out", j, T, MOD[:, 1, 16 + j, 0:1])
            last_taken(dve, "odd_out")
            norm("n2_1", T, lambda k: X[:, k, 0:T], lambda k: A[:, k, 0:T], [(0, T, lambda k: GSC[:, 4, k:k + 1])], D)
            dve.wait_ge(strip_used, FIRST["moe1"] - 2)
            at, end = 2 * NMOD * 2, 4 * NMOD * 2
            flat = MOD[:, :, :, :].rearrange("p a b c -> p (a b c)")
            dve.tensor_tensor(flat[:, at:end], bank[7][:, at:end], par_("bias", at, end - at), ALU.add).then_inc(mod_taken, 1)
            dve.wait_ge(mod_taken, 4)
            link(dve.tensor_scalar(MODP[:, :, :, :].rearrange("p a b c -> p (a b c)"), flat[:, at:end], 1.0, None, ALU.add))
            moe(1)
            norm("final", T, lambda k: X[:, k, 0:T], lambda k: X[:, k, 0:T], [(0, T, lambda k: par_("gf", k, 1))], D)

            dve.wait_ge(mid_ready, NMID["final"] + KD)
            dve.wait_ge(ctx2_in, 16)
            dve.wait_ge(tabb_in, 16)
            norm("ln_in", 2 * T, lambda k: X[:, k, :], lambda k: X[:, k, :],
                 [(0, 2 * T, lambda k: par_("lni_g", k, 1))], D, mean=True)

            def modulate(l, shift, scale, w, after):
                for k in range(KD):
                    dve.wait_ge(norm_out, after + k + 1)
                    for s in range(w // T):
                        m = dve.tensor_scalar(A[:, k, s * T:(s + 1) * T], X[:, k, s * T:(s + 1) * T],
                                              MODP[:, l, scale + k, s:s + 1], MOD[:, 2 + l, shift + k, s:s + 1],
                                              ALU.mult, ALU.add)
                    m.then_inc(a_ready, 1)

            def outer(l, stage, gate, w):
                for j in range(KD):
                    b = take(stage, j)
                    for s in range(w // T):
                        m = dve.tensor_scalar(RT[:, j % 2, s * T:(s + 1) * T], b[:, s * T:(s + 1) * T],
                                              MODP[:, l, gate + j, s:s + 1], None, ALU.mult)
                    link(m)
                    dve.scalar_tensor_tensor(X[:, j, 0:w], X[:, j, 0:w], ALPHA, RT[:, j % 2, 0:w], ALU.mult, ALU.add)\
                       .then_inc(taken["D"], 1)
                wait_taken(dve, stage, KD - 1)

            for l in range(2):
                w = streams(l)
                modulate(l, 0, 8, 2 * T, NOUT["ln_in"] if l == 0 else NOUT["ln2_0"])
                for j in range(w // P):
                    dve.tensor_copy(FT[:, j, :], take(f"f{l}", j, 512)).then_inc(taken["D"], 1)
                for j in range(4 * w // T):
                    s, g = j // 4, j % 4
                    dve.tensor_copy(YB[0][:, g, s * T:(s + 1) * T], take(f"idft{l}", j, T)).then_inc(taken["D"], 1)
                for j in range(4):
                    dve.tensor_scalar(NQ[:, j, 0:w], take(f"nq{l}", j, w), 0.125, None, ALU.mult).then_inc(taken["D"], 1)
                attention(f"na{l}", 1.0, YT2, lambda b: YB[1][:, :, b * P:(b + 1) * P])
                for j in range(4):
                    n = w if j < 2 else 2 * T
                    dve.tensor_copy(LOW[:, j, 0:n], take(f"low{l}", j, n)).then_inc(taken["D"], 1)
                wait_taken(dve, f"low{l}", 3)
                norm(f"cq{l}", w, lambda k: LOW[:, k, 0:w], lambda k: LOW[:, k, 0:w],
                     [(0, w, lambda k: par_("gq", l * 2 + k, 1))], 2 * P)
                norm(f"ckv{l}", 2 * T, lambda k: LOW[:, 2, :], lambda k: LOW[:, 2, :],
                     [(0, 2 * T, lambda k: par_("gkv", l, 1))], P)
                rot = slice(64, 96)
                cos, sin = tab(TC, "cos")[rot, :], tab(TC, "sin")[rot, :]
                dve.tensor_tensor(QT[rot, 0, :], take(f"krope{l}", 0, T)[rot, :], sin, ALU.mult).then_inc(taken["D"], 1)
                link(dve.tensor_tensor(LOW[rot, 3, 0:T], LOW[rot, 3, 0:T], cos, ALU.mult))
                dve.wait_ge(taken["D"], TAKEN[GROUP0[f"krope{l}"]])
                dve.tensor_tensor(LOW[rot, 3, 0:T], LOW[rot, 3, 0:T], QT[rot, 0, :], ALU.add).then_inc(rope_done, 1)
                dve.wait_ge(rope_done, 5 + 9 * l + 1)
                for h in range(HEADS):
                    dve.tensor_copy(MK[rot, h, :], LOW[rot, 3, :]).then_inc(kr_copied, 1)
                for j in range(4):
                    dve.tensor_copy(V2[:, j, :], take(f"mv{l}", j, 512)).then_inc(taken["D"], 1)
                for j in range(8):
                    wait_taken(dve, f"mq{l}", j)
                    dve.tensor_tensor(QT[rot, j % 2, :], take(f"qrope{l}", j, T)[rot, :], sin, ALU.mult).then_inc(taken["D"], 1)
                    link(dve.tensor_tensor(A[rot, j, 0:T], A[rot, j, 0:T], cos, ALU.mult))
                    dve.tensor_tensor(A[rot, j, 0:T], A[rot, j, 0:T], QT[rot, j % 2, :], ALU.add).then_inc(rope_done, 1)
                attention(f"mla{l}", MLA_SCALE, YT2, lambda b: YB[2][:, :, b * P:(b + 1) * P])
                modulate(l, 0, 8, w, 0)
                for o in range(KD):
                    for b in range(3):
                        j = (o * 3 + b) * 2
                        wait_taken(dve, f"merge{l}", j)
                        s = SG[:, (o * 3 + b) % 2, 0:w]
                        if b == 0:
                            dve.tensor_tensor(MG[:, o, 0:w], s, take(f"merge{l}", j + 1, w), ALU.mult).then_inc(taken["D"], 1)
                        else:
                            link(dve.tensor_tensor(RT[:, b % 2, 0:w], s, take(f"merge{l}", j + 1, w), ALU.mult))
                            wait_taken(dve, f"merge{l}", j - 1)
                            dve.tensor_tensor(MG[:, o, 0:w], MG[:, o, 0:w], RT[:, b % 2, 0:w], ALU.add)\
                               .then_inc(taken["D"], 1)
                outer(l, f"out{l}", 16, w)
                norm(f"ln1_{l}", w, lambda k: X[:, k, 0:w], lambda k: X[:, k, 0:w],
                     [(0, w, lambda k: par_("ln1_g", l * KD + k, 1))], D, mean=True)
                modulate(l, 24, 32, w, NOUT[f"ln1_{l}"])
                for j in range(KF):
                    wait_taken(dve, f"up{l}", 2 * j)
                    dve.tensor_tensor(HB[:, j, 0:w], SB_[:, j % 2, 0:w], take(f"up{l}", 2 * j + 1, w), ALU.mult)\
                       .then_inc(taken["D"], 1)
                outer(l, f"down{l}", 40, w)
                norm(f"ln2_{l}", w, lambda k: X[:, k, 0:w], lambda k: X[:, k, 0:w],
                     [(0, w, lambda k: par_("ln2_g", l * KD + k, 1))], D, mean=True)


def _f(a):
    return np.ascontiguousarray(np.asarray(a))


def _vec(a):
    return _f(a).reshape(-1, P).T


def _fm(w):
    K, N = w.shape
    return w.reshape(K // P, P, N // P, P).transpose(2, 0, 1, 3).reshape(-1, P, P)


def _tm(w):
    K, N = w.shape
    return w.reshape(K // P, P, N // P, P).transpose(0, 2, 1, 3).reshape(-1, P, P)


def _pad(n):
    return np.zeros((n, P, P), np.float32)


def lay_out(I):
    strips = np.empty((STRIPS, P, TILES, P), np.float32)

    def put(stage, parts, first=None):
        tiles = np.concatenate(parts, 0) if len(parts) > 1 else parts[0]
        s = FIRST[stage] if first is None else first
        n = len(tiles) // TILES
        assert n * TILES == len(tiles), (stage, len(tiles))
        strips[s:s + n] = tiles.reshape(n, TILES, P, P).transpose(0, 2, 1, 3)

    ada, mod2 = I["w_ada"], I["w_mod_2"]
    put("ada0a", [_fm(ada[0][:, :16 * P])])
    put("ada0b", [_fm(ada[0][:, 16 * P:])])
    put("ada1a", [_fm(ada[1][:, :32 * P])])
    put("ada1b", [_fm(ada[1][:, 32 * P:])])
    w = I["w_in_even"][0]
    order = np.concatenate([np.r_[64 * c:64 * c + 64, 64 * (c + 4):64 * (c + 4) + 64] for c in range(4)])
    put("even_in", [_fm(w[:, :512][:, order]), _fm(w[:, 512:640]), _tm(w[:, 640:768]), _fm(w[:, 768:1280]),
                    _tm(w[:, 1280:1792]), _pad(16)])
    put("even_out", [_fm(I["w_out_even"][0])])
    for l in range(2):
        for i in range(PAIRS):
            parts = []
            for e in (2 * i, 2 * i + 1):
                parts += [_fm(I["w_gate"][l, e]), _fm(I["w_up"][l, e])]
            parts += [_tm(I["w_down"][l, e]) for e in (2 * i, 2 * i + 1)]
            put(None, parts, FIRST[f"moe{l}"] + 6 * i)
    wi, wo = I["w_in_odd"][0], I["w_out_odd"][0]
    cols = np.concatenate([np.r_[c * P:(c + 1) * P, D + c * P:D + (c + 1) * P, 2 * D + c * P:2 * D + (c + 1) * P]
                           for c in range(KD)])
    own = np.concatenate([_fm(wi[:, cols]), _fm(wo)])
    m2 = np.concatenate([_fm(mod2[0]), _fm(mod2[1])])
    s = FIRST["odd"]
    for n in range(6):
        put(None, [own[32 * n:32 * n + 32]], s + 5 * n)
        put(None, [m2[128 * n:128 * n + 128]], s + 5 * n + 1)
    put(None, [own[192:256]], s + 30)

    t = np.arange(T)
    r, cl = t // 64, t % 64
    start = np.clip(cl - 8, 0, 48)
    inside = (cl[None, :] >= start[:, None]) & (cl[None, :] < start[:, None] + 16)
    dr = r[None, :] - r[:, None] + 7
    dc = np.clip(cl[None, :] - cl[:, None] + 15, 0, 30)
    for l in range(2):
        w = I["w_in_2"][l]
        o = np.cumsum([0, 512, 512, 512, 512, 256, 128, 32])
        f, nq, nk, nv, cq, ckv, kr = (w[:, o[i]:o[i + 1]] for i in range(7))
        g = w[:, o[7]:]
        put(f"l{l}_na", [_tm(f), _fm(nq), _fm(nk), _tm(nv)])
        bias = np.where(inside[None], I["na_rpb_2"][l][:, dr, dc], np.float32(NEG)).astype(np.float32)
        strips[FIRST[f"l{l}_bias"]] = bias.reshape(HEADS, TB, P, T).transpose(2, 0, 1, 3).reshape(P, TILES, P)
        krp = np.zeros((D, P), np.float32)
        krp[:, 64:96] = kr
        put(f"l{l}_low", [_fm(cq), _fm(ckv), _fm(krp)])
        q = np.zeros((256, HEADS, P), np.float32)
        q[:, :, :64] = I["w_uq_2"][l].reshape(256, HEADS, 64)
        q[:, :, 64:96] = I["w_qr_2"][l].reshape(256, HEADS, 32)
        k = np.zeros((P, HEADS, P), np.float32)
        k[:, :, :64] = I["w_uk_2"][l].reshape(P, HEADS, 64)
        put(f"l{l}_up", [_fm(q.reshape(256, -1)), _fm(k.reshape(P, -1)), _tm(I["w_uv_2"][l]), _pad(4)])
        gt = _fm(g).reshape(3, KD, KD, P, P)
        bt = np.stack([_fm(I["w_branch_2"][l, b]).reshape(KD, 4, P, P) for b in range(3)])
        both = np.concatenate([gt, bt], 2).transpose(1, 0, 2, 3, 4).reshape(-1, P, P)
        put(f"l{l}_merge", [both])
        put(f"l{l}_out", [_fm(I["w_out_2"][l])])
        gu = np.stack([_fm(I["w_ffn_gate_2"][l]).reshape(KF, KD, P, P), _fm(I["w_ffn_up_2"][l]).reshape(KF, KD, P, P)], 1)
        put(f"l{l}_ffn", [gu.reshape(-1, P, P), _fm(I["w_ffn_down_2"][l]), _pad(16)])

    par = np.zeros((P, N_PAR), np.float32)

    def p(name, a):
        o, n = PAR[name]
        par[:, o:o + n] = a.reshape(-1, n)

    pair = lambda a, b: np.stack([_vec(a), _vec(b)], -1).reshape(P, -1)
    p("c", pair(I["c"], I["c_ctx"]))
    p("c_2", pair(I["c_2"], I["c_ctx_2"]))
    bias = np.concatenate([_vec(I["b_ada"]), _vec(I["b_mod_2"])], 1)
    p("bias", np.repeat(bias, 2, axis=1))
    p("g1", _vec(I["g_norm1"]))
    p("g2", _vec(I["g_norm2"]))
    p("gf", _vec(I["g_final"]))
    p("sgu", _vec(I["g_sgu"]))
    p("conv", _vec(I["conv_w"]))
    for a, b in (("lni_g", "ln_in_g_2"), ("lni_b", "ln_in_b_2"), ("ln1_g", "ln1_g_2"), ("ln1_b", "ln1_b_2"),
                 ("ln2_g", "ln2_g_2"), ("ln2_b", "ln2_b_2"), ("gq", "mla_q_norm_g_2"), ("gkv", "mla_kv_norm_g_2")):
        p(a, _vec(I[b]))
    p("sink", np.broadcast_to(I["attn_sink"].reshape(1, HEADS), (P, HEADS)))
    rb = np.stack([np.concatenate([I["b_router_group"][l], I["b_router_expert"][l]]) for l in range(2)])
    p("rbias", np.broadcast_to(np.repeat(rb[:, None], TB, 1).reshape(1, -1), (P, 2 * TB * ROUTES)))
    p("ident", np.eye(P, dtype=np.float32))
    p("ones", np.ones((P, P), np.float32))
    p("before", (np.arange(P)[:, None] < np.arange(P)[None, :]).astype(np.float32))
    p("expert", np.broadcast_to(np.arange(EXPERTS, dtype=np.float32), (P, EXPERTS)))
    p("group", np.broadcast_to(np.arange(EXPERTS) // (EXPERTS // GROUPS), (P, EXPERTS)).astype(np.float32))
    p("slot", np.broadcast_to(np.arange(C, dtype=np.float32), (P, C)))

    ta = np.zeros((P, N_TA), np.float32)
    tc = np.zeros((P, N_TC), np.float32)

    def q(arr, where, name, a):
        o, n = where[name]
        arr[:, o:o + n] = np.asarray(a, np.float32).reshape(P, n)

    d = np.arange(P) % 64
    inv = (10000.0 ** (-np.arange(16, dtype=np.float32) / 16)).astype(np.float32)
    pos = np.where((d < 32)[:, None], r[None, :], cl[None, :]).astype(np.float32)
    ang = (pos * inv[d % 16][:, None]).astype(np.float32)
    second = (d % 32) >= 16
    q(ta, TA, "cos", np.cos(ang))
    q(ta, TA, "sin", np.where(second[:, None], np.sin(ang), -np.sin(ang)))
    partner = np.where(second, np.arange(P) - 16, np.arange(P) + 16)
    sw = np.zeros((P, P), np.float32)
    sw[partner, np.arange(P)] = 1
    q(ta, TA, "swap", sw)
    near = np.abs(t[None, :] - t[:, None]) <= 128
    q(ta, TA, "mask", np.where(near, 0.0, NEG).reshape(TB, P, T).transpose(1, 0, 2))
    bsp = np.repeat(_f(I["b_spatial"])[0].reshape(4, 2, 1, P), 64, 2).transpose(1, 2, 0, 3)
    q(ta, TA, "bsp", bsp)
    rw = np.concatenate([I["w_router_group"], I["w_router_expert"]], 2).reshape(2, KD, P, ROUTES).transpose(2, 0, 1, 3)
    q(ta, TA, "router", rw)

    inv = (10000.0 ** (-np.arange(8, dtype=np.float32) / 8)).astype(np.float32)
    ang = np.concatenate([r[:, None].astype(np.float32) * inv, cl[:, None].astype(np.float32) * inv], 1).T
    cos, sin = np.ones((P, T)), np.zeros((P, T))
    cos[64:80] = cos[80:96] = np.cos(ang)
    sin[64:80], sin[80:96] = -np.sin(ang), np.sin(ang)
    q(tc, TC, "cos", cos)
    q(tc, TC, "sin", sin)
    sw = np.zeros((P, P), np.float32)
    i = np.arange(16)
    sw[80 + i, 64 + i] = sw[64 + i, 80 + i] = 1
    q(tc, TC, "swap", sw)
    a = 2 * np.pi * (np.outer(t, t) % T) / T
    q(tc, TC, "dft", np.concatenate([np.cos(a), np.sin(a)], 1).reshape(TB, P, 2 * T).transpose(1, 0, 2))
    i = np.arange(P)
    a = 2 * np.pi * (np.outer(i, i) % P) / P
    q(tc, TC, "cd", np.cos(a) / math.sqrt(T * P))
    q(tc, TC, "sd", -np.sin(a) / math.sqrt(T * P))

    fm = lambda a: _f(a).reshape(T, KD, P).transpose(2, 1, 0)
    return {
        "stream": strips.reshape(STRIPS, P, STRIP), "par": par, "tab_a": ta, "tab_b": tc,
        "wsp": _f(I["w_spatial"][0].transpose(2, 0, 1)),
        "xt": _f(np.concatenate([fm(I["x"]), fm(I["ctx"])], 2)), "ctx2t": _f(fm(I["ctx_2"])),
    }


def kernel(**inputs):
    import concourse.bacc as _bacc
    from concourse.bass_utils import run_bass_kernel_spmd as _run

    nc = _bacc.Bacc("TRN2", target_bir_lowering=False, num_devices=1)
    arrays = lay_out({k: np.asarray(v) for k, v in inputs.items()})
    args = [nc.dram_tensor("in_" + k, a.shape, F32, kind="ExternalInput").ap() for k, a in arrays.items()]
    args.append(nc.dram_tensor("out_0", (P, KD, T), F32, kind="ExternalOutput").ap())
    build_program(nc, *args)
    r = _run(nc, [{"in_" + k: a for k, a in arrays.items()}], core_ids=[0])
    got = r.results[0]["out_0"]
    return np.ascontiguousarray(got.transpose(2, 1, 0).reshape(1, T, D))
```

```python
import math
from contextlib import ExitStack

import concourse.bass as bass
import numpy as np
from concourse import mybir

F32 = mybir.dt.float32
I32 = mybir.dt.int32
U32 = mybir.dt.uint32
ALU = mybir.AluOpType
ACT = mybir.ActivationFunctionType
AXX = mybir.AxisListType.X

P = 128
D = 1024
KD = D // P
T = 256
TB = T // P
HEADS = 8
NMOD = 6 * KD
EXPERTS, GROUPS = 32, 4
PAIRS = EXPERTS // 2
HID = 512
C = 64
PASSES = T // C
FFN = 2816
KF = FFN // P
ROUTES = GROUPS + EXPERTS
ALPHA = 4.0 ** 0.25
EPS1, EPS2 = 1e-6, 1e-5
NEG = -1e30
MLA_SCALE = 96.0 ** -0.5
MLA_ROWS = 96

TILES = 32
RING = 6
STRIP = TILES * P
ORDER = {"even": "EMMEMMEMMEMM", "l0_merge": "EM" * 8 + "E", "l0_ffn": "EM" * 12 + "E" * 5}
STAGES = [
    ("ada0a", 4), ("even", 12), ("even_out", 2),
    ("moe0", 3 * EXPERTS), ("odd", 8), ("moe1", 3 * EXPERTS),
    ("l0_na", 4), ("l0_bias", 1), ("l0_low", 1), ("l0_up", 1), ("l0_merge", 17), ("l0_out", 2), ("l0_ffn", 29),
    ("l1_na", 4), ("l1_bias", 1), ("l1_low", 1), ("l1_up", 1), ("l1_merge", 9), ("l1_out", 2), ("l1_ffn", 17),
]
FIRST = {}
_at = 0
for _name, _n in STAGES:
    FIRST[_name] = _at
    _at += _n
STRIPS = _at
SIDE = PAIRS
SIDE_ADA = NMOD // 4


def places(stage, kind):
    return [FIRST[stage] + i for i, x in enumerate(ORDER.get(stage, "E" * dict(STAGES)[stage])) if x == kind]


MODS = [(FIRST["ada0a"] + i, 0, 4 * i) for i in range(4)]
MODS += [(s, 0, 16 + 4 * i) for i, s in enumerate(places("even", "M"))]
MERGE_MOD = len(MODS)
MODS += [(s, 2, 16 + 4 * i) for i, s in enumerate(places("l0_merge", "M"))]
FFN_MOD = len(MODS)
MODS += [(s, 3, 4 * i) for i, s in enumerate(places("l0_ffn", "M"))]

LAYER_STREAMS = (2, 1)
LIN = [
    ("even_q", "DDDD"), ("even_k", "D"), ("even_v", "D"), ("even_u", "AAAA"), ("even_z", "AA"),
    ("even_rope", "DDDDD"), ("even_gate", "DD"), ("even_out", "D" * KD),
    ("turn0", "AAAA"), ("route0", "D"), ("rank0", "D"),
    ("odd_in", "AAD" * KD), ("odd_out", "D" * KD),
    ("turn1", "AAAA"), ("route1", "D"), ("rank1", "D"),
]
for _l, _s in enumerate(LAYER_STREAMS):
    LIN += [(f"f{_l}", "D" * 2 * _s), (f"dft{_l}", "A" * 4 * _s), (f"idft{_l}", "D" * 4 * _s),
            (f"nq{_l}", "DDDD"), (f"nk{_l}", "AAAA"), (f"nv{_l}", "AAAA"),
            (f"low{_l}", "DDDD"), (f"krope{_l}", "D"), (f"mq{_l}", "A" * 8), (f"mk{_l}", "A" * 8),
            (f"mv{_l}", "DDDD"), (f"qrope{_l}", "D" * 8),
            (f"merge{_l}", "ADADAD" * KD), (f"out{_l}", "D" * KD), (f"up{_l}", "AD" * KF), (f"down{_l}", "D" * KD)]
GROUP0, TAKER, TAKEN = {}, [], []
for _name, _who in LIN:
    GROUP0[_name] = len(TAKER)
    for _w in _who:
        TAKER.append(_w)
        TAKEN.append(TAKER.count(_w))
LIN_BANKS = 4

NORMS = ["n1_0", "n2_0", "n1_1", "n2_1", "final", "ln_in",
         "cq0", "ckv0", "ln1_0", "ln2_0", "cq1", "ckv1", "ln1_1", "ln2_1"]
NCHUNK = {n: 2 if n[:2] == "cq" else 1 if n[:3] == "ckv" else KD for n in NORMS}
NBASE, NMEAN, NSTAT, NOUT, NMID, NXC = {}, {}, {}, {}, {}, {}
_b = _m = _o = _d = _x = 0
for _i, _n in enumerate(NORMS):
    NBASE[_n], NSTAT[_n], NMEAN[_n], NOUT[_n], NMID[_n], NXC[_n] = _b, _i, _m, _o, _d, _x
    _b += NCHUNK[_n]
    _d += NCHUNK[_n]
    if _n[:2] == "ln":
        _m += 1
        _x += KD
    if _n[:2] in ("n1", "n2", "ln"):
        _o += KD

ATT, _u = {}, 0
for _n, _q in [("even", 2), ("na0", 4), ("mla0", 4), ("na1", 2), ("mla1", 2)]:
    ATT[_n] = (_q, _u)
    _u += _q * HEADS

def columns(parts):
    at, out = 0, {}
    for name, n in parts:
        out[name] = (at, n)
        at += n
    return out, at


PAR, N_PAR = columns([
    ("c", 2 * KD), ("c_2", 2 * KD), ("bias", 4 * NMOD * 2), ("g1", 2 * KD), ("g2", 2 * KD), ("gf", KD),
    ("sgu", 4), ("conv", 3 * KD), ("lni_g", KD), ("lni_b", KD),
    ("ln1_g", 2 * KD), ("ln1_b", 2 * KD), ("ln2_g", 2 * KD), ("ln2_b", 2 * KD),
    ("gq", 4), ("gkv", 2), ("sink", HEADS), ("rbias", 2 * TB * ROUTES),
    ("ident", P), ("ones", P), ("before", P), ("expert", EXPERTS), ("group", EXPERTS), ("slot", C),
])
TA, N_TA = columns([("cos", T), ("sin", T), ("swap", P), ("mask", TB * T), ("bsp", 4 * P), ("router", 2 * KD * ROUTES)])
TC, N_TC = columns([("dft", TB * 2 * T), ("cd", P), ("sd", P), ("cos", T), ("sin", T), ("swap", P)])


def build_program(nc, stream, par, tab_a, tab_b, wsp_d, xt, ctx2t, out):
    with ExitStack() as ctx:
        def sb(name, shape, dt=F32):
            return ctx.enter_context(nc.sbuf_tensor(name, shape, dt))

        def sem(name):
            return ctx.enter_context(nc.semaphore(name))

        ring = sb("ring", [P, RING, STRIP])
        X = sb("X", [P, KD, 2 * T])
        A = sb("A", [P, KD, 2 * T])
        par_sb = sb("par_sb", [P, N_PAR])
        tab_sb = sb("tab_sb", [P, max(N_TA, N_TC)])
        MOD = sb("MOD", [P, 4, NMOD, 2])
        MODP = sb("MODP", [P, 2, NMOD, 2])
        GSC = sb("GSC", [P, 5, KD])
        SIDEC = sb("SIDEC", [P, PAIRS * 2 * KD])
        SILC = sb("SILC", [P, 2, KD, 2])
        EPS = sb("EPS", [P, 2])
        MX = sb("MX", [P, 2, HEADS])
        NM = sb("NM", [P, 2, HEADS])
        SM = sb("SM", [P, 2, HEADS])
        ES = sb("ES", [P, 2, HEADS])
        BN = sb("BN", [P, TB, 10])
        FLAG = sb("FLAG", [P, 2], I32)
        work = sb("work", [P, 15360])
        bank = [ctx.enter_context(nc.psum_tensor(f"bank{i}", [P, 512], F32)) for i in range(8)]

        def par_(name, a=0, n=None):
            o, full = PAR[name]
            return par_sb[:, o + a:o + (full if n is None else a + n)]

        def tab(where, name, a=0, n=None):
            o, full = where[name]
            return tab_sb[:, o + a:o + (full if n is None else a + n)]

        def wk(at, *shape):
            n = int(np.prod(shape))
            v = work[:, at:at + n]
            if len(shape) == 2:
                v = v.rearrange("p (a b) -> p a b", b=shape[1])
            if len(shape) == 3:
                v = v.rearrange("p (a b c) -> p a b c", b=shape[1], c=shape[2])
            return v

        ident, ones, before = par_("ident"), par_("ones"), par_("before")

        SQ, MEAN, RSTD = wk(13312, 2, 512), wk(14336, 512), wk(14848, 512)
        QRAW, QK, KV_K = wk(0, 5, T), wk(1280, 5, T), wk(2560, 2 * T)
        V1, U1, Z1 = wk(3072, 4, P), wk(3584, 4, T), wk(4608, TB, 512)
        PR1, PT1, YT1 = wk(5632, 3, 512), wk(7168, 2, 512), wk(8192, 512)
        CAT, WSP, TMP1 = wk(8704, KD, T), wk(10752, HEADS, P), wk(11776, 2, T)
        HT, XG = wk(0, TB, D), wk(2048, KD, P)
        SIL, HTOK, HE = wk(3072, HID), wk(3584, HID), wk(10752, 4, P)
        YP, GE, GW, SPT = wk(4096, D), wk(5120, TB, P), wk(5376, TB, P), wk(5632, T)
        RK, MM, GG = wk(5888, TB, 34), wk(5956, TB, 34), wk(6024, TB, 34)
        LG, GL8, MX8, V8 = wk(6100, TB, ROUTES), wk(6172, TB, 8), wk(6188, TB, 8), wk(6204, TB, 8)
        IX8, IE8 = wk(6220, TB, 8).bitcast(U32), wk(6236, TB, 8).bitcast(U32)
        IXF, IEF = wk(6252, TB, 8), wk(6268, TB, 8)
        SML = wk(6284, TB, 16)
        GM, ME, O0, O1 = wk(6316, TB, 32), wk(6380, TB, 32), wk(6444, TB, 32), wk(6508, TB, 32)
        MS, CMAX, OPEN = wk(6572, 32), wk(6604, 1), wk(6606, 1)
        BG, CG, YC = wk(0, 2, T), wk(512, 2, T), wk(1024, 2, T + 2)
        CV, CT = wk(1600, KD, T), wk(3648, 2, T)
        FT, FU = wk(0, 4, 512), wk(2048, 8, 512)
        NQ, NK, V2 = wk(0, 4, 512), wk(2048, 4, 512), wk(4096, 4, 512)
        MK = wk(0, KD, 512)
        YB = [wk(6144 + 2048 * b, 4, 512) for b in range(3)]
        LOW = YB[2]
        PR2, YT2, PT2 = wk(12288, 3, 512), wk(13824, 512), wk(14336, 2, 512)
        MG, SG = wk(0, KD, 512), wk(4096, 2, 512)
        HB, SB_, RB = wk(0, KF, 512), wk(11264, 2, 512), wk(12288, 2, 512)
        RT = wk(12288, 2, 512)
        QT = wk(12288, 2, T)

        MACC1, MACC2 = wk(8704, 4, 512), wk(13312, 4, 512)
        STAGE = wk(6656, KD, 512)
        SACC = [X[:, 2 * s:2 * s + 2, T:2 * T] for s in range(2)]

        def macc(n, s):
            return (MACC1 if n < MERGE_MOD else MACC2)[:, 2 * (n % 2) + s, :]

        par_in, x_in, taba_in, tabb_in, wsp_in = (sem(n) for n in ("par_in", "x_in", "taba_in", "tabb_in", "wsp_in"))
        ctx2_in, out_sent = sem("ctx2_in"), sem("out_sent")
        strip_in = [sem(f"strip_in{i}") for i in range(RING)]
        strip_used = sem("strip_used")
        silc_ready, eps_ready = sem("silc_ready"), sem("eps_ready")
        lin_ready = sem("lin_ready")
        taken = {"D": sem("taken_by_vector"), "A": sem("taken_by_scalar")}
        sum_ready, xc_ready, sq_ready, sq_used = (sem(n) for n in ("sum_ready", "xc_ready", "sq_ready", "sq_used"))
        std_ready, mid_ready, norm_out = (sem(n) for n in ("std_ready", "mid_ready", "norm_out"))
        mod_taken = sem("mod_taken")
        mod_step, mod_summed, mod_done = sem("mod_step"), sem("mod_summed"), sem("mod_done")
        side_in = sem("side_in")
        side_step, side_summed = sem("side_step"), sem("side_summed")
        at_s, at_nm, at_p, at_t, at_ptc = (sem(n) for n in ("at_s", "at_nm", "at_p", "at_t", "at_ptc"))
        at_pv, at_ytm, at_yt, at_y, at_es, at_d = (sem(n) for n in ("at_pv", "at_ytm", "at_yt", "at_y", "at_es", "at_d"))
        z_var, z_std, z_norm, sg_ready = (sem(n) for n in ("z_var", "z_std", "z_norm", "sg_ready"))
        rt_exp_in, rt_exp, rt_mask, flag_ready = (sem(n) for n in ("rt_exp_in", "rt_exp", "rt_mask", "flag_ready"))
        cv_ready, a_ready, kr_copied, low_out, rope_done = (sem(n) for n in ("cv_ready", "a_ready", "kr_copied", "low_out", "rope_done"))
        tmp_ready = sem("tmp_ready")
        dve_own, act_own = sem("dve_own"), sem("act_own")

        NAMES = ["xg_ready", "ge_ready", "gw_ready", "gath_ready", "gate_ready", "up_ready", "sil_ready", "hid_ready",
                 "htr_ready", "he_ready", "y_ready", "y_copied", "comb_ready", "res_added", "tr_ready", "spt_ready"]
        main = {n: sem("m_" + n) for n in NAMES}
        over = [{n: sem(f"o{l}_{n}") for n in NAMES} for l in range(2)]
        over_in = [[sem(f"o{l}_in{i}") for i in range(RING)] for l in range(2)]
        over_used = [sem(f"o{l}_used") for l in range(2)]

        def last_taken(eng, stage):
            end = GROUP0[stage] + len(dict(LIN)[stage]) - 1
            for w in "DA":
                n = TAKER[:end + 1].count(w)
                if n:
                    eng.wait_ge(taken[w], n)

        def wait_taken(eng, stage, j):
            g = GROUP0[stage] + j
            eng.wait_ge(taken[TAKER[g]], TAKEN[g])

        def streams(l):
            return LAYER_STREAMS[l] * T

        block = ctx.enter_context(nc.Block())

        @block.sync
        def _(sp):
            def strips(a, b):
                while a < b and a < RING:
                    sp.dma_start(ring[:, a % RING, :], stream[a]).then_inc(strip_in[a % RING], 16)
                    a += 1
                turns = (b - a) // RING
                if turns:
                    with sp.Fori(0, turns) as i:
                        for j in range(RING):
                            sp.wait_ge(strip_used, i * RING + (a + j - RING + 1))
                            sp.dma_start(ring[:, (a + j) % RING, :], stream[i * RING + (a + j)])\
                              .then_inc(strip_in[(a + j) % RING], 16)
                for s in range(a + turns * RING, b):
                    sp.wait_ge(strip_used, s - RING + 1)
                    sp.dma_start(ring[:, s % RING, :], stream[s]).then_inc(strip_in[s % RING], 16)

            def overflow(l):
                first = FIRST[f"moe{l}"]
                sp.wait_ge(flag_ready, l + 1)
                full = sp.value_load(FLAG[0:1, l:l + 1], min_val=0, max_val=1)
                with sp.If(full > 0):
                    sp.wait_ge(strip_used, first + 3 * EXPERTS)
                    for j in range(RING):
                        sp.dma_start(ring[:, (first + j) % RING, :], stream[first + j])\
                          .then_inc(over_in[l][j], 16)
                    n = 3 * EXPERTS // RING
                    with sp.Fori(1, n * (PASSES - 1)) as i:
                        for j in range(RING):
                            sp.wait_ge(over_used[l], i * RING + (j - RING + 1))
                            sp.dma_start(ring[:, (first + j) % RING, :], stream[(i % n) * RING + (first + j)])\
                              .then_inc(over_in[l][j], 16)
                    sp.wait_ge(over_used[l], 3 * EXPERTS * (PASSES - 1))

            strips(0, FIRST["moe0"])
            first = FIRST["moe0"]
            for j in range(RING):
                sp.wait_ge(strip_used, first + j - RING + 1)
                sp.dma_start(ring[:, (first + j) % RING, :], stream[first + j]).then_inc(strip_in[(first + j) % RING], 16)
            last_taken(sp, "even_out")
            sp.dma_start(STAGE.rearrange("p a b -> p (a b)"), stream[STRIPS]).then_inc(side_in, 16)
            with sp.Fori(1, PAIRS) as i:
                for j in range(RING):
                    sp.wait_ge(strip_used, i * RING + (first + j - RING + 1))
                    sp.dma_start(ring[:, (first + j) % RING, :], stream[i * RING + (first + j)])\
                      .then_inc(strip_in[(first + j) % RING], 16)
                    if j == 1:
                        sp.wait_ge(side_summed, i)
                        sp.dma_start(STAGE.rearrange("p a b -> p (a b)"), stream[i + STRIPS]).then_inc(side_in, 16)
            overflow(0)
            strips(FIRST["odd"], FIRST["l0_na"])
            overflow(1)
            strips(FIRST["l0_na"], STRIPS)
            sp.wait_ge(norm_out, NOUT["ln2_1"] + KD)
            sp.dma_start(out, X[:, :, 0:T]).then_inc(out_sent, 16)
            sp.wait_ge(out_sent, 16)

        @block.tensor
        def _(pe):
            have = {}
            owed = [0]

            def strip(s):
                if s not in have:
                    pe.wait_ge(strip_in[s % RING], 16 * (s // RING + 1))
                    have[s] = ring[:, s % RING, :]
                return have[s]

            def tile(stage, n, width=1):
                v = strip(places(stage, "E")[n // TILES])
                at = n % TILES
                return v[:, at * P:(at + width) * P]

            def mm(o, w, x, start, stop, tells=False):
                m = pe.matmul(o, w, x, start=start, stop=stop)
                if owed[0] and not tells:
                    m.then_inc(strip_used, 1)
                    owed[0] -= 1
                return m

            def group(g):
                if g >= LIN_BANKS:
                    pe.wait_ge(taken[TAKER[g - LIN_BANKS]], TAKEN[g - LIN_BANKS])
                return bank[g % LIN_BANKS]

            def linear(stage, j, n, lhs, rhs, K, at=0, rows=P):
                b = group(GROUP0[stage] + j)
                for k in range(K):
                    m = mm(b[0:rows, at:at + n], lhs(k), rhs(k), k == 0, k == K - 1, tells=k == K - 1)
                m.then_inc(lin_ready, 1)

            def used():
                owed[0] += 1

            def reduce_mod(n):
                _, which, first = MODS[n]
                pe.wait_ge(mod_summed, n + 1)
                used()
                for j in range(4):
                    col = (which * NMOD + first + j) * 2
                    for s in range(2):
                        m = mm(bank[7][:, col + s:col + s + 1], macc(n, s)[:, j * P:(j + 1) * P], ones[:, 0:1],
                               True, True, tells=j == 3 and s == 1)
                m.then_inc(mod_done, 1)

            def norm(name, w, x, mean=False):
                K, base = NCHUNK[name], NBASE[name]
                if mean:
                    for k in range(K):
                        m = mm(bank[6][:, 0:w], ones, x(k), k == 0, k == K - 1, tells=k == K - 1)
                    m.then_inc(sum_ready, 1)
                for k in range(K):
                    pe.wait_ge(sq_ready, base + k + 1)
                    pe.matmul(bank[6][:, 0:w], ones, SQ[:, (base + k) % 2, 0:w], start=(k == 0), stop=(k == K - 1))\
                      .then_inc(sq_used, 1)

            def attention(name, q, k, v, PR, PT, YT, bias=None):
                nb, u0 = ATT[name]
                b0 = u0 // HEADS
                for t in range(nb * HEADS + 5):
                    if t < nb * HEADS:
                        g, b, h = u0 + t, t // HEADS, t % HEADS
                        lo = 0 if b < TB else T
                        if g >= 3:
                            pe.wait_ge(at_p, g - 2)
                        s = bank[g % 3][:, 0:2 * T - lo]
                        masked = bias is not None and b < TB
                        m = mm(s, q(h, b), k(h, lo), True, not masked, tells=not masked)
                        if masked:
                            m = pe.matmul(s[:, 0:T], ident, bias(h, b), start=False, stop=True)
                        m.then_inc(at_s, 1)
                    if 0 <= t - 2 < nb * HEADS:
                        g, b = u0 + t - 2, (t - 2) // HEADS
                        kb = 4 if b < TB else 2
                        pe.wait_ge(at_p, g + 1)
                        if g >= 2:
                            pe.wait_ge(at_ptc, g - 1)
                        for j in range(kb):
                            m = pe.transpose(bank[3 + g % 2][:, j * P:(j + 1) * P],
                                             PR[:, g % 3, j * P:(j + 1) * P], ident)
                        m.then_inc(at_t, 1)
                    if 0 <= t - 3 < nb * HEADS:
                        g, b, h = u0 + t - 3, (t - 3) // HEADS, (t - 3) % HEADS
                        kb, off = (4, 0) if b < TB else (2, 2)
                        pe.wait_ge(at_ptc, g + 1)
                        if h == 0 and b0 + b:
                            pe.wait_ge(at_ytm, b0 + b)
                        for j in range(kb):
                            m = mm(bank[5][:, h * 64:(h + 1) * 64], PT[:, g % 2, j * P:(j + 1) * P],
                                   v(off + j, h), j == 0, j == kb - 1, tells=j == kb - 1)
                        m.then_inc(at_pv, 1)
                    if t >= 4 and (t - 4) % HEADS == HEADS - 1:
                        b = b0 + (t - 4) // HEADS
                        pe.wait_ge(at_ytm, b + 1)
                        if b:
                            pe.wait_ge(at_y, b)
                        for c in range(4):
                            m = pe.transpose(bank[6][:, c * P:(c + 1) * P], YT[:, c * P:(c + 1) * P], ident)
                        m.then_inc(at_yt, 1)

            pe.wait_ge(par_in, 16)
            pe.wait_ge(x_in, 16)
            norm("n1_0", 2 * T, None)
            for n in range(4):
                reduce_mod(n)

            pe.wait_ge(norm_out, NOUT["n1_0"] + KD)
            for j in range(4):
                linear("even_q", j, T, lambda k: tile("even", j * KD + k), lambda k: A[:, k, 0:T], KD)
            used()
            reduce_mod(4)
            reduce_mod(5)
            linear("even_k", 0, 2 * T, lambda k: tile("even", 32 + k), lambda k: A[:, k, :], KD)
            b = group(GROUP0["even_v"])
            for blk in range(4):
                for k in range(KD):
                    m = mm(b[:, blk * P:(blk + 1) * P], A[:, k, blk * P:(blk + 1) * P], tile("even", 40 + k),
                           k == 0, k == KD - 1, tells=blk == 3 and k == KD - 1)
            m.then_inc(lin_ready, 1)
            for j in range(4):
                linear("even_u", j, T, lambda k: tile("even", 48 + j * KD + k), lambda k: A[:, k, 0:T], KD)
                if j == 1:
                    used()
                    reduce_mod(6)
                    reduce_mod(7)
            for blk in range(TB):
                linear("even_z", blk, 512, lambda k: A[:, k, blk * P:(blk + 1) * P],
                       lambda k: tile("even", 80 + 4 * k, 4), KD)
            used()
            reduce_mod(8)
            reduce_mod(9)
            used()
            reduce_mod(10)
            reduce_mod(11)
            pe.wait_ge(taba_in, 16)
            for j in range(5):
                wait_taken(pe, "even_k" if j == 4 else "even_q", 0 if j == 4 else j)
                linear("even_rope", j, T, lambda k: tab(TA, "swap"), lambda k: QRAW[:, j, :], 1)
            pe.wait_ge(wsp_in, 16)
            for n in range(TB):
                pe.wait_ge(z_norm, n + 1)
                b = group(GROUP0["even_gate"] + n)
                for h in range(HEADS):
                    r = 64 * (h % 2)
                    m = mm(b[r:r + 64, (h // 2) * P:(h // 2 + 1) * P], Z1[:, n, h * 64:(h + 1) * 64], WSP[:, h, :],
                           True, True, tells=h == HEADS - 1)
                m.then_inc(lin_ready, 1)
            last_taken(pe, "even_gate")
            pe.wait_ge(rope_done, 5)

            attention("even",
                      lambda h, b: QK[64 * (h // 4):64 * (h // 4) + 64, h % 4, b * P:(b + 1) * P],
                      lambda h, lo: KV_K[64 * (h // 4):64 * (h // 4) + 64, lo:2 * T],
                      lambda kb, h: V1[:, kb, 64 * (h // 4):64 * (h // 4) + 64],
                      PR1, PT1, YT1, bias=lambda h, b: tab(TA, "mask", b * T, T))
            pe.wait_ge(at_y, 2)
            pe.wait_ge(sg_ready, TB * 4)
            for j in range(KD):
                linear("even_out", j, T, lambda k: tile("even_out", j * KD + k), lambda k: CAT[:, k, :], KD)
                if j % 4 == 3:
                    used()
            def gather(q):
                for c in range(KD):
                    b = bank[2 + c // 4]
                    for blk in range(TB):
                        m = mm(b[:, (c % 4) * P:(c % 4 + 1) * P], HT[:, blk, c * P:(c + 1) * P], GE[:, blk, :],
                               blk == 0, blk == TB - 1, tells=c == KD - 1 and blk == TB - 1)
                m.then_inc(q["gath_ready"], 1)

            def combine(q, p, i, product):
                pe.wait_ge(q["y_copied"], i + (17 * p + 1))
                pe.wait_ge(q["spt_ready"], i + (17 * p + 1))
                for r in range(4):
                    pe.wait_ge(q["res_added"], i * 4 + (70 * p + r + 1))
                    for h in range(2):
                        c = 2 * r + h
                        m = product(bank[6 + r % 2][:, h * T:(h + 1) * T], YP[:, c * P:(c + 1) * P], SPT[:, :],
                                    True, True, tells=h == 1)
                    m.then_inc(q["comb_ready"], 1)

            def moe_pass(q, p, first, came, used_sem, side=False):
                pe.wait_ge(q["ge_ready"], 17 * p + 1)
                gather(q)
                with pe.Fori(0, PAIRS) as i:
                    slot = [ring[:, (first + j) % RING, :] for j in range(RING)]
                    due = [0]

                    def pe_mm(o, w, x, start, stop, tells):
                        m = pe.matmul(o, w, x, start=start, stop=stop)
                        if due[0] and not tells:
                            m.then_inc(used_sem, 1)
                            due[0] -= 1
                        return m

                    def both_up(half, ready):
                        for e in range(2):
                            came(i, 2 * half + e)
                        for k in range(KD):
                            for e in range(2):
                                m = pe_mm(bank[half][e * C:(e + 1) * C, :], XG[:, k, e * C:(e + 1) * C],
                                          slot[2 * half + e][:, k * HID:(k + 1) * HID], k == 0, k == KD - 1,
                                          tells=k == KD - 1 and e == 1)
                        m.then_inc(q[ready], 1)
                        due[0] += 2

                    pe.wait_ge(q["xg_ready"], i + (17 * p + 1))
                    both_up(0, "gate_ready")
                    both_up(1, "up_ready")
                    combine(q, p, i, pe_mm)
                    pe.wait_ge(q["hid_ready"], i + (16 * p + 1))
                    for c in range(4):
                        m = pe.transpose(bank[0][:, c * P:(c + 1) * P], HTOK[:, c * P:(c + 1) * P], ident)
                    m.then_inc(q["htr_ready"], 1)
                    pe.wait_ge(q["ge_ready"], i + (17 * p + 2))
                    gather(q)
                    for e in range(2):
                        came(i, 4 + e)
                    pe.wait_ge(q["he_ready"], i + (16 * p + 1))
                    for h in range(2):
                        for k in range(4):
                            for e in range(2):
                                m = pe_mm(bank[4 + h][e * C:(e + 1) * C, :], HE[:, k, e * C:(e + 1) * C],
                                          slot[4 + e][:, k * D + h * 512:k * D + (h + 1) * 512], k == 0, k == 3,
                                          tells=h == 1 and k == 3 and e == 1)
                    m.then_inc(q["y_ready"], 1)
                    pe.wait_ge(q["gw_ready"], i + (17 * p + 1))
                    pe.wait_ge(q["res_added"], i * 4 + (70 * p + 6))
                    if side:
                        pe.wait_ge(side_summed, i + 1)
                        for j in range(4):
                            for s in range(2):
                                m = pe.matmul(bank[6][:, T + 2 * j + s:T + 2 * j + s + 1],
                                              SACC[s][:, j // 2, (j % 2) * P:(j % 2 + 1) * P], ones[:, 0:1],
                                              start=True, stop=True)
                        m.then_inc(used_sem, 1)
                    else:
                        pe.transpose(bank[6][:, T:T + P], GW[:, 0, :], ident).then_inc(used_sem, 1)
                    pe.transpose(bank[6][:, 0:P], GW[:, 0, :], ident).then_inc(used_sem, 1)
                    pe.transpose(bank[6][:, P:2 * P], GW[:, 1, :], ident).then_inc(q["tr_ready"], 1)
                combine(q, p, PAIRS, lambda o, w, x, a, b, tells: pe.matmul(o, w, x, start=a, stop=b))

            def moe(l):
                for j in range(4):
                    b = group(GROUP0[f"turn{l}"] + j)
                    for c in range(4):
                        cc = (j % 2) * 4 + c
                        m = pe.transpose(b[:, c * P:(c + 1) * P], A[:, cc, (j // 2) * P:(j // 2 + 1) * P], ident)
                        if owed[0] and c < 3:
                            m.then_inc(strip_used, 1)
                            owed[0] -= 1
                    m.then_inc(lin_ready, 1)
                b = group(GROUP0[f"route{l}"])
                for blk in range(TB):
                    for k in range(KD):
                        m = mm(b[:, blk * ROUTES:(blk + 1) * ROUTES], A[:, k, blk * P:(blk + 1) * P],
                               tab(TA, "router", (l * KD + k) * ROUTES, ROUTES), k == 0, k == KD - 1, tells=blk == 1 and k == KD - 1)
                m.then_inc(lin_ready, 1)
                b = group(GROUP0[f"rank{l}"])
                pe.wait_ge(rt_mask, l + 1)
                mm(b[:, 0:32], before, MM[:, 0, 0:32], True, True)
                mm(b[:, 32:64], ones, MM[:, 0, 0:32], True, False)
                mm(b[:, 32:64], before, MM[:, 1, 0:32], False, True)
                mm(b[:, 64:96], ones, MM[:, 0, 0:32], True, False)
                mm(b[:, 64:96], ones, MM[:, 1, 0:32], False, True, tells=True).then_inc(lin_ready, 1)
                last_taken(pe, f"rank{l}")
                assert not owed[0]
                first = FIRST[f"moe{l}"]

                def came(i, j):
                    s = first + j
                    pe.wait_ge(strip_in[s % RING], i * 16 + 16 * (s // RING + 1))

                moe_pass(main, l, first, came, strip_used, side=l == 0)
                full = pe.value_load(FLAG[0:1, l:l + 1], min_val=0, max_val=1)
                with pe.If(full > 0):
                    with pe.Fori(0, PASSES - 1) as p:
                        moe_pass(over[l], p, first,
                                 lambda i, j: pe.wait_ge(over_in[l][j], p * (16 * PAIRS) + i * 16 + 16), over_used[l])
                    pe.wait_ge(over[l]["res_added"], 70 * (PASSES - 1))
                pe.wait_ge(main["res_added"], 70 * (l + 1))

            norm("n2_0", T, None)
            pe.wait_ge(norm_out, NOUT["n2_0"] + KD)
            pe.wait_ge(mod_taken, 2)
            moe(0)

            norm("n1_1", T, None)
            pe.wait_ge(norm_out, NOUT["n1_1"] + KD)

            for j in range(3 * KD):
                linear("odd_in", j, T, lambda k: tile("odd", j * KD + k), lambda k: A[:, k, 0:T], KD)
                if j % 4 == 3:
                    used()
            pe.wait_ge(cv_ready, KD)
            for j in range(KD):
                linear("odd_out", j, T, lambda k: tile("odd", 192 + j * KD + k), lambda k: CV[:, k, :], KD)
                if j % 4 == 3:
                    used()
            norm("n2_1", T, None)
            pe.wait_ge(norm_out, NOUT["n2_1"] + KD)
            moe(1)
            norm("final", T, None)

            pe.wait_ge(ctx2_in, 16)
            pe.wait_ge(tabb_in, 16)
            pe.wait_ge(mid_ready, NMID["final"] + KD)
            norm("ln_in", 2 * T, lambda k: X[:, k, :], mean=True)
            for l in range(2):
                w = streams(l)
                pe.wait_ge(a_ready, KD * (1 + 3 * l))
                st = f"l{l}_na"
                for blk in range(w // P):
                    linear(f"f{l}", blk, 512, lambda k: A[:, k, blk * P:(blk + 1) * P], lambda k: tile(st, 4 * k, 4), KD)
                used()
                for s in range(w // T):
                    for g in range(4):
                        for blk in range(TB):
                            wait_taken(pe, f"f{l}", s * TB + blk)
                        linear(f"dft{l}", s * 4 + g, 2 * T, lambda k: FT[:, s * TB + k, g * P:(g + 1) * P],
                               lambda k: tab(TC, "dft", k * 2 * T, 2 * T), TB)
                for j in range(4 * w // T):
                    wait_taken(pe, f"dft{l}", j)
                    linear(f"idft{l}", j, T, lambda k: tab(TC, "cd" if k == 0 else "sd"),
                           lambda k: FU[:, j, k * T:(k + 1) * T], 2)
                last_taken(pe, f"idft{l}")
                for j in range(4):
                    linear(f"nq{l}", j, w, lambda k: tile(st, 32 + j * KD + k), lambda k: A[:, k, 0:w], KD)
                used()
                for j in range(4):
                    linear(f"nk{l}", j, 2 * T, lambda k: tile(st, 64 + j * KD + k), lambda k: A[:, k, :], KD)
                used()
                for blk in range(4):
                    linear(f"nv{l}", blk, 512, lambda k: A[:, k, blk * P:(blk + 1) * P],
                           lambda k: tile(st, 96 + 4 * k, 4), KD)
                used()
                last_taken(pe, f"nv{l}")
                bs = strip(FIRST[f"l{l}_bias"])
                attention(f"na{l}",
                          lambda h, b: NQ[64 * (h % 2):64 * (h % 2) + 64, h // 2, b * P:(b + 1) * P],
                          lambda h, lo: NK[64 * (h % 2):64 * (h % 2) + 64, h // 2, lo:2 * T],
                          lambda kb, h: V2[:, kb, h * 64:(h + 1) * 64], PR2, PT2, YT2,
                          bias=lambda h, b: bs[:, (h * TB + b) * T:(h * TB + b + 1) * T])
                used()
                st = f"l{l}_low"
                for j in range(4):
                    n = w if j < 2 else 2 * T
                    linear(f"low{l}", j, n, lambda k: tile(st, j * KD + k), lambda k: A[:, k, 0:n], KD)
                used()
                pe.wait_ge(at_y, (ATT[f"na{l}"][1] // HEADS) + ATT[f"na{l}"][0])
                norm(f"cq{l}", w, None)
                norm(f"ckv{l}", 2 * T, None)
                wait_taken(pe, f"low{l}", 3)
                linear(f"krope{l}", 0, T, lambda k: tab(TC, "swap"), lambda k: LOW[:, 3, 0:T], 1)
                pe.wait_ge(mid_ready, NMID[f"ckv{l}"] + 1)
                st = f"l{l}_up"
                for j in range(8):
                    linear(f"mq{l}", j, w, lambda k: tile(st, 2 * j + k), lambda k: LOW[:, k, 0:w], 2)
                for j in range(8):
                    linear(f"mk{l}", j, 2 * T, lambda k: tile(st, 16 + j), lambda k: LOW[:, 2, :], 1)
                for blk in range(4):
                    linear(f"mv{l}", blk, 512, lambda k: LOW[:, 2, blk * P:(blk + 1) * P], lambda k: tile(st, 24, 4), 1)
                used()
                for j in range(8):
                    wait_taken(pe, f"mq{l}", j)
                    linear(f"qrope{l}", j, T, lambda k: tab(TC, "swap"), lambda k: A[:, j, 0:T], 1)
                last_taken(pe, f"qrope{l}")
                pe.wait_ge(rope_done, 5 + 9 * (l + 1))
                pe.wait_ge(kr_copied, 8 * (l + 1))
                attention(f"mla{l}",
                          lambda h, b: A[0:MLA_ROWS, h, b * P:(b + 1) * P],
                          lambda h, lo: MK[0:MLA_ROWS, h, lo:2 * T],
                          lambda kb, h: V2[:, kb, h * 64:(h + 1) * 64], PR2, PT2, YT2)
                pe.wait_ge(at_y, (ATT[f"mla{l}"][1] // HEADS) + ATT[f"mla{l}"][0])
                pe.wait_ge(a_ready, KD * (2 + 3 * l))
                st = f"l{l}_merge"
                for o in range(KD):
                    for b in range(3):
                        at = (o * 3 + b) * 12
                        j = (o * 3 + b) * 2
                        linear(f"merge{l}", j, w, lambda k: tile(st, at + k), lambda k: A[:, k, 0:w], KD)
                        linear(f"merge{l}", j + 1, w, lambda k: tile(st, at + KD + k), lambda k: YB[b][:, k, 0:w], 4)
                        if (at + 12) // TILES > at // TILES:
                            used()
                            if l == 0 and at // TILES < 8:
                                reduce_mod(MERGE_MOD + at // TILES)
                wait_taken(pe, f"merge{l}", 6 * KD - 1)
                for j in range(KD):
                    linear(f"out{l}", j, w, lambda k: tile(f"l{l}_out", j * KD + k), lambda k: MG[:, k, 0:w], KD)
                    if j % 4 == 3:
                        used()
                wait_taken(pe, f"out{l}", KD - 1)
                norm(f"ln1_{l}", w, lambda k: X[:, k, 0:w], mean=True)
                pe.wait_ge(a_ready, KD * (3 + 3 * l))
                st = f"l{l}_ffn"
                for j in range(2 * KF):
                    linear(f"up{l}", j, w, lambda k: tile(st, j * KD + k), lambda k: A[:, k, 0:w], KD)
                    if j % 4 == 3:
                        used()
                        if l == 0:
                            reduce_mod(FFN_MOD + j // 4)
                wait_taken(pe, f"up{l}", 2 * KF - 1)
                for j in range(KD):
                    at = 2 * KF * KD + j * KF
                    linear(f"down{l}", j, w, lambda k: tile(st, at + k), lambda k: HB[:, k, 0:w], KF)
                    if (at + KF) // TILES > at // TILES:
                        used()
                        if l == 0 and j == 1:
                            reduce_mod(FFN_MOD + 11)
                used()
                wait_taken(pe, f"down{l}", KD - 1)
                norm(f"ln2_{l}", w, lambda k: X[:, k, 0:w], mean=True)

        @block.scalar
        def _(act):
            act.dma_start(par_sb[:, :], par).then_inc(par_in, 16)
            act.dma_start(X[:, :, :], xt).then_inc(x_in, 16)
            act.dma_start(tab_sb[:, 0:N_TA], tab_a).then_inc(taba_in, 16)
            act.dma_start(WSP, wsp_d).then_inc(wsp_in, 16)

            def take(stage, j, n, rows=P):
                g = GROUP0[stage] + j
                act.wait_ge(lin_ready, g + 1)
                return bank[g % LIN_BANKS][0:rows, 0:n]

            def norm(name, w, x, out_, halves, dim, eps, mean=False):
                K, base = NCHUNK[name], NBASE[name]
                for k in range(K):
                    if mean:
                        act.wait_ge(xc_ready, NXC[name] + k + 1)
                    if base + k >= 2:
                        act.wait_ge(sq_used, base + k - 1)
                    act.activation(SQ[:, (base + k) % 2, 0:w], x(k), ACT.Square).then_inc(sq_ready, 1)
                act.wait_ge(sq_used, base + K)
                act.activation(RSTD[:, 0:w], bank[6][:, 0:w], ACT.Sqrt, bias=EPS[:, eps:eps + 1], scale=1.0 / dim)\
                   .then_inc(std_ready, 1)
                for k in range(K if halves else 0):
                    act.wait_ge(mid_ready, NMID[name] + k + 1)
                    for lo, hi, b in halves:
                        m = act.activation(out_(k)[:, lo:hi], out_(k)[:, lo:hi], ACT.Identity, bias=b(k))
                    m.then_inc(norm_out, 1)

            def attention(name, scale, PR, PT, sink=False):
                nb, u0 = ATT[name]
                for t in range(nb * HEADS + 4):
                    if t < nb * HEADS:
                        g, b, h = u0 + t, t // HEADS, t % HEADS
                        n = 2 * T if b < TB else T
                        pb = (u0 // HEADS + b) % 2
                        act.wait_ge(at_nm, g + 1)
                        if g >= 3:
                            act.wait_ge(at_t, g - 2)
                        act.activation(PR[:, g % 3, 0:n], bank[g % 3][:, 0:n], ACT.Exp, bias=NM[:, pb, h:h + 1],
                                       scale=scale, accum_out=SM[:, pb, h:h + 1]).then_inc(at_p, 1)
                    if 0 <= t - 2 < nb * HEADS:
                        g, b = u0 + t - 2, (t - 2) // HEADS
                        n = 2 * T if b < TB else T
                        act.wait_ge(at_t, g + 1)
                        if g >= 2:
                            act.wait_ge(at_pv, g - 1)
                        act.activation(PT[:, g % 2, 0:n], bank[3 + g % 2][:, 0:n], ACT.Copy).then_inc(at_ptc, 1)
                    if sink and t >= 3 and (t - 3) % HEADS == HEADS - 1:
                        b = (t - 3) // HEADS
                        act.wait_ge(at_d, b + 1)
                        act.activation(ES[:, b % 2, :], ES[:, b % 2, :], ACT.Exp).then_inc(at_es, 1)

            act.wait_ge(par_in, 16)
            for i, name in enumerate(("c", "c_2")):
                m = act.activation(SILC[:, i, :, :].rearrange("p a b -> p (a b)"), par_(name), ACT.Silu)
            m.then_inc(silc_ready, 1)
            act.wait_ge(x_in, 16)
            act.wait_ge(eps_ready, 1)
            mod = lambda which, first, k, s: MOD[:, which, first + k, s:s + 1]
            norm("n1_0", 2 * T, lambda k: X[:, k, :], lambda k: A[:, k, :],
                 [(0, T, lambda k: mod(0, 0, k, 0)), (T, 2 * T, lambda k: mod(0, 0, k, 1))], D, 0)
            for j in range(4):
                act.activation(U1[:, j, :], take("even_u", j, T), ACT.Gelu).then_inc(taken["A"], 1)
            for blk in range(TB):
                act.activation(Z1[:, blk, :], take("even_z", blk, 512), ACT.Gelu).then_inc(taken["A"], 1)
            for n in range(TB):
                act.wait_ge(z_var, n + 1)
                act.activation(BN[:, n, 8:9], BN[:, n, 7:8], ACT.Sqrt, bias=EPS[:, 0:1]).then_inc(z_std, 1)
            attention("even", 1.0, PR1, PT1, sink=True)

            def moe_pass(q, p):
                act.activation(OPEN, ident[:, 0:1], ACT.Copy).then_inc(q["y_copied"], 1)

                def rows(i):
                    act.wait_ge(q["gath_ready"], i + (17 * p + 1))
                    for h in range(2):
                        m = act.activation(XG[:, 4 * h:4 * h + 4, :].rearrange("p a b -> p (a b)"), bank[2 + h][:, :],
                                           ACT.Copy)
                    m.then_inc(q["xg_ready"], 1)

                rows(0)
                with act.Fori(0, PAIRS) as i:
                    act.wait_ge(q["gate_ready"], i + (16 * p + 1))
                    act.activation(SIL[:, :], bank[0][:, :], ACT.Silu).then_inc(q["sil_ready"], 1)
                    act.wait_ge(q["htr_ready"], i + (16 * p + 1))
                    act.activation(HE.rearrange("p a b -> p (a b)"), bank[0][:, :], ACT.Copy).then_inc(q["he_ready"], 1)
                    rows(i + 1)
                    act.wait_ge(q["y_ready"], i + (16 * p + 1))
                    for h in range(2):
                        m = act.activation(YP[:, h * 512:(h + 1) * 512], bank[4 + h][:, :], ACT.Copy)
                    m.then_inc(q["y_copied"], 1)

            def moe(l):
                for j in range(4):
                    act.activation(HT[:, j // 2, (j % 2) * 512:(j % 2) * 512 + 512], take(f"turn{l}", j, 512), ACT.Copy)\
                       .then_inc(taken["A"], 1)
                act.wait_ge(rt_exp_in, l + 1)
                for b in range(TB):
                    act.activation(SML[:, b, 8:12], LG[:, b, 0:4], ACT.Exp, bias=SML[:, b, 0:1], accum_out=SML[:, b, 1:2])
                    m = act.activation(SML[:, b, 3:4], SML[:, b, 2:3], ACT.Exp)
                m.then_inc(rt_exp, 1)
                if l == 1:
                    act.wait_ge(lin_ready, GROUP0["route1"] + 1)
                    act.wait_ge(flag_ready, 2)
                    act.dma_start(tab_sb[:, 0:N_TC], tab_b).then_inc(tabb_in, 16)
                    act.dma_start(X[:, :, T:2 * T], ctx2t).then_inc(ctx2_in, 16)
                moe_pass(main, l)
                act.wait_ge(flag_ready, l + 1)
                full = act.value_load(FLAG[0:1, l:l + 1], min_val=0, max_val=1)
                with act.If(full > 0):
                    with act.Fori(0, PASSES - 1) as p:
                        moe_pass(over[l], p)
                    act.wait_ge(over[l]["res_added"], 70 * (PASSES - 1))
                act.wait_ge(main["res_added"], 70 * (l + 1))

            last_taken(act, "even_out")
            norm("n2_0", T, lambda k: X[:, k, 0:T], lambda k: A[:, k, 0:T], [(0, T, lambda k: mod(0, 24, k, 0))], D, 0)
            moe(0)
            norm("n1_1", T, lambda k: X[:, k, 0:T], lambda k: A[:, k, 0:T], [(0, T, lambda k: mod(1, 0, k, 0))], D, 0)
            for c in range(KD):
                if c >= 2:
                    act.wait_ge(cv_ready, c - 1)
                act.activation(BG[:, c % 2, :], take("odd_in", 3 * c, T), ACT.Copy).then_inc(taken["A"], 1)
                act.activation(CG[:, c % 2, :], take("odd_in", 3 * c + 1, T), ACT.Copy).then_inc(taken["A"], 1)
            last_taken(act, "odd_out")
            norm("n2_1", T, lambda k: X[:, k, 0:T], lambda k: A[:, k, 0:T], [(0, T, lambda k: mod(1, 24, k, 0))], D, 0)
            moe(1)
            norm("final", T, lambda k: X[:, k, 0:T], None, None, D, 0)

            act.wait_ge(ctx2_in, 16)
            norm("ln_in", 2 * T, lambda k: X[:, k, :], lambda k: X[:, k, :],
                 [(0, 2 * T, lambda k: par_("lni_b", k, 1))], D, 1, mean=True)
            for l in range(2):
                w = streams(l)
                for j in range(4 * w // T):
                    act.activation(FU[:, j, :], take(f"dft{l}", j, 512), ACT.Copy).then_inc(taken["A"], 1)
                last_taken(act, f"idft{l}")
                for j in range(4):
                    act.activation(NK[:, j, :], take(f"nk{l}", j, 512), ACT.Copy).then_inc(taken["A"], 1)
                for j in range(4):
                    act.activation(V2[:, j, :], take(f"nv{l}", j, 512), ACT.Copy).then_inc(taken["A"], 1)
                attention(f"na{l}", 1.0, PR2, PT2)
                for j in range(2):
                    wait_taken(act, f"low{l}", j)
                norm(f"cq{l}", w, lambda k: LOW[:, k, 0:w], None, None, 2 * P, 1)
                wait_taken(act, f"low{l}", 2)
                act.wait_ge(mid_ready, NMID[f"cq{l}"] + 2)
                norm(f"ckv{l}", 2 * T, lambda k: LOW[:, 2, :], None, None, P, 1)
                for j in range(8):
                    act.activation(A[:, j, 0:w], take(f"mq{l}", j, w), ACT.Copy).then_inc(taken["A"], 1)
                for j in range(8):
                    act.activation(MK[0:64, j, :], take(f"mk{l}", j, 512, 64), ACT.Copy).then_inc(taken["A"], 1)
                attention(f"mla{l}", MLA_SCALE, PR2, PT2)
                act.wait_ge(at_y, (ATT[f"mla{l}"][1] // HEADS) + ATT[f"mla{l}"][0])
                for j in range(3 * KD):
                    if j >= 2:
                        wait_taken(act, f"merge{l}", 2 * (j - 2) + 1)
                    act.activation(SG[:, j % 2, 0:w], take(f"merge{l}", 2 * j, w), ACT.Sigmoid).then_inc(taken["A"], 1)
                norm(f"ln1_{l}", w, lambda k: X[:, k, 0:w], lambda k: X[:, k, 0:w],
                     [(0, w, lambda k: par_("ln1_b", l * KD + k, 1))], D, 1, mean=True)
                for j in range(KF):
                    if j >= 2:
                        wait_taken(act, f"up{l}", 2 * (j - 2) + 1)
                    act.activation(SB_[:, j % 2, 0:w], take(f"up{l}", 2 * j, w), ACT.Silu).then_inc(taken["A"], 1)
                norm(f"ln2_{l}", w, lambda k: X[:, k, 0:w], lambda k: X[:, k, 0:w],
                     [(0, w, lambda k: par_("ln2_b", l * KD + k, 1))], D, 1, mean=True)

        @block.vector
        def _(dve):
            own = [0]

            def link(ins):
                own[0] += 1
                ins.then_inc(dve_own, 1)
                dve.wait_ge(dve_own, own[0])

            def take(stage, j, n=None, rows=None):
                g = GROUP0[stage] + j
                dve.wait_ge(lin_ready, g + 1)
                b = bank[g % LIN_BANKS]
                return b[:, 0:n] if n else b

            def norm(name, w, x, out_, halves, dim, mean=False):
                K = NCHUNK[name]
                src = x
                if mean:
                    dve.wait_ge(sum_ready, NMEAN[name] + 1)
                    link(dve.tensor_scalar(MEAN[:, 0:w], bank[6][:, 0:w], 1.0 / dim, None, ALU.mult))
                    for k in range(K):
                        dve.tensor_tensor(out_(k), x(k), MEAN[:, 0:w], ALU.subtract).then_inc(xc_ready, 1)
                    dve.wait_ge(xc_ready, NXC[name] + K)
                    src = out_
                dve.wait_ge(std_ready, NSTAT[name] + 1)
                link(dve.reciprocal(RSTD[:, 0:w], RSTD[:, 0:w]))
                for k in range(K):
                    for lo, hi, s in halves:
                        m = dve.scalar_tensor_tensor(out_(k)[:, lo:hi], src(k)[:, lo:hi], s(k), RSTD[:, lo:hi],
                                                     ALU.mult, ALU.mult)
                    m.then_inc(mid_ready, 1)

            def attention(name, scale, YT, y, sink=False):
                nb, u0 = ATT[name]
                for t in range(nb * HEADS + 5):
                    if t < nb * HEADS:
                        g, b, h = u0 + t, t // HEADS, t % HEADS
                        n = 2 * T if b < TB else T
                        pb = (u0 // HEADS + b) % 2
                        dve.wait_ge(at_s, g + 1)
                        link(dve.reduce_max(MX[:, pb, h:h + 1], bank[g % 3][:, 0:n], AXX))
                        if sink:
                            i = dve.tensor_scalar(NM[:, pb, h:h + 1], MX[:, pb, h:h + 1], par_("sink", h, 1), -1.0,
                                                  ALU.max, ALU.mult)
                        else:
                            i = dve.tensor_scalar(NM[:, pb, h:h + 1], MX[:, pb, h:h + 1], -scale, None, ALU.mult)
                        i.then_inc(at_nm, 1)
                    if t >= 3 and (t - 3) % HEADS == HEADS - 1:
                        b = u0 // HEADS + (t - 3) // HEADS
                        pb = b % 2
                        if sink:
                            dve.wait_ge(at_nm, 8 * b + 8)
                            dve.tensor_tensor(ES[:, pb, :], par_("sink"), NM[:, pb, :], ALU.add).then_inc(at_d, 1)
                            dve.wait_ge(at_es, b + 1)
                            link(dve.tensor_tensor(SM[:, pb, :], SM[:, pb, :], ES[:, pb, :], ALU.add))
                        dve.wait_ge(at_p, 8 * b + 8)
                        link(dve.reciprocal(SM[:, pb, :], SM[:, pb, :]))
                        dve.wait_ge(at_pv, 8 * b + 8)
                        dve.tensor_tensor(YT.rearrange("p (h d) -> p h d", h=HEADS),
                                          bank[5][:, :].rearrange("p (h d) -> p h d", h=HEADS),
                                          SM[:, pb, :].unsqueeze(2).to_broadcast([P, HEADS, 64]), ALU.mult)\
                           .then_inc(at_ytm, 1)
                    if t >= 4 and (t - 4) % HEADS == HEADS - 1:
                        bb = (t - 4) // HEADS
                        dve.wait_ge(at_yt, u0 // HEADS + bb + 1)
                        dve.tensor_copy(y(bb), bank[6][:, :].rearrange("p (c n) -> p c n", c=4)).then_inc(at_y, 1)

            def products(W, cond, acc, step, base, summed):
                for k in range(KD):
                    for s in range(2):
                        if k:
                            dve.wait_ge(step, base + (2 * k + s - 1))
                            m = dve.scalar_tensor_tensor(acc(s), W(k), cond(k, s), acc(s), ALU.mult, ALU.add)
                        else:
                            m = dve.tensor_scalar(acc(s), W(k), cond(k, s), None, ALU.mult)
                        m.then_inc(summed if k == KD - 1 and s == 1 else step, 1)

            def mod_strip(n):
                st, which, _ = MODS[n]
                dve.wait_ge(strip_in[st % RING], 16 * (st // RING + 1))
                if n >= 2:
                    dve.wait_ge(mod_done, n - 1)
                v = ring[:, st % RING, :]
                products(lambda k: v[:, k * 512:(k + 1) * 512], lambda k, s: SILC[:, which // 2, k, s:s + 1],
                         lambda s: macc(n, s), mod_step, 15 * n, mod_summed)

            def take_mods(which, a, b, done, n):
                dve.wait_ge(mod_done, done)
                at, end = (which * NMOD + a) * 2, (which * NMOD + b) * 2
                flat = MOD[:, :, :, :].rearrange("p a b c -> p (a b c)")
                dve.tensor_tensor(flat[:, at:end], bank[7][:, at:end], par_("bias", at, end - at), ALU.add)\
                   .then_inc(mod_taken, 1)
                dve.wait_ge(mod_taken, n)

            def plus_one(l, a, b):
                link(dve.tensor_scalar(MODP[:, l, a:b, :], MOD[:, 2 + l, a:b, :], 1.0, None, ALU.add))

            def gain(slot, which, first, s, g):
                return dve.scalar_tensor_tensor(GSC[:, slot, :], MOD[:, which, first:first + KD, s], 1.0, g, ALU.add, ALU.mult)

            def residual(stage, j, n, gate):
                dve.scalar_tensor_tensor(X[:, j, 0:n], take(stage, j, n), gate, X[:, j, 0:n], ALU.mult, ALU.add)\
                   .then_inc(taken["D"], 1)

            dve.memset(EPS[:, 0:1], EPS1)
            dve.memset(EPS[:, 1:2], EPS2).then_inc(eps_ready, 1)
            dve.wait_ge(par_in, 16)
            dve.wait_ge(silc_ready, 1)
            for n in range(4):
                mod_strip(n)
            for i in range(PAIRS):
                m = dve.tensor_copy(SIDEC[:, i * 2 * KD:(i + 1) * 2 * KD],
                                    SILC[:, 0 if i < SIDE_ADA else 1, :, :].rearrange("p a b -> p (a b)"))
            link(m)
            dve.wait_ge(x_in, 16)
            take_mods(0, 0, 16, 4, 1)
            gain(0, 0, 8, 0, par_("g1", 0, KD))
            link(gain(1, 0, 8, 1, par_("g1", 0, KD)))
            norm("n1_0", 2 * T, lambda k: X[:, k, :], lambda k: A[:, k, :],
                 [(0, T, lambda k: GSC[:, 0, k:k + 1]), (T, 2 * T, lambda k: GSC[:, 1, k:k + 1])], D)
            for j in range(4):
                dve.tensor_scalar(QRAW[:, j, :], take("even_q", j, T), 0.125, None, ALU.mult).then_inc(taken["D"], 1)
            mod_strip(4)
            mod_strip(5)
            dve.tensor_copy(QRAW[:, 4, :], take("even_k", 0)[:, 0:T])
            dve.tensor_copy(KV_K[:, T:2 * T], take("even_k", 0)[:, T:2 * T]).then_inc(taken["D"], 1)
            dve.tensor_copy(V1.rearrange("p a b -> p (a b)"), take("even_v", 0)[:, :]).then_inc(taken["D"], 1)
            wait_taken(dve, "even_v", 0)
            for n in range(6, 12):
                mod_strip(n)
            take_mods(0, 16, 48, 12, 2)
            dve.wait_ge(taba_in, 16)
            for j in range(5):
                o = QK[:, j, :] if j < 4 else KV_K[:, 0:T]
                dve.tensor_tensor(TMP1[:, j % 2, :], take("even_rope", j, T), tab(TA, "sin"), ALU.mult).then_inc(taken["D"], 1)
                link(dve.tensor_tensor(QK[:, j, :], QRAW[:, j, :], tab(TA, "cos"), ALU.mult))
                dve.tensor_tensor(o, QK[:, j, :], TMP1[:, j % 2, :], ALU.add).then_inc(rope_done, 1)
            for n in range(TB):
                wait_taken(dve, "even_z", n)
                link(dve.bn_stats(BN[:, n, 0:6], Z1[:, n, :]))
                dve.bn_aggr(BN[:, n, 6:8], BN[:, n, 0:6]).then_inc(z_var, 1)
            for n in range(TB):
                dve.wait_ge(z_std, n + 1)
                link(dve.reciprocal(BN[:, n, 9:10], BN[:, n, 8:9]))
                dve.tensor_scalar(Z1[:, n, :], Z1[:, n, :], BN[:, n, 6:7], BN[:, n, 9:10], ALU.subtract, ALU.mult)\
                   .then_inc(z_norm, 1)
            dve.wait_ge(taken["A"], TAKEN[GROUP0["even_u"] + 3])
            for n in range(TB):
                b = take("even_gate", n)
                for c in range(4):
                    i = dve.scalar_tensor_tensor(CAT[:, 4 + c, n * P:(n + 1) * P], b[:, c * P:(c + 1) * P],
                                                 par_("sgu", c, 1), tab(TA, "bsp", c * P, P), ALU.mult, ALU.add)
                i.then_inc(taken["D"], 1)
                dve.wait_ge(taken["D"], TAKEN[GROUP0["even_gate"] + n])
                for c in range(4):
                    dve.tensor_tensor(CAT[:, 4 + c, n * P:(n + 1) * P], CAT[:, 4 + c, n * P:(n + 1) * P],
                                      U1[:, c, n * P:(n + 1) * P], ALU.mult).then_inc(sg_ready, 1)
            attention("even", 1.0, YT1, lambda b: CAT[:, 0:4, b * P:(b + 1) * P], sink=True)
            for j in range(KD):
                residual("even_out", j, T, MOD[:, 0, 16 + j, 0:1])

            def moe_pass(q, p, g2, side=False):
                flat = MOD[:, :, :, :].rearrange("p a b c -> p (a b c)")

                def side_strip(i):
                    dve.wait_ge(side_in, i * 16 + 16)
                    products(lambda k: STAGE[:, k, :].rearrange("p (a b) -> p a b", b=T),
                             lambda k, s: SIDEC[:, bass.ds(i * (2 * KD) + (2 * k + s), 1)],
                             lambda s: SACC[s], side_step, i * 15, side_summed)

                dve.memset(YP[:, :], 0.0).then_inc(q["res_added"], 1)
                dve.memset(SPT[:, :], 0.0).then_inc(q["res_added"], 1)
                dve.wait_ge(q["res_added"], 70 * p + 2)
                dve.tensor_copy(SPT[:, 0:1], SPT[:, 0:1]).then_inc(q["spt_ready"], 1)

                def columns_of(i, dst, by, ready):
                    for e in range(2):
                        for blk in range(TB):
                            m = dve.tensor_scalar(dst[:, blk, e * C:(e + 1) * C], par_("slot"),
                                                  RK[:, blk, bass.ds(i * 2 + e, 1)], by[:, blk, bass.ds(i * 2 + e, 1)],
                                                  ALU.is_equal, ALU.mult)
                    m.then_inc(q[ready], 1)

                def add(i):
                    dve.wait_ge(q["res_added"], i * 4 + (70 * p + 2))
                    for r in range(4):
                        dve.wait_ge(q["comb_ready"], i * 4 + (68 * p + r + 1))
                        for h in range(2):
                            c = 2 * r + h
                            m = dve.scalar_tensor_tensor(X[:, c, 0:T], bank[6 + r % 2][:, h * T:(h + 1) * T], g2(c),
                                                         X[:, c, 0:T], ALU.mult, ALU.add)
                        m.then_inc(q["res_added"], 1)

                columns_of(0, GE, MM, "ge_ready")
                columns_of(0, GW, GG, "gw_ready")
                with dve.Fori(0, PAIRS) as i:
                    dve.wait_ge(q["gath_ready"], i + (17 * p + 1))
                    columns_of(i + 1, GE, MM, "ge_ready")
                    if side:
                        side_strip(i)
                    dve.wait_ge(q["sil_ready"], i + (16 * p + 1))
                    dve.wait_ge(q["up_ready"], i + (16 * p + 1))
                    dve.tensor_tensor(HTOK, SIL, bank[1][:, :], ALU.mult).then_inc(q["hid_ready"], 1)
                    add(i)
                    dve.wait_ge(q["tr_ready"], i + (16 * p + 1))
                    if side:
                        at = 2 * NMOD
                        dve.tensor_tensor(flat[:, bass.ds(i * 8 + at, 8)], bank[6][:, T:T + 8],
                                          par_sb[:, bass.ds(i * 8 + (PAR["bias"][0] + at), 8)], ALU.add)
                    dve.tensor_copy(SPT[:, :], bank[6][:, 0:T]).then_inc(q["spt_ready"], 1)
                    columns_of(i + 1, GW, GG, "gw_ready")
                add(PAIRS)

            def moe(l):
                g2 = lambda c: MOD[:, l, 40 + c, 0:1]
                big = -NEG
                lg = take(f"route{l}", 0, TB * ROUTES)
                for b in range(TB):
                    dve.memset(GL8[:, b, :], NEG)
                for t_ in (RK, MM, GG):
                    dve.memset(t_, 0.0)
                dve.tensor_tensor(LG.rearrange("p a b -> p (a b)"), lg, par_("rbias", l * TB * ROUTES, TB * ROUTES), ALU.add)\
                   .then_inc(taken["D"], 1)
                wait_taken(dve, f"route{l}", 0)
                link(dve.tensor_copy(GL8[:, :, 0:4], LG[:, :, 0:4]))
                for b in range(TB):
                    m = dve.max(MX8[:, b, :], GL8[:, b, :])
                link(m)
                for b in range(TB):
                    m = dve.max_index(IX8[:, b, :], MX8[:, b, :], GL8[:, b, :])
                link(m)
                link(dve.tensor_copy(IXF, IX8))
                for b in range(TB):
                    m = dve.tensor_scalar(GM[:, b, :], par_("group"), IXF[:, b, 0:1], None, ALU.is_equal)
                link(m)
                for b in range(TB):
                    m = dve.tensor_scalar(ME[:, b, :], GM[:, b, :], big, -big, ALU.mult, ALU.add)
                link(m)
                link(dve.tensor_tensor(GM, GM, LG[:, :, 4:36], ALU.mult))
                link(dve.tensor_tensor(ME, ME, GM, ALU.add))
                for b in range(TB):
                    m = dve.max(V8[:, b, :], ME[:, b, :])
                link(m)
                for b in range(TB):
                    dve.max_index(IE8[:, b, :], V8[:, b, :], ME[:, b, :])
                dve.tensor_scalar(SML[:, :, 0], MX8[:, :, 0], -1.0, None, ALU.mult)
                link(dve.tensor_tensor(SML[:, :, 2], V8[:, :, 1], V8[:, :, 0], ALU.subtract))
                dve.tensor_copy(IEF, IE8).then_inc(rt_exp_in, 1)
                dve.wait_ge(rt_exp_in, l + 1)
                for b in range(TB):
                    dve.tensor_scalar(O0[:, b, :], par_("expert"), IEF[:, b, 0:1], None, ALU.is_equal)
                    m = dve.tensor_scalar(O1[:, b, :], par_("expert"), IEF[:, b, 1:2], None, ALU.is_equal)
                link(m)
                dve.tensor_tensor(MM[:, :, 0:32], O0, O1, ALU.add).then_inc(rt_mask, 1)
                dve.wait_ge(rt_exp, l + 1)
                link(dve.tensor_scalar(SML[:, :, 4], SML[:, :, 3], 1.0, None, ALU.add))
                link(dve.tensor_tensor(SML[:, :, 5], SML[:, :, 4], SML[:, :, 1], ALU.mult))
                link(dve.reciprocal(SML[:, :, 6], SML[:, :, 5]))
                link(dve.tensor_tensor(SML[:, :, 7], SML[:, :, 6], SML[:, :, 3], ALU.mult))
                for b in range(TB):
                    m = dve.tensor_scalar(O0[:, b, :], O0[:, b, :], SML[:, b, 6:7], None, ALU.mult)
                link(m)
                for b in range(TB):
                    m = dve.scalar_tensor_tensor(GG[:, b, 0:32], O1[:, b, :], SML[:, b, 7:8], O0[:, b, :], ALU.mult, ALU.add)
                link(m)
                r = take(f"rank{l}", 0)
                dve.tensor_copy(RK[:, :, 0:32], r[:, 0:64].rearrange("p (a b) -> p a b", a=TB))
                dve.tensor_copy(MS, r[:, 64:96]).then_inc(taken["D"], 1)
                wait_taken(dve, f"rank{l}", 0)
                link(dve.reduce_max(CMAX, MS, AXX))
                link(dve.tensor_scalar(CMAX, CMAX, float(C), None, ALU.is_gt))
                dve.tensor_copy(FLAG[:, l:l + 1], CMAX).then_inc(flag_ready, 1)
                moe_pass(main, l, g2, side=l == 0)
                dve.wait_ge(flag_ready, l + 1)
                full = dve.value_load(FLAG[0:1, l:l + 1], min_val=0, max_val=1)
                with dve.If(full > 0):
                    q = over[l]
                    dve.wait_ge(main["res_added"], 70 * (l + 1))
                    with dve.Fori(0, PASSES - 1) as p:
                        dve.tensor_scalar(RK, RK, -float(C), None, ALU.add).then_inc(tmp_ready, 1)
                        dve.wait_ge(tmp_ready, p + 1 if l == 0 else p + 1)
                        moe_pass(q, p, g2)
                    dve.wait_ge(q["res_added"], 70 * (PASSES - 1))
                dve.wait_ge(main["res_added"], 70 * (l + 1))

            link(gain(2, 0, 32, 0, par_("g2", 0, KD)))
            last_taken(dve, "even_out")
            norm("n2_0", T, lambda k: X[:, k, 0:T], lambda k: A[:, k, 0:T], [(0, T, lambda k: GSC[:, 2, k:k + 1])], D)
            moe(0)

            gain(3, 1, 8, 0, par_("g1", KD, KD))
            link(gain(4, 1, 32, 0, par_("g2", KD, KD)))
            norm("n1_1", T, lambda k: X[:, k, 0:T], lambda k: A[:, k, 0:T], [(0, T, lambda k: GSC[:, 3, k:k + 1])], D)
            for s in range(2):
                m = dve.memset(YC[:, s, :], 0.0)
            link(m)
            for c in range(KD):
                cw = lambda tap: par_("conv", tap * KD + c, 1)
                y, t_ = YC[:, c % 2, :], CT[:, c % 2, :]
                wait_taken(dve, "odd_in", 3 * c + 1)
                dve.tensor_tensor(y[:, 1:T + 1], CG[:, c % 2, :], take("odd_in", 3 * c + 2, T), ALU.mult)\
                   .then_inc(taken["D"], 1)
                wait_taken(dve, "odd_in", 3 * c + 2)
                link(dve.tensor_scalar(t_, y[:, 0:T], cw(0), None, ALU.mult))
                link(dve.scalar_tensor_tensor(t_, y[:, 1:T + 1], cw(1), t_, ALU.mult, ALU.add))
                link(dve.scalar_tensor_tensor(t_, y[:, 2:T + 2], cw(2), t_, ALU.mult, ALU.add))
                dve.tensor_tensor(CV[:, c, :], t_, BG[:, c % 2, :], ALU.mult).then_inc(cv_ready, 1)
            for j in range(KD):
                residual("odd_out", j, T, MOD[:, 1, 16 + j, 0:1])
            last_taken(dve, "odd_out")
            norm("n2_1", T, lambda k: X[:, k, 0:T], lambda k: A[:, k, 0:T], [(0, T, lambda k: GSC[:, 4, k:k + 1])], D)
            plus_one(0, KD, 2 * KD)
            moe(1)
            norm("final", T, lambda k: X[:, k, 0:T], lambda k: X[:, k, 0:T], [(0, T, lambda k: par_("gf", k, 1))], D)

            dve.wait_ge(mid_ready, NMID["final"] + KD)
            dve.wait_ge(ctx2_in, 16)
            dve.wait_ge(tabb_in, 16)
            norm("ln_in", 2 * T, lambda k: X[:, k, :], lambda k: X[:, k, :],
                 [(0, 2 * T, lambda k: par_("lni_g", k, 1))], D, mean=True)

            def modulate(l, shift, scale, w, after):
                for k in range(KD):
                    dve.wait_ge(norm_out, after + k + 1)
                    for s in range(w // T):
                        m = dve.tensor_scalar(A[:, k, s * T:(s + 1) * T], X[:, k, s * T:(s + 1) * T],
                                              MODP[:, l, scale + k, s:s + 1], MOD[:, 2 + l, shift + k, s:s + 1],
                                              ALU.mult, ALU.add)
                    m.then_inc(a_ready, 1)

            def outer(l, stage, gate, w):
                for j in range(KD):
                    b = take(stage, j)
                    for s in range(w // T):
                        m = dve.tensor_scalar(RT[:, j % 2, s * T:(s + 1) * T], b[:, s * T:(s + 1) * T],
                                              MODP[:, l, gate + j, s:s + 1], None, ALU.mult)
                    link(m)
                    dve.scalar_tensor_tensor(X[:, j, 0:w], X[:, j, 0:w], ALPHA, RT[:, j % 2, 0:w], ALU.mult, ALU.add)\
                       .then_inc(taken["D"], 1)
                wait_taken(dve, stage, KD - 1)

            for l in range(2):
                w = streams(l)
                modulate(l, 0, 8, 2 * T, NOUT["ln_in"] if l == 0 else NOUT["ln2_0"])
                for j in range(w // P):
                    dve.tensor_copy(FT[:, j, :], take(f"f{l}", j, 512)).then_inc(taken["D"], 1)
                for j in range(4 * w // T):
                    s, g = j // 4, j % 4
                    dve.tensor_copy(YB[0][:, g, s * T:(s + 1) * T], take(f"idft{l}", j, T)).then_inc(taken["D"], 1)
                for j in range(4):
                    dve.tensor_scalar(NQ[:, j, 0:w], take(f"nq{l}", j, w), 0.125, None, ALU.mult).then_inc(taken["D"], 1)
                attention(f"na{l}", 1.0, YT2, lambda b: YB[1][:, :, b * P:(b + 1) * P])
                for j in range(4):
                    n = w if j < 2 else 2 * T
                    dve.tensor_copy(LOW[:, j, 0:n], take(f"low{l}", j, n)).then_inc(taken["D"], 1)
                wait_taken(dve, f"low{l}", 3)
                norm(f"cq{l}", w, lambda k: LOW[:, k, 0:w], lambda k: LOW[:, k, 0:w],
                     [(0, w, lambda k: par_("gq", l * 2 + k, 1))], 2 * P)
                norm(f"ckv{l}", 2 * T, lambda k: LOW[:, 2, :], lambda k: LOW[:, 2, :],
                     [(0, 2 * T, lambda k: par_("gkv", l, 1))], P)
                rot = slice(64, 96)
                cos, sin = tab(TC, "cos")[rot, :], tab(TC, "sin")[rot, :]
                dve.tensor_tensor(QT[rot, 0, :], take(f"krope{l}", 0, T)[rot, :], sin, ALU.mult).then_inc(taken["D"], 1)
                link(dve.tensor_tensor(LOW[rot, 3, 0:T], LOW[rot, 3, 0:T], cos, ALU.mult))
                dve.wait_ge(taken["D"], TAKEN[GROUP0[f"krope{l}"]])
                dve.tensor_tensor(LOW[rot, 3, 0:T], LOW[rot, 3, 0:T], QT[rot, 0, :], ALU.add).then_inc(rope_done, 1)
                dve.wait_ge(rope_done, 5 + 9 * l + 1)
                for h in range(HEADS):
                    dve.tensor_copy(MK[rot, h, :], LOW[rot, 3, :]).then_inc(kr_copied, 1)
                for j in range(4):
                    dve.tensor_copy(V2[:, j, :], take(f"mv{l}", j, 512)).then_inc(taken["D"], 1)
                for j in range(8):
                    wait_taken(dve, f"mq{l}", j)
                    dve.tensor_tensor(QT[rot, j % 2, :], take(f"qrope{l}", j, T)[rot, :], sin, ALU.mult).then_inc(taken["D"], 1)
                    link(dve.tensor_tensor(A[rot, j, 0:T], A[rot, j, 0:T], cos, ALU.mult))
                    dve.tensor_tensor(A[rot, j, 0:T], A[rot, j, 0:T], QT[rot, j % 2, :], ALU.add).then_inc(rope_done, 1)
                attention(f"mla{l}", MLA_SCALE, YT2, lambda b: YB[2][:, :, b * P:(b + 1) * P])
                modulate(l, 0, 8, w, 0)
                for o in range(KD):
                    if l == 0:
                        mod_strip(MERGE_MOD + o)
                    for b in range(3):
                        j = (o * 3 + b) * 2
                        wait_taken(dve, f"merge{l}", j)
                        s = SG[:, (o * 3 + b) % 2, 0:w]
                        if b == 0:
                            dve.tensor_tensor(MG[:, o, 0:w], s, take(f"merge{l}", j + 1, w), ALU.mult).then_inc(taken["D"], 1)
                        else:
                            link(dve.tensor_tensor(RT[:, b % 2, 0:w], s, take(f"merge{l}", j + 1, w), ALU.mult))
                            wait_taken(dve, f"merge{l}", j - 1)
                            dve.tensor_tensor(MG[:, o, 0:w], MG[:, o, 0:w], RT[:, b % 2, 0:w], ALU.add)\
                               .then_inc(taken["D"], 1)
                if l == 0:
                    take_mods(2, 16, 48, FFN_MOD, 3)
                    plus_one(0, 16, 48)
                outer(l, f"out{l}", 16, w)
                norm(f"ln1_{l}", w, lambda k: X[:, k, 0:w], lambda k: X[:, k, 0:w],
                     [(0, w, lambda k: par_("ln1_g", l * KD + k, 1))], D, mean=True)
                modulate(l, 24, 32, w, NOUT[f"ln1_{l}"])
                for j in range(KF):
                    if l == 0 and j % 2 == 0:
                        mod_strip(FFN_MOD + j // 2)
                    wait_taken(dve, f"up{l}", 2 * j)
                    dve.tensor_tensor(HB[:, j, 0:w], SB_[:, j % 2, 0:w], take(f"up{l}", 2 * j + 1, w), ALU.mult)\
                       .then_inc(taken["D"], 1)
                if l == 0:
                    mod_strip(FFN_MOD + 11)
                outer(l, f"down{l}", 40, w)
                if l == 0:
                    take_mods(3, 0, NMOD, len(MODS), 4)
                    plus_one(1, 0, NMOD)
                norm(f"ln2_{l}", w, lambda k: X[:, k, 0:w], lambda k: X[:, k, 0:w],
                     [(0, w, lambda k: par_("ln2_g", l * KD + k, 1))], D, mean=True)


def _f(a):
    return np.ascontiguousarray(np.asarray(a))


def _vec(a):
    return _f(a).reshape(-1, P).T


def _fm(w):
    K, N = w.shape
    return w.reshape(K // P, P, N // P, P).transpose(2, 0, 1, 3).reshape(-1, P, P)


def _tm(w):
    K, N = w.shape
    return w.reshape(K // P, P, N // P, P).transpose(0, 2, 1, 3).reshape(-1, P, P)


def _pad(n):
    return np.zeros((n, P, P), np.float32)


def lay_out(I):
    strips = np.empty((STRIPS + SIDE, P, TILES, P), np.float32)

    def put(stage, parts, first=None):
        tiles = np.concatenate(parts, 0) if len(parts) > 1 else parts[0]
        n = len(tiles) // TILES
        to = places(stage, "E") if first is None else list(range(first, first + n))
        assert n * TILES == len(tiles) and len(to) == n, (stage, len(tiles))
        strips[to] = tiles.reshape(n, TILES, P, P).transpose(0, 2, 1, 3)

    ada, mod2 = I["w_ada"], I["w_mod_2"]
    ada = [_tm(ada[l].reshape(D, 12, 512)[:, i]) for l in range(2) for i in range(12)]
    mod2 = [_tm(mod2[l].reshape(D, 12, 512)[:, i]) for l in range(2) for i in range(12)]
    sets = (ada[:12], ada[12:], mod2[:12], mod2[12:])
    for s, which, chunk in MODS:
        put(None, [sets[which][chunk // 4]], s)
    for i, parts in enumerate(sets[1] + sets[2][:SIDE - SIDE_ADA]):
        put(None, [parts], STRIPS + i)
    w = I["w_in_even"][0]
    order = np.concatenate([np.r_[64 * c:64 * c + 64, 64 * (c + 4):64 * (c + 4) + 64] for c in range(4)])
    put("even", [_fm(w[:, :512][:, order]), _fm(w[:, 512:640]), _tm(w[:, 640:768]), _fm(w[:, 768:1280]),
                 _tm(w[:, 1280:1792]), _pad(16)])
    put("even_out", [_fm(I["w_out_even"][0])])
    for l in range(2):
        for i in range(PAIRS):
            parts = []
            for name in ("w_gate", "w_up"):
                parts += [_tm(I[name][l, e]) for e in (2 * i, 2 * i + 1)]
            parts += [_tm(I["w_down"][l, e]) for e in (2 * i, 2 * i + 1)]
            put(None, parts, FIRST[f"moe{l}"] + 6 * i)
    wi, wo = I["w_in_odd"][0], I["w_out_odd"][0]
    cols = np.concatenate([np.r_[c * P:(c + 1) * P, D + c * P:D + (c + 1) * P, 2 * D + c * P:2 * D + (c + 1) * P]
                           for c in range(KD)])
    put("odd", [_fm(wi[:, cols]), _fm(wo)])

    t = np.arange(T)
    r, cl = t // 64, t % 64
    start = np.clip(cl - 8, 0, 48)
    inside = (cl[None, :] >= start[:, None]) & (cl[None, :] < start[:, None] + 16)
    dr = r[None, :] - r[:, None] + 7
    dc = np.clip(cl[None, :] - cl[:, None] + 15, 0, 30)
    for l in range(2):
        w = I["w_in_2"][l]
        o = np.cumsum([0, 512, 512, 512, 512, 256, 128, 32])
        f, nq, nk, nv, cq, ckv, kr = (w[:, o[i]:o[i + 1]] for i in range(7))
        g = w[:, o[7]:]
        put(f"l{l}_na", [_tm(f), _fm(nq), _fm(nk), _tm(nv)])
        bias = np.where(inside[None], I["na_rpb_2"][l][:, dr, dc], np.float32(NEG)).astype(np.float32)
        strips[FIRST[f"l{l}_bias"]] = bias.reshape(HEADS, TB, P, T).transpose(2, 0, 1, 3).reshape(P, TILES, P)
        krp = np.zeros((D, P), np.float32)
        krp[:, 64:96] = kr
        put(f"l{l}_low", [_fm(cq), _fm(ckv), _fm(krp)])
        q = np.zeros((256, HEADS, P), np.float32)
        q[:, :, :64] = I["w_uq_2"][l].reshape(256, HEADS, 64)
        q[:, :, 64:96] = I["w_qr_2"][l].reshape(256, HEADS, 32)
        k = np.zeros((P, HEADS, P), np.float32)
        k[:, :, :64] = I["w_uk_2"][l].reshape(P, HEADS, 64)
        put(f"l{l}_up", [_fm(q.reshape(256, -1)), _fm(k.reshape(P, -1)), _tm(I["w_uv_2"][l]), _pad(4)])
        gt = _fm(g).reshape(3, KD, KD, P, P)
        bt = np.stack([_fm(I["w_branch_2"][l, b]).reshape(KD, 4, P, P) for b in range(3)])
        both = np.concatenate([gt, bt], 2).transpose(1, 0, 2, 3, 4).reshape(-1, P, P)
        put(f"l{l}_merge", [both])
        put(f"l{l}_out", [_fm(I["w_out_2"][l])])
        gu = np.stack([_fm(I["w_ffn_gate_2"][l]).reshape(KF, KD, P, P), _fm(I["w_ffn_up_2"][l]).reshape(KF, KD, P, P)], 1)
        put(f"l{l}_ffn", [gu.reshape(-1, P, P), _fm(I["w_ffn_down_2"][l]), _pad(16)])

    par = np.zeros((P, N_PAR), np.float32)

    def p(name, a):
        o, n = PAR[name]
        par[:, o:o + n] = a.reshape(-1, n)

    pair = lambda a, b: np.stack([_vec(a), _vec(b)], -1).reshape(P, -1)
    p("c", pair(I["c"], I["c_ctx"]))
    p("c_2", pair(I["c_2"], I["c_ctx_2"]))
    bias = np.concatenate([_vec(I["b_ada"]), _vec(I["b_mod_2"])], 1)
    p("bias", np.repeat(bias, 2, axis=1))
    p("g1", _vec(I["g_norm1"]))
    p("g2", _vec(I["g_norm2"]))
    p("gf", _vec(I["g_final"]))
    p("sgu", _vec(I["g_sgu"]))
    p("conv", _vec(I["conv_w"]))
    for a, b in (("lni_g", "ln_in_g_2"), ("lni_b", "ln_in_b_2"), ("ln1_g", "ln1_g_2"), ("ln1_b", "ln1_b_2"),
                 ("ln2_g", "ln2_g_2"), ("ln2_b", "ln2_b_2"), ("gq", "mla_q_norm_g_2"), ("gkv", "mla_kv_norm_g_2")):
        p(a, _vec(I[b]))
    p("sink", np.broadcast_to(I["attn_sink"].reshape(1, HEADS), (P, HEADS)))
    rb = np.stack([np.concatenate([I["b_router_group"][l], I["b_router_expert"][l]]) for l in range(2)])
    p("rbias", np.broadcast_to(np.repeat(rb[:, None], TB, 1).reshape(1, -1), (P, 2 * TB * ROUTES)))
    p("ident", np.eye(P, dtype=np.float32))
    p("ones", np.ones((P, P), np.float32))
    p("before", (np.arange(P)[:, None] < np.arange(P)[None, :]).astype(np.float32))
    p("expert", np.broadcast_to(np.arange(EXPERTS, dtype=np.float32), (P, EXPERTS)))
    p("group", np.broadcast_to(np.arange(EXPERTS) // (EXPERTS // GROUPS), (P, EXPERTS)).astype(np.float32))
    p("slot", np.broadcast_to(np.arange(C, dtype=np.float32), (P, C)))

    ta = np.zeros((P, N_TA), np.float32)
    tc = np.zeros((P, N_TC), np.float32)

    def q(arr, where, name, a):
        o, n = where[name]
        arr[:, o:o + n] = np.asarray(a, np.float32).reshape(P, n)

    d = np.arange(P) % 64
    inv = (10000.0 ** (-np.arange(16, dtype=np.float32) / 16)).astype(np.float32)
    pos = np.where((d < 32)[:, None], r[None, :], cl[None, :]).astype(np.float32)
    ang = (pos * inv[d % 16][:, None]).astype(np.float32)
    second = (d % 32) >= 16
    q(ta, TA, "cos", np.cos(ang))
    q(ta, TA, "sin", np.where(second[:, None], np.sin(ang), -np.sin(ang)))
    partner = np.where(second, np.arange(P) - 16, np.arange(P) + 16)
    sw = np.zeros((P, P), np.float32)
    sw[partner, np.arange(P)] = 1
    q(ta, TA, "swap", sw)
    near = np.abs(t[None, :] - t[:, None]) <= 128
    q(ta, TA, "mask", np.where(near, 0.0, NEG).reshape(TB, P, T).transpose(1, 0, 2))
    bsp = np.repeat(_f(I["b_spatial"])[0].reshape(4, 2, 1, P), 64, 2).transpose(1, 2, 0, 3)
    q(ta, TA, "bsp", bsp)
    rw = np.concatenate([I["w_router_group"], I["w_router_expert"]], 2).reshape(2, KD, P, ROUTES).transpose(2, 0, 1, 3)
    q(ta, TA, "router", rw)

    inv = (10000.0 ** (-np.arange(8, dtype=np.float32) / 8)).astype(np.float32)
    ang = np.concatenate([r[:, None].astype(np.float32) * inv, cl[:, None].astype(np.float32) * inv], 1).T
    cos, sin = np.ones((P, T)), np.zeros((P, T))
    cos[64:80] = cos[80:96] = np.cos(ang)
    sin[64:80], sin[80:96] = -np.sin(ang), np.sin(ang)
    q(tc, TC, "cos", cos)
    q(tc, TC, "sin", sin)
    sw = np.zeros((P, P), np.float32)
    i = np.arange(16)
    sw[80 + i, 64 + i] = sw[64 + i, 80 + i] = 1
    q(tc, TC, "swap", sw)
    a = 2 * np.pi * (np.outer(t, t) % T) / T
    q(tc, TC, "dft", np.concatenate([np.cos(a), np.sin(a)], 1).reshape(TB, P, 2 * T).transpose(1, 0, 2))
    i = np.arange(P)
    a = 2 * np.pi * (np.outer(i, i) % P) / P
    q(tc, TC, "cd", np.cos(a) / math.sqrt(T * P))
    q(tc, TC, "sd", -np.sin(a) / math.sqrt(T * P))

    fm = lambda a: _f(a).reshape(T, KD, P).transpose(2, 1, 0)
    return {
        "stream": strips.reshape(STRIPS + SIDE, P, STRIP), "par": par, "tab_a": ta, "tab_b": tc,
        "wsp": _f(I["w_spatial"][0].transpose(2, 0, 1)),
        "xt": _f(np.concatenate([fm(I["x"]), fm(I["ctx"])], 2)), "ctx2t": _f(fm(I["ctx_2"])),
    }


def kernel(**inputs):
    import concourse.bacc as _bacc
    from concourse.bass_utils import run_bass_kernel_spmd as _run

    nc = _bacc.Bacc("TRN2", target_bir_lowering=False, num_devices=1)
    arrays = lay_out({k: np.asarray(v) for k, v in inputs.items()})
    args = [nc.dram_tensor("in_" + k, a.shape, F32, kind="ExternalInput").ap() for k, a in arrays.items()]
    args.append(nc.dram_tensor("out_0", (P, KD, T), F32, kind="ExternalOutput").ap())
    build_program(nc, *args)
    r = _run(nc, [{"in_" + k: a for k, a in arrays.items()}], core_ids=[0])
    got = r.results[0]["out_0"]
    return np.ascontiguousarray(got.transpose(2, 1, 0).reshape(1, T, D))
```

```python
import math
from contextlib import ExitStack

import concourse.bass as bass
import numpy as np
from concourse import mybir

F32 = mybir.dt.float32
I32 = mybir.dt.int32
U32 = mybir.dt.uint32
ALU = mybir.AluOpType
ACT = mybir.ActivationFunctionType
AXX = mybir.AxisListType.X

P = 128
D = 1024
KD = D // P
T = 256
TB = T // P
HEADS = 8
NMOD = 6 * KD
EXPERTS, GROUPS = 32, 4
PAIRS = EXPERTS // 2
HID = 512
C = 64
PASSES = T // C
FFN = 2816
KF = FFN // P
ROUTES = GROUPS + EXPERTS
ALPHA = 4.0 ** 0.25
EPS1, EPS2 = 1e-6, 1e-5
NEG = -1e30
MLA_SCALE = 96.0 ** -0.5
MLA_ROWS = 96

TILES = 32
RING = 6
STRIP = TILES * P
ORDER = {
    "even": "EMMM" * 3 + "E", "even_out": "EEMMM", "odd": "EMM" * 4 + "EM" * 4,
    "l0_merge": "EM" * 8 + "E", "l0_ffn": "EM" * 12 + "E" * 5,
}
STAGES = [
    ("ada0a", 4), ("even", 13), ("even_out", 5),
    ("moe0", 3 * EXPERTS), ("odd", 20), ("moe1", 3 * EXPERTS),
    ("l0_na", 4), ("l0_bias", 1), ("l0_low", 1), ("l0_up", 1), ("l0_merge", 17), ("l0_out", 2), ("l0_ffn", 29),
    ("l1_na", 4), ("l1_bias", 1), ("l1_low", 1), ("l1_up", 1), ("l1_merge", 9), ("l1_out", 2), ("l1_ffn", 17),
]
FIRST = {}
_at = 0
for _name, _n in STAGES:
    FIRST[_name] = _at
    _at += _n
STRIPS = _at


def places(stage, kind):
    return [FIRST[stage] + i for i, x in enumerate(ORDER.get(stage, "E" * dict(STAGES)[stage])) if x == kind]


MODS = [(FIRST["ada0a"] + i, 0, 4 * i, 2) for i in range(4)]
_sets = [(0, 16 + 4 * i, 1) for i in range(8)] + [(1, 4 * i, 1) for i in range(4)]
MODS += [(s, *x) for s, x in zip(places("even", "M") + places("even_out", "M"), _sets)]
EVEN_OUT_MOD, ODD_MOD = len(MODS) - 3, len(MODS)
_sets = [(1, 16 + 4 * i, 1) for i in range(8)] + [(2, 4 * i, 2) for i in range(4)]
MODS += [(s, *x) for s, x in zip(places("odd", "M"), _sets)]
ODD_REDUCE, _n = [], ODD_MOD
for _part in ORDER["odd"].split("E")[1:]:
    ODD_REDUCE.append((_n, _n + len(_part)))
    _n += len(_part)
MERGE_MOD = len(MODS)
MODS += [(s, 2, 16 + 4 * i, 2) for i, s in enumerate(places("l0_merge", "M"))]
FFN_MOD = len(MODS)
MODS += [(s, 3, 4 * i, 2 if i < 4 else 1) for i, s in enumerate(places("l0_ffn", "M"))]


def mod_rows(n):
    rows = lambda m: [2 * (m % 2), 2 * (m % 2) + 1] if MODS[m][3] == 2 else [m % 4]
    before = [m + 1 for m in range(n) if set(rows(m)) & set(rows(n))]
    return rows(n), max(before, default=0)


LAYER_STREAMS = (2, 1)
LIN = [
    ("even_q", "DDDD"), ("even_k", "D"), ("even_v", "D"), ("even_rope", "DDDDD"),
    ("even_u", "AAAA"), ("even_z", "AA"), ("even_gate", "DD"), ("even_out", "D" * KD),
    ("route0", "D"), ("turn0", "AAAA"), ("rank0", "D"),
    ("odd_in", "AAD" * KD), ("odd_out", "D" * KD),
    ("route1", "D"), ("turn1", "AAAA"), ("rank1", "D"),
]
for _l, _s in enumerate(LAYER_STREAMS):
    LIN += [(f"f{_l}", "D" * 2 * _s), (f"dft{_l}", "A" * 4 * _s), (f"idft{_l}", "D" * 4 * _s),
            (f"nq{_l}", "DDDD"), (f"nk{_l}", "AAAA"), (f"nv{_l}", "AAAA"),
            (f"low{_l}", "DDDD"), (f"krope{_l}", "D"), (f"mq{_l}", "A" * 8), (f"mk{_l}", "A" * 8),
            (f"mv{_l}", "DDDD"), (f"qrope{_l}", "D" * 8),
            (f"merge{_l}", "ADADAD" * KD), (f"out{_l}", "D" * KD), (f"up{_l}", "AD" * KF), (f"down{_l}", "D" * KD)]
GROUP0, TAKER, TAKEN = {}, [], []
for _name, _who in LIN:
    GROUP0[_name] = len(TAKER)
    for _w in _who:
        TAKER.append(_w)
        TAKEN.append(TAKER.count(_w))
LIN_BANKS = 4

NORMS = ["n1_0", "n2_0", "n1_1", "n2_1", "final", "ln_in",
         "cq0", "ckv0", "ln1_0", "ln2_0", "cq1", "ckv1", "ln1_1", "ln2_1"]
NCHUNK = {n: 2 if n[:2] == "cq" else 1 if n[:3] == "ckv" else KD for n in NORMS}
NBASE, NMEAN, NSTAT, NOUT, NMID, NXC = {}, {}, {}, {}, {}, {}
_b = _m = _o = _d = _x = 0
for _i, _n in enumerate(NORMS):
    NBASE[_n], NSTAT[_n], NMEAN[_n], NOUT[_n], NMID[_n], NXC[_n] = _b, _i, _m, _o, _d, _x
    _b += NCHUNK[_n]
    _d += NCHUNK[_n]
    if _n[:2] == "ln":
        _m += 1
        _x += KD
    if _n[:2] in ("n1", "n2") or _n == "ln2_1":
        _o += KD

ATT, _u = {}, 0
for _n, _q in [("even", 2), ("na0", 4), ("mla0", 4), ("na1", 2), ("mla1", 2)]:
    ATT[_n] = (_q, _u)
    _u += _q * HEADS

def columns(parts):
    at, out = 0, {}
    for name, n in parts:
        out[name] = (at, n)
        at += n
    return out, at


PAR, N_PAR = columns([
    ("c", 2 * KD), ("c_2", 2 * KD), ("bias", 4 * NMOD * 2), ("g1", 2 * KD), ("g2", 2 * KD), ("gf", KD),
    ("sgu", 4), ("conv", 3 * KD), ("lni_g", KD), ("lni_b", KD),
    ("ln1_g", 2 * KD), ("ln1_b", 2 * KD), ("ln2_g", 2 * KD), ("ln2_b", 2 * KD),
    ("gq", 4), ("gkv", 2), ("sink", HEADS), ("rbias", 2 * TB * ROUTES),
    ("ident", P), ("ones", P), ("before", P), ("expert", EXPERTS), ("group", EXPERTS), ("slot", C),
])
TA, N_TA = columns([("cos", T), ("sin", T), ("swap", P), ("mask", TB * T), ("bsp", 4 * P), ("router", 2 * KD * ROUTES)])
TC, N_TC = columns([("dft", TB * 2 * T), ("cd", P), ("sd", P), ("cos", T), ("sin", T), ("swap", P)])


def build_program(nc, stream, par, tab_a, tab_b, wsp_d, xt, ctx2t, out):
    with ExitStack() as ctx:
        def sb(name, shape, dt=F32):
            return ctx.enter_context(nc.sbuf_tensor(name, shape, dt))

        def sem(name):
            return ctx.enter_context(nc.semaphore(name))

        ring = sb("ring", [P, RING, STRIP])
        X = sb("X", [P, KD, 2 * T])
        A = sb("A", [P, KD, 2 * T])
        par_sb = sb("par_sb", [P, N_PAR])
        tab_sb = sb("tab_sb", [P, max(N_TA, N_TC)])
        MOD = sb("MOD", [P, 4, NMOD, 2])
        MODP = sb("MODP", [P, 2, NMOD, 2])
        GSC = sb("GSC", [P, 5, KD])
        SILC = sb("SILC", [P, 2, KD, 2])
        FG = sb("FG", [P, KD, 2])
        FB = sb("FB", [P, KD, 2])
        EPS = sb("EPS", [P, 2])
        OPEN = sb("OPEN", [P, 1])
        MX = sb("MX", [P, 2, HEADS])
        NM = sb("NM", [P, 2, HEADS])
        SM = sb("SM", [P, 2, HEADS])
        ES = sb("ES", [P, 2, HEADS])
        BN = sb("BN", [P, TB, 10])
        FLAG = sb("FLAG", [P, 2], I32)
        work = sb("work", [P, 15360])
        bank = [ctx.enter_context(nc.psum_tensor(f"bank{i}", [P, 512], F32)) for i in range(8)]

        def par_(name, a=0, n=None):
            o, full = PAR[name]
            return par_sb[:, o + a:o + (full if n is None else a + n)]

        def tab(where, name, a=0, n=None):
            o, full = where[name]
            return tab_sb[:, o + a:o + (full if n is None else a + n)]

        def wk(at, *shape):
            n = int(np.prod(shape))
            v = work[:, at:at + n]
            if len(shape) == 2:
                v = v.rearrange("p (a b) -> p a b", b=shape[1])
            if len(shape) == 3:
                v = v.rearrange("p (a b c) -> p a b c", b=shape[1], c=shape[2])
            return v

        ident, ones, before = par_("ident"), par_("ones"), par_("before")

        SQ, MEAN, RSTD = wk(13312, 2, 512), wk(14336, 512), wk(14848, 512)
        QRAW, QK, KV_K = wk(0, 5, T), wk(1280, 5, T), wk(2560, 2 * T)
        V1, U1, Z1 = wk(3072, 4, P), wk(3584, 4, T), wk(4608, TB, 512)
        PR1, PT1 = wk(5632, 3, 512), wk(7168, 2, 512)
        CAT, WSP, TMP1 = wk(8704, KD, T), wk(10752, HEADS, P), wk(11776, 2, T)
        HT, XG = wk(0, TB, D), wk(2048, KD, P)
        SIL, HTOK, HE = wk(3072, HID), wk(3584, HID), wk(10752, 4, P)
        YP, GE, GW, SPT = wk(4096, D), wk(5120, TB, P), wk(5376, TB, P), wk(5632, T)
        RK, MM, GG = wk(5888, TB, 34), wk(5956, TB, 34), wk(6024, TB, 34)
        LG, GL8, MX8, V8 = wk(6100, TB, ROUTES), wk(6172, TB, 8), wk(6188, TB, 8), wk(6204, TB, 8)
        IX8, IE8 = wk(6220, TB, 8).bitcast(U32), wk(6236, TB, 8).bitcast(U32)
        IXF, IEF = wk(6252, TB, 8), wk(6268, TB, 8)
        SML = wk(6284, TB, 16)
        GM, ME, O0, O1 = wk(6316, TB, 32), wk(6380, TB, 32), wk(6444, TB, 32), wk(6508, TB, 32)
        MS, CMAX = wk(6572, 32), wk(6604, 1)
        BG, CG, YC = wk(0, 2, T), wk(512, 2, T), wk(1024, 2, T + 2)
        CV, CT = wk(1600, KD, T), wk(3648, 2, T)
        FT, FU = wk(0, 4, 512), wk(2048, 8, 512)
        NQ, NK, V2 = wk(0, 4, 512), wk(2048, 4, 512), wk(4096, 4, 512)
        MK = wk(0, KD, 512)
        YB = [wk(6144 + 2048 * b, 4, 512) for b in range(3)]
        LOW = YB[2]
        PR2, PT2 = wk(12288, 3, 512), wk(14336, 2, 512)
        XSUM = wk(11264, 512)
        MG, SG = wk(0, KD, 512), wk(4096, 2, 512)
        HB, SB_, RB = wk(0, KF, 512), wk(11264, 2, 512), wk(12288, 2, 512)
        RT = wk(12288, 2, 512)
        QT = wk(12288, 2, T)

        MACC1, MACC_OUT, MACC2 = wk(8704, 4, 512), wk(0, 4, 512), wk(13312, 4, 512)

        def macc(n, s):
            at = MACC_OUT if EVEN_OUT_MOD <= n < ODD_MOD else MACC1 if n < MERGE_MOD else MACC2
            return at[:, mod_rows(n)[0][s], :]

        par_in, x_in, taba_in, tabb_in, wsp_in = (sem(n) for n in ("par_in", "x_in", "taba_in", "tabb_in", "wsp_in"))
        ctx2_in, out_sent = sem("ctx2_in"), sem("out_sent")
        strip_in = [sem(f"strip_in{i}") for i in range(RING)]
        strip_used = sem("strip_used")
        silc_ready, eps_ready = sem("silc_ready"), sem("eps_ready")
        lin_ready = sem("lin_ready")
        taken = {"D": sem("taken_by_vector"), "A": sem("taken_by_scalar")}
        sum_ready, xc_ready, sq_ready, sq_used = (sem(n) for n in ("sum_ready", "xc_ready", "sq_ready", "sq_used"))
        mid_ready, norm_out, std_ready = (sem(n) for n in ("mid_ready", "norm_out", "std_ready"))
        xsum_step, xsum_ready, x_done, a_again = (sem(n) for n in ("xsum_step", "xsum_ready", "x_done", "a_again"))
        mod_taken = sem("mod_taken")
        mod_step, mod_summed, mod_done = sem("mod_step"), sem("mod_summed"), sem("mod_done")
        at_s, at_nm, at_p, at_t, at_ptc = (sem(n) for n in ("at_s", "at_nm", "at_p", "at_t", "at_ptc"))
        at_pn, at_pv, at_y, at_es = (sem(n) for n in ("at_pn", "at_pv", "at_y", "at_es"))
        z_var, z_std, z_norm, sg_ready = (sem(n) for n in ("z_var", "z_std", "z_norm", "sg_ready"))
        rt_exp_in, rt_exp, rt_mask, flag_ready = (sem(n) for n in ("rt_exp_in", "rt_exp", "rt_mask", "flag_ready"))
        cv_ready, a_ready, kr_copied, rope_done = (sem(n) for n in ("cv_ready", "a_ready", "kr_copied", "rope_done"))
        ranks_moved = [sem(f"o{l}_ranks_moved") for l in range(2)]
        dve_own = sem("dve_own")

        NAMES = ["xg_ready", "ge_ready", "gw_ready", "gath_ready", "gate_ready", "up_ready", "sil_ready", "hid_ready",
                 "htr_ready", "he_ready", "y_ready", "y_copied", "comb_ready", "res_added", "tr_ready", "spt_ready"]
        main = {n: sem("m_" + n) for n in NAMES}
        over = [{n: sem(f"o{l}_{n}") for n in NAMES} for l in range(2)]
        over_in = [[sem(f"o{l}_in{i}") for i in range(RING)] for l in range(2)]
        over_used = [sem(f"o{l}_used") for l in range(2)]

        def last_taken(eng, stage):
            end = GROUP0[stage] + len(dict(LIN)[stage]) - 1
            for w in "DA":
                n = TAKER[:end + 1].count(w)
                if n:
                    eng.wait_ge(taken[w], n)

        def wait_taken(eng, stage, j):
            g = GROUP0[stage] + j
            eng.wait_ge(taken[TAKER[g]], TAKEN[g])

        def streams(l):
            return LAYER_STREAMS[l] * T

        block = ctx.enter_context(nc.Block())

        @block.sync
        def _(sp):
            def strips(a, b):
                while a < b and a < RING:
                    sp.dma_start(ring[:, a % RING, :], stream[a]).then_inc(strip_in[a % RING], 16)
                    a += 1
                turns = (b - a) // RING
                if turns:
                    with sp.Fori(0, turns) as i:
                        for j in range(RING):
                            sp.wait_ge(strip_used, i * RING + (a + j - RING + 1))
                            sp.dma_start(ring[:, (a + j) % RING, :], stream[i * RING + (a + j)])\
                              .then_inc(strip_in[(a + j) % RING], 16)
                for s in range(a + turns * RING, b):
                    sp.wait_ge(strip_used, s - RING + 1)
                    sp.dma_start(ring[:, s % RING, :], stream[s]).then_inc(strip_in[s % RING], 16)

            def overflow(l):
                first = FIRST[f"moe{l}"]
                sp.wait_ge(flag_ready, l + 1)
                full = sp.value_load(FLAG[0:1, l:l + 1], min_val=0, max_val=1)
                with sp.If(full > 0):
                    sp.wait_ge(strip_used, first + 3 * EXPERTS)
                    for j in range(RING):
                        sp.dma_start(ring[:, (first + j) % RING, :], stream[first + j])\
                          .then_inc(over_in[l][j], 16)
                    n = 3 * EXPERTS // RING
                    with sp.Fori(1, n * (PASSES - 1)) as i:
                        for j in range(RING):
                            sp.wait_ge(over_used[l], i * RING + (j - RING + 1))
                            sp.dma_start(ring[:, (first + j) % RING, :], stream[(i % n) * RING + (first + j)])\
                              .then_inc(over_in[l][j], 16)
                    sp.wait_ge(over_used[l], 3 * EXPERTS * (PASSES - 1))

            strips(0, FIRST["odd"])
            overflow(0)
            strips(FIRST["odd"], FIRST["l0_na"])
            overflow(1)
            strips(FIRST["l0_na"], STRIPS)
            sp.wait_ge(norm_out, NOUT["ln2_1"] + KD)
            sp.dma_start(out, X[:, :, 0:T]).then_inc(out_sent, 16)
            sp.wait_ge(out_sent, 16)

        @block.tensor
        def _(pe):
            have = {}
            owed = [0]

            def strip(s):
                if s not in have:
                    pe.wait_ge(strip_in[s % RING], 16 * (s // RING + 1))
                    have[s] = ring[:, s % RING, :]
                return have[s]

            def tile(stage, n, width=1):
                v = strip(places(stage, "E")[n // TILES])
                at = n % TILES
                return v[:, at * P:(at + width) * P]

            def mm(o, w, x, start, stop, tells=False):
                m = pe.matmul(o, w, x, start=start, stop=stop)
                if owed[0] and not tells:
                    m.then_inc(strip_used, 1)
                    owed[0] -= 1
                return m

            def group(g):
                if g >= LIN_BANKS:
                    pe.wait_ge(taken[TAKER[g - LIN_BANKS]], TAKEN[g - LIN_BANKS])
                return bank[g % LIN_BANKS]

            def linear(stage, j, n, lhs, rhs, K, at=0, rows=P, wait=None):
                b = group(GROUP0[stage] + j)
                for k in range(K):
                    if wait:
                        wait(k)
                    m = mm(b[0:rows, at:at + n], lhs(k), rhs(k), k == 0, k == K - 1, tells=k == K - 1)
                m.then_inc(lin_ready, 1)

            def used():
                owed[0] += 1

            def reduce_mod(n):
                _, which, first, conds = MODS[n]
                pe.wait_ge(mod_summed, n + 1)
                used()
                for j in range(4):
                    col = (which * NMOD + first + j) * 2
                    for s in range(conds):
                        m = mm(bank[7][:, col + s:col + s + 1], macc(n, s)[:, j * P:(j + 1) * P], ones[:, 0:1],
                               True, True, tells=j == 3 and s == conds - 1)
                m.then_inc(mod_done, 1)

            def norm(name, w, mean=False):
                K, base = NCHUNK[name], NBASE[name]
                if mean:
                    pe.wait_ge(xsum_ready, NMEAN[name] + 1)
                    pe.matmul(bank[6][:, 0:w], ones, XSUM[:, 0:w], start=True, stop=True).then_inc(sum_ready, 1)
                for k in range(K):
                    pe.wait_ge(sq_ready, base + k + 1)
                    pe.matmul(bank[6][:, 0:w], ones, SQ[:, (base + k) % 2, 0:w], start=(k == 0), stop=(k == K - 1))\
                      .then_inc(sq_used, 1)

            def attention(name, q, k, v, PR, PT, bias=None):
                nb, u0 = ATT[name]
                b0 = u0 // HEADS
                for t in range(nb * HEADS + 5):
                    if t < nb * HEADS:
                        g, b, h = u0 + t, t // HEADS, t % HEADS
                        lo = 0 if b < TB else T
                        if g >= 3:
                            pe.wait_ge(at_p, g - 2)
                        s = bank[g % 3][:, 0:2 * T - lo]
                        masked = bias is not None and b < TB
                        m = mm(s, q(h, b), k(h, lo), True, not masked, tells=not masked)
                        if masked:
                            m = pe.matmul(s[:, 0:T], ident, bias(h, b), start=False, stop=True)
                        m.then_inc(at_s, 1)
                    if 0 <= t - 2 < nb * HEADS:
                        g, b = u0 + t - 2, (t - 2) // HEADS
                        kb = 4 if b < TB else 2
                        pe.wait_ge(at_pn, g + 1)
                        if g >= 2:
                            pe.wait_ge(at_ptc, g - 1)
                        for j in range(kb):
                            m = pe.transpose(bank[3 + g % 2][:, j * P:(j + 1) * P],
                                             PR[:, g % 3, j * P:(j + 1) * P], ident)
                        m.then_inc(at_t, 1)
                    if 0 <= t - 3 < nb * HEADS and (t - 3) % 2:
                        g, b, h = u0 + t - 3, (t - 3) // HEADS, (t - 3) % HEADS
                        kb, off = (4, 0) if b < TB else (2, 2)
                        pe.wait_ge(at_ptc, g + 1)
                        if h == 1 and b0 + b >= 2:
                            pe.wait_ge(at_y, b0 + b - 1)
                        for j in range(kb):
                            for e in range(2):
                                m = mm(bank[5 + b % 2][64 * e:64 * e + 64, (h // 2) * P:(h // 2 + 1) * P],
                                       v(off + j, h - 1 + e), PT[:, e, j * P:(j + 1) * P], j == 0, j == kb - 1,
                                       tells=j == kb - 1 and e == 1)
                        m.then_inc(at_pv, 1)

            pe.wait_ge(par_in, 16)
            pe.wait_ge(x_in, 16)
            for n in range(2):
                reduce_mod(n)
            norm("n1_0", 2 * T)
            for n in range(2, 4):
                reduce_mod(n)

            normed = lambda name: lambda k: pe.wait_ge(norm_out, NOUT[name] + k + 1)
            for j in range(4):
                linear("even_q", j, T, lambda k: tile("even", j * KD + k), lambda k: A[:, k, 0:T], KD,
                       wait=normed("n1_0") if j == 0 else None)
            used()
            for n in range(4, 7):
                reduce_mod(n)
            linear("even_k", 0, 2 * T, lambda k: tile("even", 32 + k), lambda k: A[:, k, :], KD)
            b = group(GROUP0["even_v"])
            for blk in range(4):
                for k in range(KD):
                    m = mm(b[:, blk * P:(blk + 1) * P], A[:, k, blk * P:(blk + 1) * P], tile("even", 40 + k),
                           k == 0, k == KD - 1, tells=blk == 3 and k == KD - 1)
            m.then_inc(lin_ready, 1)
            pe.wait_ge(taba_in, 16)
            for j in range(5):
                wait_taken(pe, "even_k" if j == 4 else "even_q", 0 if j == 4 else j)
                linear("even_rope", j, T, lambda k: tab(TA, "swap"), lambda k: QRAW[:, j, :], 1)
            for j in range(4):
                linear("even_u", j, T, lambda k: tile("even", 48 + j * KD + k), lambda k: A[:, k, 0:T], KD)
                if j == 1:
                    used()
                    for n in range(7, 10):
                        reduce_mod(n)
            for blk in range(TB):
                linear("even_z", blk, 512, lambda k: A[:, k, blk * P:(blk + 1) * P],
                       lambda k: tile("even", 80 + 4 * k, 4), KD)
            used()
            for n in range(10, EVEN_OUT_MOD):
                reduce_mod(n)
            used()
            pe.wait_ge(wsp_in, 16)
            for n in range(TB):
                pe.wait_ge(z_norm, n + 1)
                b = group(GROUP0["even_gate"] + n)
                for h in range(HEADS):
                    r = 64 * (h % 2)
                    m = mm(b[r:r + 64, (h // 2) * P:(h // 2 + 1) * P], Z1[:, n, h * 64:(h + 1) * 64], WSP[:, h, :],
                           True, True, tells=h == HEADS - 1)
                m.then_inc(lin_ready, 1)
            last_taken(pe, "even_gate")
            pe.wait_ge(rope_done, 5)

            attention("even",
                      lambda h, b: QK[64 * (h // 4):64 * (h // 4) + 64, h % 4, b * P:(b + 1) * P],
                      lambda h, lo: KV_K[64 * (h // 4):64 * (h // 4) + 64, lo:2 * T],
                      lambda kb, h: V1[:, kb, 64 * (h // 4):64 * (h // 4) + 64],
                      PR1, PT1, bias=lambda h, b: tab(TA, "mask", b * T, T))
            pe.wait_ge(at_y, 2)
            pe.wait_ge(sg_ready, TB * 4)
            for j in range(KD):
                linear("even_out", j, T, lambda k: tile("even_out", j * KD + k), lambda k: CAT[:, k, :], KD)
                if j % 4 == 3:
                    used()
            for n in range(EVEN_OUT_MOD, ODD_MOD):
                reduce_mod(n)
            def gather(q):
                for c in range(KD):
                    b = bank[2 + c // 4]
                    for blk in range(TB):
                        m = mm(b[:, (c % 4) * P:(c % 4 + 1) * P], HT[:, blk, c * P:(c + 1) * P], GE[:, blk, :],
                               blk == 0, blk == TB - 1, tells=c == KD - 1 and blk == TB - 1)
                m.then_inc(q["gath_ready"], 1)

            def combine(q, p, i, product):
                pe.wait_ge(q["y_copied"], i + (17 * p + 1))
                pe.wait_ge(q["spt_ready"], i + (17 * p + 1))
                for r in range(4):
                    pe.wait_ge(q["res_added"], i * 4 + (70 * p + r + 1))
                    for h in range(2):
                        c = 2 * r + h
                        m = product(bank[6 + r % 2][:, h * T:(h + 1) * T], YP[:, c * P:(c + 1) * P], SPT[:, :],
                                    True, True, tells=h == 1)
                    m.then_inc(q["comb_ready"], 1)

            def moe_pass(q, p, first, came, used_sem):
                pe.wait_ge(q["ge_ready"], 17 * p + 1)
                gather(q)
                with pe.Fori(0, PAIRS) as i:
                    slot = [ring[:, (first + j) % RING, :] for j in range(RING)]
                    due = [0]

                    def pe_mm(o, w, x, start, stop, tells):
                        m = pe.matmul(o, w, x, start=start, stop=stop)
                        if due[0] and not tells:
                            m.then_inc(used_sem, 1)
                            due[0] -= 1
                        return m

                    def both_up(half, ready):
                        for e in range(2):
                            came(i, 2 * half + e)
                        for k in range(KD):
                            for e in range(2):
                                m = pe_mm(bank[half][e * C:(e + 1) * C, :], XG[:, k, e * C:(e + 1) * C],
                                          slot[2 * half + e][:, k * HID:(k + 1) * HID], k == 0, k == KD - 1,
                                          tells=k == KD - 1 and e == 1)
                        m.then_inc(q[ready], 1)
                        due[0] += 2

                    pe.wait_ge(q["xg_ready"], i + (17 * p + 1))
                    both_up(0, "gate_ready")
                    both_up(1, "up_ready")
                    combine(q, p, i, pe_mm)
                    pe.wait_ge(q["hid_ready"], i + (16 * p + 1))
                    for c in range(4):
                        m = pe.transpose(bank[0][:, c * P:(c + 1) * P], HTOK[:, c * P:(c + 1) * P], ident)
                    m.then_inc(q["htr_ready"], 1)
                    pe.wait_ge(q["ge_ready"], i + (17 * p + 2))
                    gather(q)
                    for e in range(2):
                        came(i, 4 + e)
                    pe.wait_ge(q["he_ready"], i + (16 * p + 1))
                    for h in range(2):
                        for k in range(4):
                            for e in range(2):
                                m = pe_mm(bank[4 + h][e * C:(e + 1) * C, :], HE[:, k, e * C:(e + 1) * C],
                                          slot[4 + e][:, k * D + h * 512:k * D + (h + 1) * 512], k == 0, k == 3,
                                          tells=h == 1 and k == 3 and e == 1)
                    m.then_inc(q["y_ready"], 1)
                    pe.wait_ge(q["gw_ready"], i + (17 * p + 1))
                    pe.wait_ge(q["res_added"], i * 4 + (70 * p + 6))
                    pe.transpose(bank[6][:, 0:P], GW[:, 0, :], ident).then_inc(used_sem, 2)
                    pe.transpose(bank[6][:, P:2 * P], GW[:, 1, :], ident).then_inc(q["tr_ready"], 1)
                combine(q, p, PAIRS, lambda o, w, x, a, b, tells: pe.matmul(o, w, x, start=a, stop=b))

            def moe(l):
                b = group(GROUP0[f"route{l}"])
                for blk in range(TB):
                    for k in range(KD):
                        if blk == 0:
                            pe.wait_ge(norm_out, NOUT[f"n2_{l}"] + k + 1)
                        m = mm(b[:, blk * ROUTES:(blk + 1) * ROUTES], A[:, k, blk * P:(blk + 1) * P],
                               tab(TA, "router", (l * KD + k) * ROUTES, ROUTES), k == 0, k == KD - 1, tells=blk == 1 and k == KD - 1)
                m.then_inc(lin_ready, 1)
                for j in range(4):
                    b = group(GROUP0[f"turn{l}"] + j)
                    for c in range(4):
                        cc = (j % 2) * 4 + c
                        m = pe.transpose(b[:, c * P:(c + 1) * P], A[:, cc, (j // 2) * P:(j // 2 + 1) * P], ident)
                        if owed[0] and c < 3:
                            m.then_inc(strip_used, 1)
                            owed[0] -= 1
                    m.then_inc(lin_ready, 1)
                b = group(GROUP0[f"rank{l}"])
                pe.wait_ge(rt_mask, l + 1)
                mm(b[:, 0:32], before, MM[:, 0, 0:32], True, True)
                mm(b[:, 32:64], ones, MM[:, 0, 0:32], True, False)
                mm(b[:, 32:64], before, MM[:, 1, 0:32], False, True)
                mm(b[:, 64:96], ones, MM[:, 0, 0:32], True, False)
                mm(b[:, 64:96], ones, MM[:, 1, 0:32], False, True, tells=True).then_inc(lin_ready, 1)
                last_taken(pe, f"rank{l}")
                assert not owed[0]
                first = FIRST[f"moe{l}"]

                def came(i, j):
                    s = first + j
                    pe.wait_ge(strip_in[s % RING], i * 16 + 16 * (s // RING + 1))

                moe_pass(main, l, first, came, strip_used)
                full = pe.value_load(FLAG[0:1, l:l + 1], min_val=0, max_val=1)
                with pe.If(full > 0):
                    with pe.Fori(0, PASSES - 1) as p:
                        moe_pass(over[l], p, first,
                                 lambda i, j: pe.wait_ge(over_in[l][j], p * (16 * PAIRS) + i * 16 + 16), over_used[l])
                    pe.wait_ge(over[l]["res_added"], 70 * (PASSES - 1))
                pe.wait_ge(main["res_added"], 70 * (l + 1))

            norm("n2_0", T)
            pe.wait_ge(mod_taken, 4)
            moe(0)

            norm("n1_1", T)

            for j in range(3 * KD):
                linear("odd_in", j, T, lambda k: tile("odd", j * KD + k), lambda k: A[:, k, 0:T], KD,
                       wait=normed("n1_1") if j == 0 else None)
                if j % 4 == 3:
                    used()
                    for n in range(*ODD_REDUCE[j // 4]):
                        reduce_mod(n)
            pe.wait_ge(cv_ready, KD)
            for j in range(KD):
                linear("odd_out", j, T, lambda k: tile("odd", 192 + j * KD + k), lambda k: CV[:, k, :], KD)
                if j % 4 == 3:
                    used()
                    for n in range(*ODD_REDUCE[6 + j // 4]):
                        reduce_mod(n)
            norm("n2_1", T)
            pe.wait_ge(mod_taken, 6)
            moe(1)
            norm("final", T)

            pe.wait_ge(ctx2_in, 16)
            pe.wait_ge(tabb_in, 16)
            pe.wait_ge(mid_ready, NMID["final"] + KD)
            norm("ln_in", 2 * T, mean=True)
            for l in range(2):
                w = streams(l)
                modulated = lambda n: lambda k: pe.wait_ge(a_ready, KD * (2 * l + n) + k + 1)
                st = f"l{l}_na"
                for blk in range(w // P):
                    linear(f"f{l}", blk, 512, lambda k: A[:, k, blk * P:(blk + 1) * P], lambda k: tile(st, 4 * k, 4), KD,
                           wait=modulated(0) if blk == 0 else None)
                used()
                for s in range(w // T):
                    for g in range(4):
                        for blk in range(TB):
                            wait_taken(pe, f"f{l}", s * TB + blk)
                        linear(f"dft{l}", s * 4 + g, 2 * T, lambda k: FT[:, s * TB + k, g * P:(g + 1) * P],
                               lambda k: tab(TC, "dft", k * 2 * T, 2 * T), TB)
                for j in range(4 * w // T):
                    wait_taken(pe, f"dft{l}", j)
                    linear(f"idft{l}", j, T, lambda k: tab(TC, "cd" if k == 0 else "sd"),
                           lambda k: FU[:, j, k * T:(k + 1) * T], 2)
                last_taken(pe, f"idft{l}")
                for j in range(4):
                    linear(f"nq{l}", j, w, lambda k: tile(st, 32 + j * KD + k), lambda k: A[:, k, 0:w], KD)
                used()
                for j in range(4):
                    linear(f"nk{l}", j, 2 * T, lambda k: tile(st, 64 + j * KD + k), lambda k: A[:, k, :], KD)
                used()
                for blk in range(4):
                    linear(f"nv{l}", blk, 512, lambda k: A[:, k, blk * P:(blk + 1) * P],
                           lambda k: tile(st, 96 + 4 * k, 4), KD)
                used()
                last_taken(pe, f"nv{l}")
                bs = strip(FIRST[f"l{l}_bias"])
                attention(f"na{l}",
                          lambda h, b: NQ[64 * (h % 2):64 * (h % 2) + 64, h // 2, b * P:(b + 1) * P],
                          lambda h, lo: NK[64 * (h % 2):64 * (h % 2) + 64, h // 2, lo:2 * T],
                          lambda kb, h: V2[:, kb, h * 64:(h + 1) * 64], PR2, PT2,
                          bias=lambda h, b: bs[:, (h * TB + b) * T:(h * TB + b + 1) * T])
                used()
                st = f"l{l}_low"
                for j in range(4):
                    n = w if j < 2 else 2 * T
                    linear(f"low{l}", j, n, lambda k: tile(st, j * KD + k), lambda k: A[:, k, 0:n], KD)
                used()
                pe.wait_ge(at_y, (ATT[f"na{l}"][1] // HEADS) + ATT[f"na{l}"][0])
                norm(f"cq{l}", w)
                norm(f"ckv{l}", 2 * T)
                wait_taken(pe, f"low{l}", 3)
                linear(f"krope{l}", 0, T, lambda k: tab(TC, "swap"), lambda k: LOW[:, 3, 0:T], 1)
                pe.wait_ge(mid_ready, NMID[f"ckv{l}"] + 1)
                st = f"l{l}_up"
                for j in range(8):
                    linear(f"mq{l}", j, w, lambda k: tile(st, 2 * j + k), lambda k: LOW[:, k, 0:w], 2)
                for j in range(8):
                    linear(f"mk{l}", j, 2 * T, lambda k: tile(st, 16 + j), lambda k: LOW[:, 2, :], 1)
                for blk in range(4):
                    linear(f"mv{l}", blk, 512, lambda k: LOW[:, 2, blk * P:(blk + 1) * P], lambda k: tile(st, 24, 4), 1)
                used()
                for j in range(8):
                    wait_taken(pe, f"mq{l}", j)
                    linear(f"qrope{l}", j, T, lambda k: tab(TC, "swap"), lambda k: A[:, j, 0:T], 1)
                last_taken(pe, f"qrope{l}")
                pe.wait_ge(rope_done, 5 + 9 * (l + 1))
                pe.wait_ge(kr_copied, 8 * (l + 1))
                attention(f"mla{l}",
                          lambda h, b: A[0:MLA_ROWS, h, b * P:(b + 1) * P],
                          lambda h, lo: MK[0:MLA_ROWS, h, lo:2 * T],
                          lambda kb, h: V2[:, kb, h * 64:(h + 1) * 64], PR2, PT2)
                pe.wait_ge(at_y, (ATT[f"mla{l}"][1] // HEADS) + ATT[f"mla{l}"][0])
                st = f"l{l}_merge"
                for o in range(KD):
                    for b in range(3):
                        at = (o * 3 + b) * 12
                        j = (o * 3 + b) * 2
                        linear(f"merge{l}", j, w, lambda k: tile(st, at + k), lambda k: A[:, k, 0:w], KD,
                               wait=(lambda k: pe.wait_ge(a_again, KD * l + k + 1)) if j == 0 else None)
                        linear(f"merge{l}", j + 1, w, lambda k: tile(st, at + KD + k), lambda k: YB[b][:, k, 0:w], 4)
                        if (at + 12) // TILES > at // TILES:
                            used()
                            if l == 0 and at // TILES < 8:
                                reduce_mod(MERGE_MOD + at // TILES)
                wait_taken(pe, f"merge{l}", 6 * KD - 1)
                for j in range(KD):
                    linear(f"out{l}", j, w, lambda k: tile(f"l{l}_out", j * KD + k), lambda k: MG[:, k, 0:w], KD)
                    if j % 4 == 3:
                        used()
                wait_taken(pe, f"out{l}", KD - 1)
                norm(f"ln1_{l}", w, mean=True)
                st = f"l{l}_ffn"
                for j in range(2 * KF):
                    linear(f"up{l}", j, w, lambda k: tile(st, j * KD + k), lambda k: A[:, k, 0:w], KD,
                           wait=modulated(1) if j == 0 else None)
                    if j % 4 == 3:
                        used()
                        if l == 0:
                            reduce_mod(FFN_MOD + j // 4)
                wait_taken(pe, f"up{l}", 2 * KF - 1)
                for j in range(KD):
                    at = 2 * KF * KD + j * KF
                    linear(f"down{l}", j, w, lambda k: tile(st, at + k), lambda k: HB[:, k, 0:w], KF)
                    if (at + KF) // TILES > at // TILES:
                        used()
                        if l == 0 and j == 1:
                            reduce_mod(FFN_MOD + 11)
                used()
                wait_taken(pe, f"down{l}", KD - 1)
                norm(f"ln2_{l}", w, mean=True)

        @block.scalar
        def _(act):
            act.dma_start(par_sb[:, :], par).then_inc(par_in, 16)
            act.dma_start(X[:, :, :], xt).then_inc(x_in, 16)
            act.dma_start(tab_sb[:, 0:N_TA], tab_a).then_inc(taba_in, 16)
            act.dma_start(WSP, wsp_d).then_inc(wsp_in, 16)

            def take(stage, j, n, rows=P):
                g = GROUP0[stage] + j
                act.wait_ge(lin_ready, g + 1)
                return bank[g % LIN_BANKS][0:rows, 0:n]

            def squares(name, w, x, mean=False, come=None):
                base, dim, eps = NBASE[name], NCHUNK[name] * P, 0 if name[:2] in ("n1", "n2", "fi") else 1
                act.activation(OPEN[:, :], EPS[:, 0:1], ACT.Sqrt)
                for k in range(NCHUNK[name]):
                    if come:
                        come(k)
                    if mean:
                        act.wait_ge(xc_ready, NXC[name] + k + 1)
                    if base + k >= 2:
                        act.wait_ge(sq_used, base + k - 1)
                    act.activation(SQ[:, (base + k) % 2, 0:w], x(k), ACT.Square).then_inc(sq_ready, 1)
                act.wait_ge(sq_used, base + NCHUNK[name])
                act.activation(RSTD[:, 0:w], bank[6][:, 0:w], ACT.Sqrt, bias=EPS[:, eps:eps + 1], scale=1.0 / dim)\
                   .then_inc(std_ready, 1)

            def shifts(name, out_, halves):
                for k in range(KD):
                    act.wait_ge(mid_ready, NMID[name] + k + 1)
                    for lo, hi, b in halves:
                        m = act.activation(out_(k)[:, lo:hi], out_(k)[:, lo:hi], ACT.Identity, bias=b(k))
                    m.then_inc(norm_out, 1)

            def norm(name, w, shift, come=None):
                squares(name, w, lambda k: X[:, k, 0:w], come=come)
                shifts(name, lambda k: A[:, k, 0:w], [(0, w, shift)])

            def layer_norm(name, w):
                squares(name, w, lambda k: X[:, k, 0:w], mean=True)
                for k in range(KD):
                    act.wait_ge(mid_ready, NMID[name] + k + 1)
                    for s in range(w // T):
                        m = act.activation(A[:, k, s * T:(s + 1) * T], X[:, k, s * T:(s + 1) * T], ACT.Identity,
                                           bias=FB[:, k, s:s + 1], scale=FG[:, k, s:s + 1])
                    m.then_inc(a_ready, 1)

            def attention(name, scale, PR, PT, sink=False):
                nb, u0 = ATT[name]

                def turned(u):
                    if 0 <= u < nb * HEADS:
                        g, n = u0 + u, 2 * T if u // HEADS < TB else T
                        act.wait_ge(at_t, g + 1)
                        if g >= 2:
                            act.wait_ge(at_pv, g // 2)
                        act.activation(PT[:, g % 2, 0:n], bank[3 + g % 2][:, 0:n], ACT.Copy).then_inc(at_ptc, 1)

                for t in range(nb * HEADS + 4):
                    if t % 2:
                        turned(t - 2)
                    if t < nb * HEADS:
                        g, b, h = u0 + t, t // HEADS, t % HEADS
                        n = 2 * T if b < TB else T
                        pb = (u0 // HEADS + b) % 2
                        act.wait_ge(at_nm, g + 1)
                        if g >= 3:
                            act.wait_ge(at_t, g - 2)
                        act.activation(PR[:, g % 3, 0:n], bank[g % 3][:, 0:n], ACT.Exp, bias=NM[:, pb, h:h + 1],
                                       scale=scale, accum_out=SM[:, pb, h:h + 1]).then_inc(at_p, 1)
                        if sink:
                            act.activation(ES[:, pb, h:h + 1], par_("sink", h, 1), ACT.Exp, bias=NM[:, pb, h:h + 1])\
                               .then_inc(at_es, 1)
                    if t % 2 == 0:
                        turned(t - 2)

            act.wait_ge(par_in, 16)
            for i, name in enumerate(("c", "c_2")):
                m = act.activation(SILC[:, i, :, :].rearrange("p a b -> p (a b)"), par_(name), ACT.Silu)
            m.then_inc(silc_ready, 1)
            act.wait_ge(x_in, 16)
            act.wait_ge(eps_ready, 1)
            mod = lambda which, first, k, s: MOD[:, which, first + k, s:s + 1]
            squares("n1_0", 2 * T, lambda k: X[:, k, :])
            shifts("n1_0", lambda k: A[:, k, :], [(0, T, lambda k: mod(0, 0, k, 0)), (T, 2 * T, lambda k: mod(0, 0, k, 1))])
            for j in range(4):
                act.activation(U1[:, j, :], take("even_u", j, T), ACT.Gelu).then_inc(taken["A"], 1)
            for blk in range(TB):
                act.activation(Z1[:, blk, :], take("even_z", blk, 512), ACT.Gelu).then_inc(taken["A"], 1)
            for n in range(TB):
                act.wait_ge(z_var, n + 1)
                act.activation(BN[:, n, 8:9], BN[:, n, 7:8], ACT.Sqrt, bias=EPS[:, 0:1]).then_inc(z_std, 1)
            attention("even", 1.0, PR1, PT1, sink=True)

            def moe_pass(q, p):
                act.activation(OPEN[:, :], ident[:, 0:1], ACT.Copy).then_inc(q["y_copied"], 1)

                def rows(i):
                    act.wait_ge(q["gath_ready"], i + (17 * p + 1))
                    for h in range(2):
                        m = act.activation(XG[:, 4 * h:4 * h + 4, :].rearrange("p a b -> p (a b)"), bank[2 + h][:, :],
                                           ACT.Copy)
                    m.then_inc(q["xg_ready"], 1)

                rows(0)
                with act.Fori(0, PAIRS) as i:
                    act.wait_ge(q["gate_ready"], i + (16 * p + 1))
                    act.activation(SIL[:, :], bank[0][:, :], ACT.Silu).then_inc(q["sil_ready"], 1)
                    act.wait_ge(q["htr_ready"], i + (16 * p + 1))
                    act.activation(HE.rearrange("p a b -> p (a b)"), bank[0][:, :], ACT.Copy).then_inc(q["he_ready"], 1)
                    rows(i + 1)
                    act.wait_ge(q["y_ready"], i + (16 * p + 1))
                    for h in range(2):
                        m = act.activation(YP[:, h * 512:(h + 1) * 512], bank[4 + h][:, :], ACT.Copy)
                    m.then_inc(q["y_copied"], 1)

            def moe(l):
                for j in range(4):
                    act.activation(HT[:, j // 2, (j % 2) * 512:(j % 2) * 512 + 512], take(f"turn{l}", j, 512), ACT.Copy)\
                       .then_inc(taken["A"], 1)
                act.wait_ge(rt_exp_in, l + 1)
                for b in range(TB):
                    act.activation(SML[:, b, 8:12], LG[:, b, 0:4], ACT.Exp, bias=SML[:, b, 0:1], accum_out=SML[:, b, 1:2])
                    m = act.activation(SML[:, b, 3:4], SML[:, b, 2:3], ACT.Exp)
                m.then_inc(rt_exp, 1)
                if l == 1:
                    act.wait_ge(lin_ready, GROUP0["route1"] + 1)
                    act.wait_ge(flag_ready, 2)
                    act.dma_start(tab_sb[:, 0:N_TC], tab_b).then_inc(tabb_in, 16)
                    act.dma_start(X[:, :, T:2 * T], ctx2t).then_inc(ctx2_in, 16)
                moe_pass(main, l)
                act.wait_ge(flag_ready, l + 1)
                full = act.value_load(FLAG[0:1, l:l + 1], min_val=0, max_val=1)
                with act.If(full > 0):
                    with act.Fori(0, PASSES - 1) as p:
                        moe_pass(over[l], p)
                    act.wait_ge(over[l]["res_added"], 70 * (PASSES - 1))
                act.wait_ge(main["res_added"], 70 * (l + 1))

            norm("n2_0", T, lambda k: mod(0, 24, k, 0), come=lambda k: wait_taken(act, "even_out", k))
            moe(0)
            norm("n1_1", T, lambda k: mod(1, 0, k, 0))
            for c in range(KD):
                if c >= 2:
                    act.wait_ge(cv_ready, c - 1)
                act.activation(BG[:, c % 2, :], take("odd_in", 3 * c, T), ACT.Copy).then_inc(taken["A"], 1)
                act.activation(CG[:, c % 2, :], take("odd_in", 3 * c + 1, T), ACT.Copy).then_inc(taken["A"], 1)
            norm("n2_1", T, lambda k: mod(1, 24, k, 0), come=lambda k: wait_taken(act, "odd_out", k))
            moe(1)
            squares("final", T, lambda k: X[:, k, 0:T])

            act.wait_ge(ctx2_in, 16)
            layer_norm("ln_in", 2 * T)
            for l in range(2):
                w = streams(l)
                for j in range(4 * w // T):
                    act.activation(FU[:, j, :], take(f"dft{l}", j, 512), ACT.Copy).then_inc(taken["A"], 1)
                last_taken(act, f"idft{l}")
                for j in range(4):
                    act.activation(NK[:, j, :], take(f"nk{l}", j, 512), ACT.Copy).then_inc(taken["A"], 1)
                for j in range(4):
                    act.activation(V2[:, j, :], take(f"nv{l}", j, 512), ACT.Copy).then_inc(taken["A"], 1)
                attention(f"na{l}", 1.0, PR2, PT2)
                for j in range(2):
                    wait_taken(act, f"low{l}", j)
                squares(f"cq{l}", w, lambda k: LOW[:, k, 0:w])
                wait_taken(act, f"low{l}", 2)
                act.wait_ge(mid_ready, NMID[f"cq{l}"] + 2)
                squares(f"ckv{l}", 2 * T, lambda k: LOW[:, 2, :])
                for j in range(8):
                    act.activation(A[:, j, 0:w], take(f"mq{l}", j, w), ACT.Copy).then_inc(taken["A"], 1)
                for j in range(8):
                    act.activation(MK[0:64, j, :], take(f"mk{l}", j, 512, 64), ACT.Copy).then_inc(taken["A"], 1)
                attention(f"mla{l}", MLA_SCALE, PR2, PT2)
                act.wait_ge(at_y, (ATT[f"mla{l}"][1] // HEADS) + ATT[f"mla{l}"][0])
                for j in range(3 * KD):
                    if j >= 2:
                        wait_taken(act, f"merge{l}", 2 * (j - 2) + 1)
                    act.activation(SG[:, j % 2, 0:w], take(f"merge{l}", 2 * j, w), ACT.Sigmoid).then_inc(taken["A"], 1)
                layer_norm(f"ln1_{l}", w)
                for j in range(KF):
                    if j >= 2:
                        wait_taken(act, f"up{l}", 2 * (j - 2) + 1)
                    act.activation(SB_[:, j % 2, 0:w], take(f"up{l}", 2 * j, w), ACT.Silu).then_inc(taken["A"], 1)
                if l == 0:
                    layer_norm("ln2_0", w)
                else:
                    squares("ln2_1", w, lambda k: X[:, k, 0:w], mean=True)
                    shifts("ln2_1", lambda k: X[:, k, 0:w], [(0, w, lambda k: par_("ln2_b", KD + k, 1))])

        @block.vector
        def _(dve):
            own = [0]

            def link(ins):
                own[0] += 1
                ins.then_inc(dve_own, 1)
                dve.wait_ge(dve_own, own[0])

            def take(stage, j, n=None, rows=None):
                g = GROUP0[stage] + j
                dve.wait_ge(lin_ready, g + 1)
                b = bank[g % LIN_BANKS]
                return b[:, 0:n] if n else b

            def root(name, w):
                dve.wait_ge(std_ready, NSTAT[name] + 1)
                link(dve.reciprocal(RSTD[:, 0:w], RSTD[:, 0:w]))

            def norm(name, w, x, out_, halves):
                root(name, w)
                for k in range(NCHUNK[name]):
                    for lo, hi, s in halves:
                        m = dve.scalar_tensor_tensor(out_(k)[:, lo:hi], x(k)[:, lo:hi], s(k), RSTD[:, lo:hi],
                                                     ALU.mult, ALU.mult)
                    m.then_inc(mid_ready, 1)

            def center(name, w):
                dve.wait_ge(sum_ready, NMEAN[name] + 1)
                link(dve.tensor_scalar(MEAN[:, 0:w], bank[6][:, 0:w], 1.0 / D, None, ALU.mult))
                for k in range(KD):
                    dve.tensor_tensor(X[:, k, 0:w], X[:, k, 0:w], MEAN[:, 0:w], ALU.subtract).then_inc(xc_ready, 1)

            done_x = [0]

            def layer_norm(name, w, g, b, l, shift, scale):
                center(name, w)
                for s in range(w // T):
                    one = MODP[:, l, scale:scale + KD, s]
                    dve.tensor_tensor(FG[:, :, s], one, par_(*g), ALU.mult)
                    link(dve.tensor_tensor(FB[:, :, s], one, par_(*b), ALU.mult))
                    link(dve.tensor_tensor(FB[:, :, s], FB[:, :, s], MOD[:, 2 + l, shift:shift + KD, s], ALU.add))
                dve.wait_ge(xc_ready, NXC[name] + KD)
                root(name, w)
                for k in range(KD):
                    dve.tensor_tensor(X[:, k, 0:w], X[:, k, 0:w], RSTD[:, 0:w], ALU.mult).then_inc(mid_ready, 1)
                for k in range(KD):
                    dve.wait_ge(a_ready, done_x[0] + k + 1)
                    dve.tensor_scalar(X[:, k, 0:w], X[:, k, 0:w], par_(g[0], g[1] + k, 1), par_(b[0], b[1] + k, 1),
                                      ALU.mult, ALU.add).then_inc(x_done, 1)
                done_x[0] += KD
                dve.wait_ge(x_done, done_x[0])

            summed = [0]

            def sum_up(k, w):
                if k:
                    if k > 1:
                        dve.wait_ge(xsum_step, summed[0])
                    m = dve.tensor_tensor(XSUM[:, 0:w], X[:, 0, 0:w] if k == 1 else XSUM[:, 0:w], X[:, k, 0:w], ALU.add)
                    if k == KD - 1:
                        m.then_inc(xsum_ready, 1)
                    else:
                        m.then_inc(xsum_step, 1)
                        summed[0] += 1

            def attention(name, scale, PR, y, sink=False):
                nb, u0 = ATT[name]
                for t in range(nb * HEADS + 5):
                    if t < nb * HEADS:
                        g, b, h = u0 + t, t // HEADS, t % HEADS
                        n = 2 * T if b < TB else T
                        pb = (u0 // HEADS + b) % 2
                        dve.wait_ge(at_s, g + 1)
                        link(dve.reduce_max(MX[:, pb, h:h + 1], bank[g % 3][:, 0:n], AXX))
                        if sink:
                            i = dve.tensor_scalar(NM[:, pb, h:h + 1], MX[:, pb, h:h + 1], par_("sink", h, 1), -1.0,
                                                  ALU.max, ALU.mult)
                        else:
                            i = dve.tensor_scalar(NM[:, pb, h:h + 1], MX[:, pb, h:h + 1], -scale, None, ALU.mult)
                        i.then_inc(at_nm, 1)
                    if 0 <= t - 1 < nb * HEADS:
                        g, b, h = u0 + t - 1, (t - 1) // HEADS, (t - 1) % HEADS
                        n = 2 * T if b < TB else T
                        pb = (u0 // HEADS + b) % 2
                        total = SM[:, pb, h:h + 1]
                        dve.wait_ge(at_p, g + 1)
                        if sink:
                            dve.wait_ge(at_es, g + 1)
                            link(dve.tensor_tensor(total, total, ES[:, pb, h:h + 1], ALU.add))
                        link(dve.reciprocal(total, total))
                        dve.tensor_scalar(PR[:, g % 3, 0:n], PR[:, g % 3, 0:n], total, None, ALU.mult).then_inc(at_pn, 1)
                    if t >= 4 and (t - 4) % HEADS == HEADS - 1:
                        b = (t - 4) // HEADS
                        dve.wait_ge(at_pv, (u0 // HEADS + b + 1) * HEADS // 2)
                        dve.tensor_copy(y(b), bank[5 + b % 2][:, :].rearrange("p (c n) -> p c n", c=4)).then_inc(at_y, 1)

            steps = [0]

            def mod_strip(n):
                st, which, _, conds = MODS[n]
                dve.wait_ge(strip_in[st % RING], 16 * (st // RING + 1))
                if mod_rows(n)[1]:
                    dve.wait_ge(mod_done, mod_rows(n)[1])
                for k in range(KD):
                    W = ring[:, st % RING, k * 512:(k + 1) * 512]
                    for s in range(conds):
                        c = SILC[:, which // 2, k, s:s + 1]
                        if k:
                            dve.wait_ge(mod_step, steps[0] - conds + 1)
                            m = dve.scalar_tensor_tensor(macc(n, s), W, c, macc(n, s), ALU.mult, ALU.add)
                        else:
                            m = dve.tensor_scalar(macc(n, s), W, c, None, ALU.mult)
                        if k == KD - 1 and s == conds - 1:
                            m.then_inc(mod_summed, 1)
                        else:
                            m.then_inc(mod_step, 1)
                            steps[0] += 1

            mods_taken = [0]

            def take_mods(which, a, b, conds, done):
                dve.wait_ge(mod_done, done)
                at, end = (which * NMOD + a) * 2, (which * NMOD + b) * 2
                pairs = lambda v: v.rearrange("p (a b) -> p a b", b=2)[:, :, 0:conds]
                dve.tensor_tensor(MOD[:, which, a:b, 0:conds], pairs(bank[7][:, at:end]),
                                  pairs(par_("bias", at, end - at)), ALU.add).then_inc(mod_taken, 1)
                mods_taken[0] += 1
                dve.wait_ge(mod_taken, mods_taken[0])

            def plus_one(l, a, b, conds=2):
                link(dve.tensor_scalar(MODP[:, l, a:b, 0:conds], MOD[:, 2 + l, a:b, 0:conds], 1.0, None, ALU.add))

            def gain(slot, which, first, s, g):
                return dve.scalar_tensor_tensor(GSC[:, slot, :], MOD[:, which, first:first + KD, s], 1.0, g, ALU.add, ALU.mult)

            def residual(stage, j, n, gate):
                dve.scalar_tensor_tensor(X[:, j, 0:n], take(stage, j, n), gate, X[:, j, 0:n], ALU.mult, ALU.add)\
                   .then_inc(taken["D"], 1)

            dve.memset(EPS[:, 0:1], EPS1)
            dve.memset(EPS[:, 1:2], EPS2).then_inc(eps_ready, 1)
            dve.wait_ge(par_in, 16)
            dve.wait_ge(silc_ready, 1)
            for n in range(4):
                mod_strip(n)
            dve.wait_ge(x_in, 16)
            take_mods(0, 0, 16, 2, 4)
            gain(0, 0, 8, 0, par_("g1", 0, KD))
            link(gain(1, 0, 8, 1, par_("g1", 0, KD)))
            norm("n1_0", 2 * T, lambda k: X[:, k, :], lambda k: A[:, k, :],
                 [(0, T, lambda k: GSC[:, 0, k:k + 1]), (T, 2 * T, lambda k: GSC[:, 1, k:k + 1])])
            for j in range(4):
                if j < 3:
                    mod_strip(4 + j)
                dve.tensor_scalar(QRAW[:, j, :], take("even_q", j, T), 0.125, None, ALU.mult).then_inc(taken["D"], 1)
            dve.tensor_copy(QRAW[:, 4, :], take("even_k", 0)[:, 0:T])
            dve.tensor_copy(KV_K[:, T:2 * T], take("even_k", 0)[:, T:2 * T]).then_inc(taken["D"], 1)
            dve.tensor_copy(V1.rearrange("p a b -> p (a b)"), take("even_v", 0)[:, :]).then_inc(taken["D"], 1)
            wait_taken(dve, "even_v", 0)
            dve.wait_ge(taba_in, 16)
            for j in range(5):
                o = QK[:, j, :] if j < 4 else KV_K[:, 0:T]
                dve.tensor_tensor(TMP1[:, j % 2, :], take("even_rope", j, T), tab(TA, "sin"), ALU.mult).then_inc(taken["D"], 1)
                link(dve.tensor_tensor(QK[:, j, :], QRAW[:, j, :], tab(TA, "cos"), ALU.mult))
                dve.tensor_tensor(o, QK[:, j, :], TMP1[:, j % 2, :], ALU.add).then_inc(rope_done, 1)
            for n in range(7, EVEN_OUT_MOD):
                mod_strip(n)
            for n in range(TB):
                wait_taken(dve, "even_z", n)
                link(dve.bn_stats(BN[:, n, 0:6], Z1[:, n, :]))
                dve.bn_aggr(BN[:, n, 6:8], BN[:, n, 0:6]).then_inc(z_var, 1)
            for n in range(TB):
                dve.wait_ge(z_std, n + 1)
                link(dve.reciprocal(BN[:, n, 9:10], BN[:, n, 8:9]))
                dve.tensor_scalar(Z1[:, n, :], Z1[:, n, :], BN[:, n, 6:7], BN[:, n, 9:10], ALU.subtract, ALU.mult)\
                   .then_inc(z_norm, 1)
            dve.wait_ge(taken["A"], TAKEN[GROUP0["even_u"] + 3])
            for n in range(TB):
                b = take("even_gate", n)
                for c in range(4):
                    i = dve.scalar_tensor_tensor(CAT[:, 4 + c, n * P:(n + 1) * P], b[:, c * P:(c + 1) * P],
                                                 par_("sgu", c, 1), tab(TA, "bsp", c * P, P), ALU.mult, ALU.add)
                i.then_inc(taken["D"], 1)
                dve.wait_ge(taken["D"], TAKEN[GROUP0["even_gate"] + n])
                for c in range(4):
                    dve.tensor_tensor(CAT[:, 4 + c, n * P:(n + 1) * P], CAT[:, 4 + c, n * P:(n + 1) * P],
                                      U1[:, c, n * P:(n + 1) * P], ALU.mult).then_inc(sg_ready, 1)
            attention("even", 1.0, PR1, lambda b: CAT[:, 0:4, b * P:(b + 1) * P], sink=True)
            take_mods(0, 16, 40, 1, EVEN_OUT_MOD)
            for j in range(KD):
                residual("even_out", j, T, MOD[:, 0, 16 + j, 0:1])
                if j in (1, 3, 5):
                    mod_strip(EVEN_OUT_MOD + j // 2)

            def moe_pass(q, p, g2):
                dve.memset(YP[:, :], 0.0).then_inc(q["res_added"], 1)
                dve.memset(SPT[:, :], 0.0).then_inc(q["res_added"], 1)
                dve.wait_ge(q["res_added"], 70 * p + 2)
                dve.tensor_copy(SPT[:, 0:1], SPT[:, 0:1]).then_inc(q["spt_ready"], 1)

                def columns_of(i, dst, by, ready):
                    for e in range(2):
                        for blk in range(TB):
                            m = dve.tensor_scalar(dst[:, blk, e * C:(e + 1) * C], par_("slot"),
                                                  RK[:, blk, bass.ds(i * 2 + e, 1)], by[:, blk, bass.ds(i * 2 + e, 1)],
                                                  ALU.is_equal, ALU.mult)
                    m.then_inc(q[ready], 1)

                def add(i):
                    dve.wait_ge(q["res_added"], i * 4 + (70 * p + 2))
                    for r in range(4):
                        dve.wait_ge(q["comb_ready"], i * 4 + (68 * p + r + 1))
                        for h in range(2):
                            c = 2 * r + h
                            m = dve.scalar_tensor_tensor(X[:, c, 0:T], bank[6 + r % 2][:, h * T:(h + 1) * T], g2(c),
                                                         X[:, c, 0:T], ALU.mult, ALU.add)
                        m.then_inc(q["res_added"], 1)

                columns_of(0, GE, MM, "ge_ready")
                columns_of(0, GW, GG, "gw_ready")
                with dve.Fori(0, PAIRS) as i:
                    dve.wait_ge(q["gath_ready"], i + (17 * p + 1))
                    columns_of(i + 1, GE, MM, "ge_ready")
                    dve.wait_ge(q["sil_ready"], i + (16 * p + 1))
                    dve.wait_ge(q["up_ready"], i + (16 * p + 1))
                    dve.tensor_tensor(HTOK, SIL, bank[1][:, :], ALU.mult).then_inc(q["hid_ready"], 1)
                    add(i)
                    dve.wait_ge(q["tr_ready"], i + (16 * p + 1))
                    dve.tensor_copy(SPT[:, :], bank[6][:, 0:T]).then_inc(q["spt_ready"], 1)
                    columns_of(i + 1, GW, GG, "gw_ready")
                add(PAIRS)

            def moe(l):
                g2 = lambda c: MOD[:, l, 40 + c, 0:1]
                big = -NEG
                lg = take(f"route{l}", 0, TB * ROUTES)
                for b in range(TB):
                    dve.memset(GL8[:, b, :], NEG)
                for t_ in (RK, MM, GG):
                    dve.memset(t_, 0.0)
                dve.tensor_tensor(LG.rearrange("p a b -> p (a b)"), lg, par_("rbias", l * TB * ROUTES, TB * ROUTES), ALU.add)\
                   .then_inc(taken["D"], 1)
                wait_taken(dve, f"route{l}", 0)
                link(dve.tensor_copy(GL8[:, :, 0:4], LG[:, :, 0:4]))
                for b in range(TB):
                    m = dve.max(MX8[:, b, :], GL8[:, b, :])
                link(m)
                for b in range(TB):
                    m = dve.max_index(IX8[:, b, :], MX8[:, b, :], GL8[:, b, :])
                link(m)
                link(dve.tensor_copy(IXF, IX8))
                for b in range(TB):
                    m = dve.tensor_scalar(GM[:, b, :], par_("group"), IXF[:, b, 0:1], None, ALU.is_equal)
                link(m)
                for b in range(TB):
                    m = dve.tensor_scalar(ME[:, b, :], GM[:, b, :], big, -big, ALU.mult, ALU.add)
                link(m)
                link(dve.tensor_tensor(GM, GM, LG[:, :, 4:36], ALU.mult))
                link(dve.tensor_tensor(ME, ME, GM, ALU.add))
                for b in range(TB):
                    m = dve.max(V8[:, b, :], ME[:, b, :])
                link(m)
                for b in range(TB):
                    dve.max_index(IE8[:, b, :], V8[:, b, :], ME[:, b, :])
                dve.tensor_scalar(SML[:, :, 0], MX8[:, :, 0], -1.0, None, ALU.mult)
                link(dve.tensor_tensor(SML[:, :, 2], V8[:, :, 1], V8[:, :, 0], ALU.subtract))
                dve.tensor_copy(IEF, IE8).then_inc(rt_exp_in, 1)
                dve.wait_ge(rt_exp_in, l + 1)
                for b in range(TB):
                    dve.tensor_scalar(O0[:, b, :], par_("expert"), IEF[:, b, 0:1], None, ALU.is_equal)
                    m = dve.tensor_scalar(O1[:, b, :], par_("expert"), IEF[:, b, 1:2], None, ALU.is_equal)
                link(m)
                dve.tensor_tensor(MM[:, :, 0:32], O0, O1, ALU.add).then_inc(rt_mask, 1)
                dve.wait_ge(rt_exp, l + 1)
                link(dve.tensor_scalar(SML[:, :, 4], SML[:, :, 3], 1.0, None, ALU.add))
                link(dve.tensor_tensor(SML[:, :, 5], SML[:, :, 4], SML[:, :, 1], ALU.mult))
                link(dve.reciprocal(SML[:, :, 6], SML[:, :, 5]))
                link(dve.tensor_tensor(SML[:, :, 7], SML[:, :, 6], SML[:, :, 3], ALU.mult))
                for b in range(TB):
                    m = dve.tensor_scalar(O0[:, b, :], O0[:, b, :], SML[:, b, 6:7], None, ALU.mult)
                link(m)
                for b in range(TB):
                    m = dve.scalar_tensor_tensor(GG[:, b, 0:32], O1[:, b, :], SML[:, b, 7:8], O0[:, b, :], ALU.mult, ALU.add)
                link(m)
                r = take(f"rank{l}", 0)
                dve.tensor_copy(RK[:, :, 0:32], r[:, 0:64].rearrange("p (a b) -> p a b", a=TB))
                dve.tensor_copy(MS, r[:, 64:96]).then_inc(taken["D"], 1)
                wait_taken(dve, f"rank{l}", 0)
                link(dve.reduce_max(CMAX, MS, AXX))
                link(dve.tensor_scalar(CMAX, CMAX, float(C), None, ALU.is_gt))
                dve.tensor_copy(FLAG[:, l:l + 1], CMAX).then_inc(flag_ready, 1)
                moe_pass(main, l, g2)
                dve.wait_ge(flag_ready, l + 1)
                full = dve.value_load(FLAG[0:1, l:l + 1], min_val=0, max_val=1)
                with dve.If(full > 0):
                    q = over[l]
                    dve.wait_ge(main["res_added"], 70 * (l + 1))
                    with dve.Fori(0, PASSES - 1) as p:
                        dve.tensor_scalar(RK, RK, -float(C), None, ALU.add).then_inc(ranks_moved[l], 1)
                        dve.wait_ge(ranks_moved[l], p + 1)
                        moe_pass(q, p, g2)
                    dve.wait_ge(q["res_added"], 70 * (PASSES - 1))
                dve.wait_ge(main["res_added"], 70 * (l + 1))

            take_mods(0, 40, 48, 1, ODD_MOD)
            take_mods(1, 0, 16, 1, ODD_MOD)
            link(gain(2, 0, 32, 0, par_("g2", 0, KD)))
            last_taken(dve, "even_out")
            norm("n2_0", T, lambda k: X[:, k, 0:T], lambda k: A[:, k, 0:T], [(0, T, lambda k: GSC[:, 2, k:k + 1])])
            moe(0)

            link(gain(3, 1, 8, 0, par_("g1", KD, KD)))
            norm("n1_1", T, lambda k: X[:, k, 0:T], lambda k: A[:, k, 0:T], [(0, T, lambda k: GSC[:, 3, k:k + 1])])
            for s in range(2):
                m = dve.memset(YC[:, s, :], 0.0)
            link(m)
            before_chunk = dict(zip((0, 1, 3, 4, 6, 7), ODD_REDUCE))
            for c in range(KD):
                for n in range(*before_chunk.get(c, (0, 0))):
                    mod_strip(n)
                cw = lambda tap: par_("conv", tap * KD + c, 1)
                y, t_ = YC[:, c % 2, :], CT[:, c % 2, :]
                wait_taken(dve, "odd_in", 3 * c + 1)
                dve.tensor_tensor(y[:, 1:T + 1], CG[:, c % 2, :], take("odd_in", 3 * c + 2, T), ALU.mult)\
                   .then_inc(taken["D"], 1)
                wait_taken(dve, "odd_in", 3 * c + 2)
                link(dve.tensor_scalar(t_, y[:, 0:T], cw(0), None, ALU.mult))
                link(dve.scalar_tensor_tensor(t_, y[:, 1:T + 1], cw(1), t_, ALU.mult, ALU.add))
                link(dve.scalar_tensor_tensor(t_, y[:, 2:T + 2], cw(2), t_, ALU.mult, ALU.add))
                dve.tensor_tensor(CV[:, c, :], t_, BG[:, c % 2, :], ALU.mult).then_inc(cv_ready, 1)
            take_mods(1, 16, 48, 1, ODD_REDUCE[6][0])
            gain(4, 1, 32, 0, par_("g2", KD, KD))
            for j in range(KD):
                residual("odd_out", j, T, MOD[:, 1, 16 + j, 0:1])
                if j in (0, 3):
                    for n in range(*ODD_REDUCE[6 + j // 3]):
                        mod_strip(n)
            last_taken(dve, "odd_out")
            norm("n2_1", T, lambda k: X[:, k, 0:T], lambda k: A[:, k, 0:T], [(0, T, lambda k: GSC[:, 4, k:k + 1])])
            take_mods(2, 0, 16, 2, MERGE_MOD)
            plus_one(0, KD, 2 * KD)
            moe(1)
            norm("final", T, lambda k: X[:, k, 0:T], lambda k: X[:, k, 0:T], [(0, T, lambda k: par_("gf", k, 1))])

            dve.wait_ge(ctx2_in, 16)
            dve.wait_ge(tabb_in, 16)
            for k in range(KD):
                dve.wait_ge(mid_ready, NMID["final"] + k + 1)
                sum_up(k, 2 * T)
            layer_norm("ln_in", 2 * T, ("lni_g", 0, KD), ("lni_b", 0, KD), 0, 0, 8)

            def modulate(l, shift, scale, w):
                for k in range(KD):
                    for s in range(w // T):
                        m = dve.tensor_scalar(A[:, k, s * T:(s + 1) * T], X[:, k, s * T:(s + 1) * T],
                                              MODP[:, l, scale + k, s:s + 1], MOD[:, 2 + l, shift + k, s:s + 1],
                                              ALU.mult, ALU.add)
                    m.then_inc(a_again, 1)

            def outer(l, stage, gate, w):
                for j in range(KD):
                    b = take(stage, j)
                    for s in range(w // T):
                        m = dve.tensor_scalar(RT[:, j % 2, s * T:(s + 1) * T], b[:, s * T:(s + 1) * T],
                                              MODP[:, l, gate + j, s:s + 1], None, ALU.mult)
                    link(m)
                    dve.scalar_tensor_tensor(X[:, j, 0:w], X[:, j, 0:w], ALPHA, RT[:, j % 2, 0:w], ALU.mult, ALU.add)\
                       .then_inc(taken["D"], 1)
                    if j:
                        wait_taken(dve, stage, j)
                        sum_up(j, w)

            for l in range(2):
                w = streams(l)
                for j in range(w // P):
                    dve.tensor_copy(FT[:, j, :], take(f"f{l}", j, 512)).then_inc(taken["D"], 1)
                for j in range(4 * w // T):
                    s, g = j // 4, j % 4
                    dve.tensor_copy(YB[0][:, g, s * T:(s + 1) * T], take(f"idft{l}", j, T)).then_inc(taken["D"], 1)
                for j in range(4):
                    dve.tensor_scalar(NQ[:, j, 0:w], take(f"nq{l}", j, w), 0.125, None, ALU.mult).then_inc(taken["D"], 1)
                attention(f"na{l}", 1.0, PR2, lambda b: YB[1][:, :, b * P:(b + 1) * P])
                for j in range(4):
                    n = w if j < 2 else 2 * T
                    dve.tensor_copy(LOW[:, j, 0:n], take(f"low{l}", j, n)).then_inc(taken["D"], 1)
                wait_taken(dve, f"low{l}", 3)
                norm(f"cq{l}", w, lambda k: LOW[:, k, 0:w], lambda k: LOW[:, k, 0:w],
                     [(0, w, lambda k: par_("gq", l * 2 + k, 1))])
                norm(f"ckv{l}", 2 * T, lambda k: LOW[:, 2, :], lambda k: LOW[:, 2, :],
                     [(0, 2 * T, lambda k: par_("gkv", l, 1))])
                rot = slice(64, 96)
                cos, sin = tab(TC, "cos")[rot, :], tab(TC, "sin")[rot, :]
                dve.tensor_tensor(QT[rot, 0, :], take(f"krope{l}", 0, T)[rot, :], sin, ALU.mult).then_inc(taken["D"], 1)
                link(dve.tensor_tensor(LOW[rot, 3, 0:T], LOW[rot, 3, 0:T], cos, ALU.mult))
                dve.wait_ge(taken["D"], TAKEN[GROUP0[f"krope{l}"]])
                dve.tensor_tensor(LOW[rot, 3, 0:T], LOW[rot, 3, 0:T], QT[rot, 0, :], ALU.add).then_inc(rope_done, 1)
                dve.wait_ge(rope_done, 5 + 9 * l + 1)
                for h in range(HEADS):
                    dve.tensor_copy(MK[rot, h, :], LOW[rot, 3, :]).then_inc(kr_copied, 1)
                for j in range(4):
                    dve.tensor_copy(V2[:, j, :], take(f"mv{l}", j, 512)).then_inc(taken["D"], 1)
                for j in range(8):
                    wait_taken(dve, f"mq{l}", j)
                    dve.tensor_tensor(QT[rot, j % 2, :], take(f"qrope{l}", j, T)[rot, :], sin, ALU.mult).then_inc(taken["D"], 1)
                    link(dve.tensor_tensor(A[rot, j, 0:T], A[rot, j, 0:T], cos, ALU.mult))
                    dve.tensor_tensor(A[rot, j, 0:T], A[rot, j, 0:T], QT[rot, j % 2, :], ALU.add).then_inc(rope_done, 1)
                attention(f"mla{l}", MLA_SCALE, PR2, lambda b: YB[2][:, :, b * P:(b + 1) * P])
                modulate(l, 0, 8, w)
                for o in range(KD):
                    if l == 0:
                        mod_strip(MERGE_MOD + o)
                    for b in range(3):
                        j = (o * 3 + b) * 2
                        wait_taken(dve, f"merge{l}", j)
                        s = SG[:, (o * 3 + b) % 2, 0:w]
                        if b == 0:
                            dve.tensor_tensor(MG[:, o, 0:w], s, take(f"merge{l}", j + 1, w), ALU.mult).then_inc(taken["D"], 1)
                        else:
                            link(dve.tensor_tensor(RT[:, b % 2, 0:w], s, take(f"merge{l}", j + 1, w), ALU.mult))
                            wait_taken(dve, f"merge{l}", j - 1)
                            dve.tensor_tensor(MG[:, o, 0:w], MG[:, o, 0:w], RT[:, b % 2, 0:w], ALU.add)\
                               .then_inc(taken["D"], 1)
                if l == 0:
                    take_mods(2, 16, 48, 2, FFN_MOD)
                    plus_one(0, 16, 48)
                outer(l, f"out{l}", 16, w)
                layer_norm(f"ln1_{l}", w, ("ln1_g", l * KD, KD), ("ln1_b", l * KD, KD), l, 24, 32)
                for j in range(KF):
                    if l == 0 and j % 2 == 0:
                        mod_strip(FFN_MOD + j // 2)
                    wait_taken(dve, f"up{l}", 2 * j)
                    dve.tensor_tensor(HB[:, j, 0:w], SB_[:, j % 2, 0:w], take(f"up{l}", 2 * j + 1, w), ALU.mult)\
                       .then_inc(taken["D"], 1)
                if l == 0:
                    mod_strip(FFN_MOD + 11)
                outer(l, f"down{l}", 40, w)
                if l == 0:
                    take_mods(3, 0, 16, 2, len(MODS))
                    take_mods(3, 16, NMOD, 1, len(MODS))
                    plus_one(1, 0, 16)
                    plus_one(1, 16, NMOD, 1)
                if l == 0:
                    layer_norm("ln2_0", w, ("ln2_g", 0, KD), ("ln2_b", 0, KD), 1, 0, 8)
                else:
                    center("ln2_1", w)
                    dve.wait_ge(xc_ready, NXC["ln2_1"] + KD)
                    norm("ln2_1", w, lambda k: X[:, k, 0:w], lambda k: X[:, k, 0:w],
                         [(0, w, lambda k: par_("ln2_g", KD + k, 1))])


def _f(a):
    return np.ascontiguousarray(np.asarray(a))


def _vec(a):
    return _f(a).reshape(-1, P).T


def _fm(w):
    K, N = w.shape
    return w.reshape(K // P, P, N // P, P).transpose(2, 0, 1, 3).reshape(-1, P, P)


def _tm(w):
    K, N = w.shape
    return w.reshape(K // P, P, N // P, P).transpose(0, 2, 1, 3).reshape(-1, P, P)


def _pad(n):
    return np.zeros((n, P, P), np.float32)


def lay_out(I):
    strips = np.empty((STRIPS, P, TILES, P), np.float32)

    def put(stage, parts, first=None):
        tiles = np.concatenate(parts, 0) if len(parts) > 1 else parts[0]
        n = len(tiles) // TILES
        to = places(stage, "E") if first is None else list(range(first, first + n))
        assert n * TILES == len(tiles) and len(to) == n, (stage, len(tiles))
        strips[to] = tiles.reshape(n, TILES, P, P).transpose(0, 2, 1, 3)

    ada, mod2 = I["w_ada"], I["w_mod_2"]
    ada = [_tm(ada[l].reshape(D, 12, 512)[:, i]) for l in range(2) for i in range(12)]
    mod2 = [_tm(mod2[l].reshape(D, 12, 512)[:, i]) for l in range(2) for i in range(12)]
    sets = (ada[:12], ada[12:], mod2[:12], mod2[12:])
    for s, which, chunk, _ in MODS:
        put(None, [sets[which][chunk // 4]], s)
    w = I["w_in_even"][0]
    order = np.concatenate([np.r_[64 * c:64 * c + 64, 64 * (c + 4):64 * (c + 4) + 64] for c in range(4)])
    put("even", [_fm(w[:, :512][:, order]), _fm(w[:, 512:640]), _tm(w[:, 640:768]), _fm(w[:, 768:1280]),
                 _tm(w[:, 1280:1792]), _pad(16)])
    put("even_out", [_fm(I["w_out_even"][0])])
    for l in range(2):
        for i in range(PAIRS):
            parts = []
            for name in ("w_gate", "w_up"):
                parts += [_tm(I[name][l, e]) for e in (2 * i, 2 * i + 1)]
            parts += [_tm(I["w_down"][l, e]) for e in (2 * i, 2 * i + 1)]
            put(None, parts, FIRST[f"moe{l}"] + 6 * i)
    wi, wo = I["w_in_odd"][0], I["w_out_odd"][0]
    cols = np.concatenate([np.r_[c * P:(c + 1) * P, D + c * P:D + (c + 1) * P, 2 * D + c * P:2 * D + (c + 1) * P]
                           for c in range(KD)])
    put("odd", [_fm(wi[:, cols]), _fm(wo)])

    t = np.arange(T)
    r, cl = t // 64, t % 64
    start = np.clip(cl - 8, 0, 48)
    inside = (cl[None, :] >= start[:, None]) & (cl[None, :] < start[:, None] + 16)
    dr = r[None, :] - r[:, None] + 7
    dc = np.clip(cl[None, :] - cl[:, None] + 15, 0, 30)
    for l in range(2):
        w = I["w_in_2"][l]
        o = np.cumsum([0, 512, 512, 512, 512, 256, 128, 32])
        f, nq, nk, nv, cq, ckv, kr = (w[:, o[i]:o[i + 1]] for i in range(7))
        g = w[:, o[7]:]
        put(f"l{l}_na", [_tm(f), _fm(nq), _fm(nk), _tm(nv)])
        bias = np.where(inside[None], I["na_rpb_2"][l][:, dr, dc], np.float32(NEG)).astype(np.float32)
        strips[FIRST[f"l{l}_bias"]] = bias.reshape(HEADS, TB, P, T).transpose(2, 0, 1, 3).reshape(P, TILES, P)
        krp = np.zeros((D, P), np.float32)
        krp[:, 64:96] = kr
        put(f"l{l}_low", [_fm(cq), _fm(ckv), _fm(krp)])
        q = np.zeros((256, HEADS, P), np.float32)
        q[:, :, :64] = I["w_uq_2"][l].reshape(256, HEADS, 64)
        q[:, :, 64:96] = I["w_qr_2"][l].reshape(256, HEADS, 32)
        k = np.zeros((P, HEADS, P), np.float32)
        k[:, :, :64] = I["w_uk_2"][l].reshape(P, HEADS, 64)
        put(f"l{l}_up", [_fm(q.reshape(256, -1)), _fm(k.reshape(P, -1)), _tm(I["w_uv_2"][l]), _pad(4)])
        gt = _fm(g).reshape(3, KD, KD, P, P)
        bt = np.stack([_fm(I["w_branch_2"][l, b]).reshape(KD, 4, P, P) for b in range(3)])
        both = np.concatenate([gt, bt], 2).transpose(1, 0, 2, 3, 4).reshape(-1, P, P)
        put(f"l{l}_merge", [both])
        put(f"l{l}_out", [_fm(I["w_out_2"][l])])
        gu = np.stack([_fm(I["w_ffn_gate_2"][l]).reshape(KF, KD, P, P), _fm(I["w_ffn_up_2"][l]).reshape(KF, KD, P, P)], 1)
        put(f"l{l}_ffn", [gu.reshape(-1, P, P), _fm(I["w_ffn_down_2"][l]), _pad(16)])

    par = np.zeros((P, N_PAR), np.float32)

    def p(name, a):
        o, n = PAR[name]
        par[:, o:o + n] = a.reshape(-1, n)

    pair = lambda a, b: np.stack([_vec(a), _vec(b)], -1).reshape(P, -1)
    p("c", pair(I["c"], I["c_ctx"]))
    p("c_2", pair(I["c_2"], I["c_ctx_2"]))
    bias = np.concatenate([_vec(I["b_ada"]), _vec(I["b_mod_2"])], 1)
    p("bias", np.repeat(bias, 2, axis=1))
    p("g1", _vec(I["g_norm1"]))
    p("g2", _vec(I["g_norm2"]))
    p("gf", _vec(I["g_final"]))
    p("sgu", _vec(I["g_sgu"]))
    p("conv", _vec(I["conv_w"]))
    for a, b in (("lni_g", "ln_in_g_2"), ("lni_b", "ln_in_b_2"), ("ln1_g", "ln1_g_2"), ("ln1_b", "ln1_b_2"),
                 ("ln2_g", "ln2_g_2"), ("ln2_b", "ln2_b_2"), ("gq", "mla_q_norm_g_2"), ("gkv", "mla_kv_norm_g_2")):
        p(a, _vec(I[b]))
    p("sink", np.broadcast_to(I["attn_sink"].reshape(1, HEADS), (P, HEADS)))
    rb = np.stack([np.concatenate([I["b_router_group"][l], I["b_router_expert"][l]]) for l in range(2)])
    p("rbias", np.broadcast_to(np.repeat(rb[:, None], TB, 1).reshape(1, -1), (P, 2 * TB * ROUTES)))
    p("ident", np.eye(P, dtype=np.float32))
    p("ones", np.ones((P, P), np.float32))
    p("before", (np.arange(P)[:, None] < np.arange(P)[None, :]).astype(np.float32))
    p("expert", np.broadcast_to(np.arange(EXPERTS, dtype=np.float32), (P, EXPERTS)))
    p("group", np.broadcast_to(np.arange(EXPERTS) // (EXPERTS // GROUPS), (P, EXPERTS)).astype(np.float32))
    p("slot", np.broadcast_to(np.arange(C, dtype=np.float32), (P, C)))

    ta = np.zeros((P, N_TA), np.float32)
    tc = np.zeros((P, N_TC), np.float32)

    def q(arr, where, name, a):
        o, n = where[name]
        arr[:, o:o + n] = np.asarray(a, np.float32).reshape(P, n)

    d = np.arange(P) % 64
    inv = (10000.0 ** (-np.arange(16, dtype=np.float32) / 16)).astype(np.float32)
    pos = np.where((d < 32)[:, None], r[None, :], cl[None, :]).astype(np.float32)
    ang = (pos * inv[d % 16][:, None]).astype(np.float32)
    second = (d % 32) >= 16
    q(ta, TA, "cos", np.cos(ang))
    q(ta, TA, "sin", np.where(second[:, None], np.sin(ang), -np.sin(ang)))
    partner = np.where(second, np.arange(P) - 16, np.arange(P) + 16)
    sw = np.zeros((P, P), np.float32)
    sw[partner, np.arange(P)] = 1
    q(ta, TA, "swap", sw)
    near = np.abs(t[None, :] - t[:, None]) <= 128
    q(ta, TA, "mask", np.where(near, 0.0, NEG).reshape(TB, P, T).transpose(1, 0, 2))
    bsp = np.repeat(_f(I["b_spatial"])[0].reshape(4, 2, 1, P), 64, 2).transpose(1, 2, 0, 3)
    q(ta, TA, "bsp", bsp)
    rw = np.concatenate([I["w_router_group"], I["w_router_expert"]], 2).reshape(2, KD, P, ROUTES).transpose(2, 0, 1, 3)
    q(ta, TA, "router", rw)

    inv = (10000.0 ** (-np.arange(8, dtype=np.float32) / 8)).astype(np.float32)
    ang = np.concatenate([r[:, None].astype(np.float32) * inv, cl[:, None].astype(np.float32) * inv], 1).T
    cos, sin = np.ones((P, T)), np.zeros((P, T))
    cos[64:80] = cos[80:96] = np.cos(ang)
    sin[64:80], sin[80:96] = -np.sin(ang), np.sin(ang)
    q(tc, TC, "cos", cos)
    q(tc, TC, "sin", sin)
    sw = np.zeros((P, P), np.float32)
    i = np.arange(16)
    sw[80 + i, 64 + i] = sw[64 + i, 80 + i] = 1
    q(tc, TC, "swap", sw)
    a = 2 * np.pi * (np.outer(t, t) % T) / T
    q(tc, TC, "dft", np.concatenate([np.cos(a), np.sin(a)], 1).reshape(TB, P, 2 * T).transpose(1, 0, 2))
    i = np.arange(P)
    a = 2 * np.pi * (np.outer(i, i) % P) / P
    q(tc, TC, "cd", np.cos(a) / math.sqrt(T * P))
    q(tc, TC, "sd", -np.sin(a) / math.sqrt(T * P))

    fm = lambda a: _f(a).reshape(T, KD, P).transpose(2, 1, 0)
    return {
        "stream": strips.reshape(STRIPS, P, STRIP), "par": par, "tab_a": ta, "tab_b": tc,
        "wsp": _f(I["w_spatial"][0].transpose(2, 0, 1)),
        "xt": _f(np.concatenate([fm(I["x"]), fm(I["ctx"])], 2)), "ctx2t": _f(fm(I["ctx_2"])),
    }


def kernel(**inputs):
    import concourse.bacc as _bacc
    from concourse.bass_utils import run_bass_kernel_spmd as _run

    nc = _bacc.Bacc("TRN2", target_bir_lowering=False, num_devices=1)
    arrays = lay_out({k: np.asarray(v) for k, v in inputs.items()})
    args = [nc.dram_tensor("in_" + k, a.shape, F32, kind="ExternalInput").ap() for k, a in arrays.items()]
    args.append(nc.dram_tensor("out_0", (P, KD, T), F32, kind="ExternalOutput").ap())
    build_program(nc, *args)
    r = _run(nc, [{"in_" + k: a for k, a in arrays.items()}], core_ids=[0])
    got = r.results[0]["out_0"]
    return np.ascontiguousarray(got.transpose(2, 1, 0).reshape(1, T, D))
```
